# Optimizing a Trainium2 kernel written in Bass

```python
import math
import jax, jax.numpy as jnp
from jax import lax
import numpy as np

D_MODEL = 1024
BATCH = 1
SEQ = 512
DEPTH = 1

GRID_W = 64
PLE_DIM = 256
ATT_HEADS = 8
ATT_KV_HEADS = 2
HEAD_DIM = 128
Q_BLOCK = 128
ROPE_THETA = 10000.0
DN_HEADS = 8
DN_DK = 128
DN_DV = 128
CONV_K = 5
CHUNK = 64
EPS = 1e-6

ATT_W = ATT_HEADS * HEAD_DIM
KV_W = ATT_KV_HEADS * HEAD_DIM
DN_KW = DN_HEADS * DN_DK
DN_VW = DN_HEADS * DN_DV
IN_SIZES = (ATT_W, KV_W, KV_W, ATT_W,
            DN_KW, DN_KW, DN_VW, 2 * DN_HEADS, 2 * DN_HEADS, DN_VW,
            D_MODEL, D_MODEL)
IN_W = ATT_W + 2 * KV_W + ATT_W + 2 * DN_KW + DN_VW + 4 * DN_HEADS + DN_VW + 2 * D_MODEL


def rms_norm(x, w):
    xf = x.astype(jnp.float32)
    y = xf * lax.rsqrt(jnp.mean(xf * xf, axis=-1, keepdims=True) + EPS)
    return (y * w.astype(jnp.float32)).astype(x.dtype)

def l2_norm(x):
    xf = x.astype(jnp.float32)
    return xf * lax.rsqrt(jnp.sum(xf * xf, axis=-1, keepdims=True) + EPS)

def split_cols(t):
    outs, start = [], 0
    for size in IN_SIZES:
        outs.append(t[..., start:start + size])
        start += size
    return outs

def axial_rope_angles(seq_len):
    rows = seq_len // GRID_W
    row = jnp.broadcast_to(jnp.arange(rows)[:, None], (rows, GRID_W)).reshape(seq_len)
    col = jnp.broadcast_to(jnp.arange(GRID_W)[None, :], (rows, GRID_W)).reshape(seq_len)
    n_freq = HEAD_DIM // 4
    inv_freq = ROPE_THETA ** (-jnp.arange(n_freq, dtype=jnp.float32) / n_freq)
    ang = jnp.concatenate([row.astype(jnp.float32)[:, None] * inv_freq,
                           col.astype(jnp.float32)[:, None] * inv_freq], axis=-1)
    return jnp.cos(ang), jnp.sin(ang)

def apply_rope(x, cos, sin):
    xf = x.astype(jnp.float32).reshape(*x.shape[:-1], HEAD_DIM // 2, 2)
    x0, x1 = xf[..., 0], xf[..., 1]
    out = jnp.stack([x0 * cos - x1 * sin, x0 * sin + x1 * cos], axis=-1)
    return out.reshape(x.shape).astype(x.dtype)

def gqa_attention(q, k, v):
    B, Hq, S, D = q.shape
    G = Hq // ATT_KV_HEADS
    nb = S // Q_BLOCK
    qb = q.reshape(B, ATT_KV_HEADS, G, nb, Q_BLOCK, D).transpose(3, 0, 1, 2, 4, 5)
    scale = D ** -0.5

    def block(qi):
        s = jnp.einsum('bkgqd,bksd->bkgqs', qi, k).astype(jnp.float32) * scale
        pr = jax.nn.softmax(s, axis=-1).astype(v.dtype)
        return jnp.einsum('bkgqs,bksd->bkgqd', pr, v)

    o = lax.map(block, qb)
    return o.transpose(1, 2, 3, 0, 4, 5).reshape(B, Hq, S, D)

def short_conv(x, w):
    C = x.shape[-1]
    return lax.conv_general_dilated(
        x, w[:, None, :].astype(x.dtype), window_strides=(1,),
        padding=((CONV_K // 2, CONV_K // 2),),
        dimension_numbers=('NWC', 'WIO', 'NWC'), feature_group_count=C)

def chunk_gated_delta_rule(q, k, v, g, beta):
    B, H, S, DK = q.shape
    DV = v.shape[-1]
    n = S // CHUNK
    q = q.reshape(B, H, n, CHUNK, DK)
    k = k.reshape(B, H, n, CHUNK, DK)
    v = v.reshape(B, H, n, CHUNK, DV)
    beta = beta.reshape(B, H, n, CHUNK)
    g = jnp.cumsum(g.reshape(B, H, n, CHUNK), axis=-1)
    tril = jnp.tril(jnp.ones((CHUNK, CHUNK), dtype=bool))
    eye = jnp.eye(CHUNK, dtype=jnp.float32)
    decay = jnp.exp(jnp.where(tril, g[..., :, None] - g[..., None, :], -jnp.inf))
    k_beta = k * beta[..., None]
    v_beta = v * beta[..., None]
    L = jnp.tril(jnp.einsum('bhncd,bhnjd->bhncj', k_beta, k) * decay, -1)
    T = lax.linalg.triangular_solve(eye + L, jnp.broadcast_to(eye, L.shape),
                                    left_side=True, lower=True, unit_diagonal=True)
    u = jnp.einsum('bhncj,bhnjv->bhncv', T, v_beta)
    w = jnp.einsum('bhncj,bhnjd->bhncd', T, k_beta * jnp.exp(g)[..., None])
    a_intra = jnp.einsum('bhncd,bhnjd->bhncj', q, k) * decay

    def step(state, xs):
        q_c, k_c, u_c, w_c, g_c, a_c = xs
        g_last = g_c[..., -1]
        v_new = u_c - jnp.einsum('bhcd,bhdv->bhcv', w_c, state)
        o = (jnp.einsum('bhcd,bhdv->bhcv', q_c * jnp.exp(g_c)[..., None], state)
             + jnp.einsum('bhcj,bhjv->bhcv', a_c, v_new))
        k_dec = k_c * jnp.exp(g_last[..., None] - g_c)[..., None]
        state = state * jnp.exp(g_last)[..., None, None] + jnp.einsum('bhcd,bhcv->bhdv', k_dec, v_new)
        return state, o

    front = lambda t: jnp.moveaxis(t, 2, 0)
    xs = (front(q), front(k), front(u), front(w), front(g), front(a_intra))
    state0 = jnp.zeros((B, H, DK, DV), jnp.float32)
    _, o = lax.scan(step, state0, xs)
    return jnp.moveaxis(o, 0, 2).reshape(B, H, S, DV)

def bidir_gated_deltanet(q, k, v, g, beta):
    flip = lambda t: jnp.flip(t, axis=2)
    o_f = chunk_gated_delta_rule(q, k, v, g[0], beta[0])
    o_b = flip(chunk_gated_delta_rule(flip(q), flip(k), flip(v), flip(g[1]), flip(beta[1])))
    return o_f + o_b

def first_inputs(seed: int = 0) -> dict:
    key = jax.random.key(seed)
    ks = jax.random.split(key, 20)
    nrm = lambda k, shape, scale: jax.random.normal(k, shape, jnp.float32) * scale
    gain = lambda k, shape: 1.0 + 0.02 * jax.random.normal(k, shape, jnp.float32)
    dt = jnp.exp(jax.random.uniform(ks[8], (DEPTH, 2, DN_HEADS), jnp.float32,
                                    math.log(1e-3), math.log(1e-1)))
    return {
        'x': nrm(ks[0], (BATCH, SEQ, D_MODEL), 1.0),
        'p': nrm(ks[1], (DEPTH, BATCH, SEQ, PLE_DIM), 1.0),
        'norm_pre': gain(ks[2], (DEPTH, D_MODEL)),
        'w_in': nrm(ks[3], (DEPTH, D_MODEL, IN_W), D_MODEL ** -0.5),
        'q_norm': gain(ks[4], (DEPTH, HEAD_DIM)),
        'k_norm': gain(ks[5], (DEPTH, HEAD_DIM)),
        'conv_w': nrm(ks[6], (DEPTH, CONV_K, 2 * DN_KW + DN_VW), CONV_K ** -0.5),
        'a_log': jnp.log(jax.random.uniform(ks[7], (DEPTH, 2, DN_HEADS), jnp.float32, 1.0, 16.0)),
        'dt_bias': dt + jnp.log(-jnp.expm1(-dt)),
        'dn_norm': gain(ks[9], (DEPTH, DN_DV)),
        'w_br_att': nrm(ks[10], (DEPTH, ATT_W, D_MODEL), ATT_W ** -0.5),
        'w_br_dn': nrm(ks[11], (DEPTH, DN_VW, D_MODEL), DN_VW ** -0.5),
        'w_out': nrm(ks[12], (DEPTH, D_MODEL, D_MODEL), D_MODEL ** -0.5),
        'norm_post': gain(ks[13], (DEPTH, D_MODEL)),
        'w_ple_proj': nrm(ks[14], (DEPTH, PLE_DIM, D_MODEL), PLE_DIM ** -0.5),
        'w_ple_gate': nrm(ks[15], (DEPTH, D_MODEL, D_MODEL), D_MODEL ** -0.5),
        'ple_norm': gain(ks[16], (DEPTH, D_MODEL)),
    }

def first_block(x, p, norm_pre, w_in, q_norm, k_norm, conv_w, a_log, dt_bias, dn_norm,
              w_br_att, w_br_dn, w_out, norm_post, w_ple_proj, w_ple_gate, ple_norm):
    B, S, _ = x.shape
    cos, sin = axial_rope_angles(S)
    heads = lambda t, nh, hd: t.reshape(B, S, nh, hd).transpose(0, 2, 1, 3)
    for i in range(DEPTH):
        h = rms_norm(x, norm_pre[i])
        (aq, ak, av, az, dq, dk, dv, db, da, dz, gate_att, gate_dn) = split_cols(h @ w_in[i])

        q = apply_rope(rms_norm(heads(aq, ATT_HEADS, HEAD_DIM), q_norm[i]), cos, sin)
        k = apply_rope(rms_norm(heads(ak, ATT_KV_HEADS, HEAD_DIM), k_norm[i]), cos, sin)
        v = heads(av, ATT_KV_HEADS, HEAD_DIM)
        o_att = gqa_attention(q, k, v).transpose(0, 2, 1, 3).reshape(B, S, ATT_W)
        y_att = (o_att * jax.nn.silu(az)) @ w_br_att[i]

        qkv = jax.nn.silu(short_conv(jnp.concatenate([dq, dk, dv], axis=-1), conv_w[i]))
        cq, ck, cv = qkv[..., :DN_KW], qkv[..., DN_KW:2 * DN_KW], qkv[..., 2 * DN_KW:]
        qd = l2_norm(heads(cq, DN_HEADS, DN_DK)) * (DN_DK ** -0.5)
        kd = l2_norm(heads(ck, DN_HEADS, DN_DK))
        vd = heads(cv, DN_HEADS, DN_DV).astype(jnp.float32)
        da4 = da.astype(jnp.float32).reshape(B, S, 2, DN_HEADS)
        db4 = db.astype(jnp.float32).reshape(B, S, 2, DN_HEADS)
        g = -jnp.exp(a_log[i].astype(jnp.float32)) * jax.nn.softplus(da4 + dt_bias[i].astype(jnp.float32))
        beta = jax.nn.sigmoid(db4)
        g = g.transpose(2, 0, 3, 1)
        beta = beta.transpose(2, 0, 3, 1)
        o_dn = bidir_gated_deltanet(qd, kd, vd, g, beta).astype(x.dtype)
        o_dn = rms_norm(o_dn.transpose(0, 2, 1, 3), dn_norm[i]).reshape(B, S, DN_VW)
        y_dn = (o_dn * jax.nn.silu(dz)) @ w_br_dn[i]

        mix = (jax.nn.sigmoid(gate_att) * y_att + jax.nn.sigmoid(gate_dn) * y_dn) @ w_out[i]
        x = x + rms_norm(mix, norm_post[i])

        e = p[i] @ w_ple_proj[i]
        x = x + rms_norm(jax.nn.sigmoid(x @ w_ple_gate[i]) * e, ple_norm[i])
    return x


CTX_LEN = 256
GLA_HEADS = 4
GLA_DK = 64
GLA_DV = 128
GLA_WIDTH = GLA_HEADS * GLA_DV
GATE_RANK = 16
GATE_NORMALIZER = 16.0
POOL_WINDOWS = (2, 4, 8, 16)
POOL_GROUP = 128
POOL_WIDTH = POOL_GROUP * len(POOL_WINDOWS)
MIX_WIDTH = GLA_WIDTH + POOL_WIDTH
Q_COLS = GLA_HEADS * GLA_DK
K_COLS = GLA_HEADS * GLA_DK
V_COLS = GLA_WIDTH
G_COLS = GLA_WIDTH
A_COLS = 2 * GATE_RANK
P_COLS = POOL_WIDTH
OFF_K = Q_COLS
OFF_V = OFF_K + K_COLS
OFF_G = OFF_V + V_COLS
OFF_A = OFF_G + G_COLS
OFF_P = OFF_A + A_COLS
IN_COLS = OFF_P + P_COLS
N_GROUPS = 4
EXPERTS_PER_GROUP = 8
N_EXPERTS = N_GROUPS * EXPERTS_PER_GROUP
TOP_K_INNER = 2
D_EXPERT = 256


def rmsnorm(x, g):
    xf = x.astype(jnp.float32)
    y = xf * lax.rsqrt(jnp.mean(xf * xf, axis=-1, keepdims=True) + EPS)
    return (y * g).astype(x.dtype)

def modulate(h, shift, scale):
    return h * (1.0 + scale) + shift

def flip(t):
    return jnp.flip(t, axis=1)

def split_heads_qkv(q, k, v):
    B, L, _ = q.shape
    q = q.reshape(B, L, GLA_HEADS, GLA_DK) * (GLA_DK ** -0.5)
    k = k.reshape(B, L, GLA_HEADS, GLA_DK)
    v = v.reshape(B, L, GLA_HEADS, GLA_DV)
    return q, k, v

def log_decay(a_low, w_dec, b_dec):
    B, L, _ = a_low.shape
    a = a_low.reshape(B, L, 2, GATE_RANK).astype(jnp.float32)
    la = jax.nn.log_sigmoid(jnp.einsum('bldr,drk->bldk', a, w_dec) + b_dec) / GATE_NORMALIZER
    la = la.reshape(B, L, 2, GLA_HEADS, GLA_DK)
    return la[:, :, 0], la[:, :, 1]

def gla_state(k, v, la, s0):
    B, L, H, dk = k.shape
    dv = v.shape[-1]
    N = L // CHUNK
    kc = k.reshape(B, N, CHUNK, H, dk).astype(jnp.float32)
    vc = v.reshape(B, N, CHUNK, H, dv)
    b = jnp.cumsum(la.reshape(B, N, CHUNK, H, dk), axis=2)
    b_last = b[:, :, -1]
    k_st = kc * jnp.exp(b_last[:, :, None] - b)
    d_state = jnp.einsum('bnchd,bnche->nbhde', k_st, vc)
    decay = jnp.exp(b_last).transpose(1, 0, 2, 3)

    def step(S, inp):
        d, ds = inp
        return d[..., None] * S + ds, S

    s_fin, s_prev = lax.scan(step, s0, (decay, d_state))
    return s_prev, s_fin, b

def gla_chunked(q, k, v, la, s0):
    s_prev, s_fin, b = gla_state(k, v, la, s0)
    B, L, H, dk = q.shape
    dv = v.shape[-1]
    N = L // CHUNK
    qb = q.reshape(B, N, CHUNK, H, dk).astype(jnp.float32) * jnp.exp(b)
    kb = k.reshape(B, N, CHUNK, H, dk).astype(jnp.float32) * jnp.exp(-b)
    vc = v.reshape(B, N, CHUNK, H, dv)
    mask = jnp.tril(jnp.ones((CHUNK, CHUNK), dtype=bool))
    scores = jnp.where(mask, jnp.einsum('bnihd,bnjhd->bnhij', qb, kb), 0.0)
    o = jnp.einsum('bnhij,bnjhe->bnihe', scores, vc) + jnp.einsum('bnihd,nbhde->bnihe', qb, s_prev)
    return o.reshape(B, L, H, dv), s_fin

def gla_bidirectional(q, k, v, la_f, la_b, s0_f, s0_b):
    o_f, s_f = gla_chunked(q, k, v, la_f, s0_f)
    o_b, s_b = gla_chunked(flip(q), flip(k), flip(v), flip(la_b), s0_b)
    return o_f + flip(o_b), s_f, s_b

def window_mean(x, w, axis):
    n = x.shape[axis]
    lo = w // 2
    hi = w - 1 - lo
    cs = jnp.cumsum(x.astype(jnp.float32), axis=axis)
    pad = [(0, 0)] * x.ndim
    pad[axis] = (1, 0)
    cs = jnp.pad(cs, pad)
    idx = np.arange(n)
    start = np.clip(idx - lo, 0, n)
    end = np.clip(idx + hi + 1, 0, n)
    s = jnp.take(cs, jnp.asarray(end), axis=axis) - jnp.take(cs, jnp.asarray(start), axis=axis)
    cshape = [1] * x.ndim
    cshape[axis] = n
    cnt = jnp.asarray((end - start).astype(np.float32).reshape(cshape))
    return s / cnt

def pool_mixer(p, w_pool, pool_scale, rows):
    B, L, _ = p.shape
    groups = p.reshape(B, L, len(POOL_WINDOWS), POOL_GROUP)
    outs = []
    for gi, w in enumerate(POOL_WINDOWS):
        xg = groups[:, :, gi]
        if rows is None:
            m = window_mean(xg, w, 1)
        else:
            xg2 = xg.reshape(B, rows, GRID_W, POOL_GROUP)
            m = window_mean(window_mean(xg2, w, 2), w, 1).reshape(B, L, POOL_GROUP)
        outs.append(m - xg)
    y = jnp.stack(outs, axis=2)
    y = jnp.einsum('blgc,gcd->blgd', y, w_pool).reshape(B, L, POOL_WIDTH)
    return y * pool_scale

def token_mixer(h, w_in, w_dec, b_dec, gla_norm_g, w_pool, pool_scale, w_out, s0_f, s0_b, rows):
    B, L, _ = h.shape
    proj = h @ w_in
    q, k, v, g, a_low, p = jnp.split(proj, [OFF_K, OFF_V, OFF_G, OFF_A, OFF_P], axis=-1)
    q, k, v = split_heads_qkv(q, k, v)
    la_f, la_b = log_decay(a_low, w_dec, b_dec)
    o, s_f, s_b = gla_bidirectional(q, k, v, la_f, la_b, s0_f, s0_b)
    o = rmsnorm(o, gla_norm_g).reshape(B, L, GLA_WIDTH) * jax.nn.silu(g)
    pooled = pool_mixer(p, w_pool, pool_scale, rows)
    out = jnp.concatenate([o, pooled.astype(o.dtype)], axis=-1) @ w_out
    return out, s_f, s_b

def context_states(h, w_in, w_dec, b_dec):
    B, L, _ = h.shape
    kv = h @ w_in[:, OFF_K:OFF_G]
    a_low = h @ w_in[:, OFF_A:OFF_P]
    k = kv[..., :K_COLS].reshape(B, L, GLA_HEADS, GLA_DK)
    v = kv[..., K_COLS:].reshape(B, L, GLA_HEADS, GLA_DV)
    la_f, la_b = log_decay(a_low, w_dec, b_dec)
    s0 = jnp.zeros((B, GLA_HEADS, GLA_DK, GLA_DV), jnp.float32)
    _, s_f, _ = gla_state(k, v, la_f, s0)
    _, s_b, _ = gla_state(flip(k), flip(v), flip(la_b), s0)
    return s_f, s_b

def hier_moe(h, w_rg, w_re, w_e_in, w_e_out):
    B, L, D = h.shape
    t = h.reshape(-1, D)
    pg = jax.nn.softmax((t @ w_rg).astype(jnp.float32), axis=-1)
    gp, gi = lax.top_k(pg, 1)
    le = (t @ w_re).astype(jnp.float32).reshape(-1, N_GROUPS, EXPERTS_PER_GROUP)
    le = jnp.take_along_axis(le, gi[:, :, None], axis=1)[:, 0]
    ew, ei = lax.top_k(jax.nn.softmax(le, axis=-1), TOP_K_INNER)
    ew = ew / jnp.sum(ew, axis=-1, keepdims=True)
    weights = gp * ew
    eid = gi * EXPERTS_PER_GROUP + ei
    gates = jnp.einsum('tk,tke->et', weights, jax.nn.one_hot(eid, N_EXPERTS, dtype=jnp.float32))

    def body(acc, inp):
        wi, wo, ge = inp
        a, u = jnp.split(t @ wi, 2, axis=-1)
        return acc + ((jax.nn.silu(a) * u) @ wo) * ge[:, None], None

    y, _ = lax.scan(body, jnp.zeros(t.shape, jnp.float32), (w_e_in, w_e_out, gates))
    return y.reshape(B, L, D).astype(h.dtype)

def second_inputs(seed: int = 0) -> dict:
    key = jax.random.key(seed)
    ks = jax.random.split(key, 24)
    f32 = jnp.float32

    def nrm(k, shape, s):
        return jax.random.normal(k, shape, f32) * s

    D = D_MODEL
    return {
        "x": nrm(ks[0], (BATCH, SEQ, D), 1.0),
        "c": nrm(ks[1], (BATCH, D), 1.0),
        "ctx": nrm(ks[2], (BATCH, CTX_LEN, D), 1.0),
        "c_ctx": nrm(ks[3], (D,), 1.0),
        "w_ada": nrm(ks[4], (DEPTH, D, 6 * D), D ** -0.5),
        "b_ada": nrm(ks[5], (DEPTH, 6 * D), 0.02),
        "norm1_g": 1.0 + nrm(ks[6], (DEPTH, D), 0.02),
        "w_in": nrm(ks[7], (DEPTH, D, IN_COLS), D ** -0.5),
        "w_decay": nrm(ks[8], (DEPTH, 2, GATE_RANK, GLA_HEADS * GLA_DK), GATE_RANK ** -0.5),
        "b_decay": nrm(ks[9], (DEPTH, 2, GLA_HEADS * GLA_DK), 0.1),
        "gla_norm_g": 1.0 + nrm(ks[10], (DEPTH, GLA_DV), 0.02),
        "w_pool": nrm(ks[11], (DEPTH, len(POOL_WINDOWS), POOL_GROUP, POOL_GROUP), POOL_GROUP ** -0.5),
        "pool_scale": 1.0 + nrm(ks[12], (DEPTH, POOL_WIDTH), 0.02),
        "w_out": nrm(ks[13], (DEPTH, MIX_WIDTH, D), MIX_WIDTH ** -0.5),
        "norm2_g": 1.0 + nrm(ks[14], (DEPTH, D), 0.02),
        "w_router_group": nrm(ks[15], (DEPTH, D, N_GROUPS), D ** -0.5),
        "w_router_expert": nrm(ks[16], (DEPTH, D, N_EXPERTS), D ** -0.5),
        "w_expert_in": nrm(ks[17], (DEPTH, N_EXPERTS, D, 2 * D_EXPERT), D ** -0.5),
        "w_expert_out": nrm(ks[18], (DEPTH, N_EXPERTS, D_EXPERT, D), D_EXPERT ** -0.5),
        "final_norm_g": 1.0 + nrm(ks[19], (D,), 0.02),
    }

def second_block(x, c, ctx, c_ctx, w_ada, b_ada, norm1_g, w_in, w_decay, b_decay, gla_norm_g, w_pool,
              pool_scale, w_out, norm2_g, w_router_group, w_router_expert, w_expert_in, w_expert_out,
              final_norm_g):
    rows = x.shape[1] // GRID_W
    xc = ctx
    for i in range(DEPTH):
        mod = jax.nn.silu(c) @ w_ada[i] + b_ada[i]
        sh_a, sc_a, gt_a, sh_m, sc_m, gt_m = jnp.split(mod[:, None, :], 6, axis=-1)
        mod_c = jax.nn.silu(c_ctx) @ w_ada[i] + b_ada[i]
        csh_a, csc_a, cgt_a, csh_m, csc_m, cgt_m = jnp.split(mod_c, 6, axis=-1)

        hc = modulate(rmsnorm(xc, norm1_g[i]), csh_a, csc_a)
        if i + 1 < DEPTH:
            zero_s = jnp.zeros((xc.shape[0], GLA_HEADS, GLA_DK, GLA_DV), jnp.float32)
            out_c, s_f, s_b = token_mixer(hc, w_in[i], w_decay[i], b_decay[i], gla_norm_g[i], w_pool[i],
                                          pool_scale[i], w_out[i], zero_s, zero_s, None)
            xc_next = xc + (cgt_a * out_c).astype(xc.dtype)
            hc2 = modulate(rmsnorm(xc_next, norm2_g[i]), csh_m, csc_m)
            xc_next = xc_next + (cgt_m * hier_moe(hc2, w_router_group[i], w_router_expert[i],
                                                  w_expert_in[i], w_expert_out[i])).astype(xc.dtype)
        else:
            s_f, s_b = context_states(hc, w_in[i], w_decay[i], b_decay[i])
            xc_next = xc

        h = modulate(rmsnorm(x, norm1_g[i]), sh_a, sc_a)
        out, _, _ = token_mixer(h, w_in[i], w_decay[i], b_decay[i], gla_norm_g[i], w_pool[i],
                                pool_scale[i], w_out[i], s_f, s_b, rows)
        x = x + (gt_a * out).astype(x.dtype)
        h2 = modulate(rmsnorm(x, norm2_g[i]), sh_m, sc_m)
        x = x + (gt_m * hier_moe(h2, w_router_group[i], w_router_expert[i],
                                 w_expert_in[i], w_expert_out[i])).astype(x.dtype)
        xc = xc_next
    return rmsnorm(x, final_norm_g)


def setup_inputs(seed=0):
    out = dict(first_inputs(seed))
    for name, value in second_inputs(seed + 1).items():
        if name != "x":
            out[name + "_2"] = value
    return out


def reference(
    x, p, norm_pre, w_in, q_norm, k_norm, conv_w, a_log, dt_bias, dn_norm, w_br_att, w_br_dn,
    w_out, norm_post, w_ple_proj, w_ple_gate, ple_norm, c_2, ctx_2, c_ctx_2, w_ada_2, b_ada_2,
    norm1_g_2, w_in_2, w_decay_2, b_decay_2, gla_norm_g_2, w_pool_2, pool_scale_2, w_out_2,
    norm2_g_2, w_router_group_2, w_router_expert_2, w_expert_in_2, w_expert_out_2,
    final_norm_g_2,
):
    x = first_block(
        x, p, norm_pre, w_in, q_norm, k_norm, conv_w, a_log, dt_bias, dn_norm, w_br_att,
        w_br_dn, w_out, norm_post, w_ple_proj, w_ple_gate, ple_norm,
    )
    return second_block(
        x, c_2, ctx_2, c_ctx_2, w_ada_2, b_ada_2, norm1_g_2, w_in_2, w_decay_2, b_decay_2,
        gla_norm_g_2, w_pool_2, pool_scale_2, w_out_2, norm2_g_2, w_router_group_2,
        w_router_expert_2, w_expert_in_2, w_expert_out_2, final_norm_g_2,
    )


_drawn_inputs = setup_inputs


def setup_inputs(seed=0):
    import zlib

    import numpy as np

    out = dict(_drawn_inputs(seed))
    spreads = {}
    factors = {'q_norm': 7.639,
     'k_norm': 8.0,
     'ple_norm': 3.0,
     'norm1_g_2': 3.633,
     'b_decay_2': 3.991,
     'gla_norm_g_2': 23.201,
     'pool_scale_2': 15.747,
     'dn_norm': 5.037,
     'norm_post': 3.817,
     'norm2_g_2': 8.0}
    for name, (base, spread) in spreads.items():
        noise = np.random.default_rng([zlib.crc32(name.encode()), seed]).standard_normal(out[name].shape)
        drawn = base * np.exp(spread * noise) if base else spread * noise
        out[name] = __import__('jax').numpy.asarray(drawn.astype(out[name].dtype))
    for name, factor in factors.items():
        out[name] = (out[name] * factor).astype(out[name].dtype)
    return out
```

```python
from contextlib import ExitStack

import numpy as np

import concourse.bass as bass
from concourse import mybir

F32 = mybir.dt.float32
U32 = mybir.dt.uint32
ALU = mybir.AluOpType
ACT = mybir.ActivationFunctionType
AXX = mybir.AxisListType.X

P = 128
SEQ, DM = 512, 1024
NT = SEQ // P
KC = DM // P
EPS = 1e-6
HD = 128
NH, NKV = 8, 2
GRID_W = 64
ROPE_THETA = 10000.0
CONV_K = 5
PLE = 256
CTX = 256
NTC = CTX // P
CH2 = 64
H2, DK2, DV2 = 4, 64, 128
RANK = 16
WINDOWS = (2, 4, 8, 16)
NE, NG, EPG, DE = 32, 4, 8, 256
CAP = 64
ROUNDS = SEQ // CAP
SLOTS = ROUNDS * NE * CAP
XPT = 4
O_AQ, O_AK, O_AV, O_AZ = 0, 1024, 1280, 1536
O_DQ, O_DB, O_DZ, O_GA, O_GD = 2560, 5632, 5664, 6688, 7712
O2_Q, O2_K, O2_V, O2_G, O2_A, O2_P = 0, 256, 512, 1024, 1536, 1568
WC = 256
NW = 2
LEVELS = 7

C_ID, C_ONE, C_LE, C_GE = 0, 128, 256, 384
C_LV = 512
C_BLE = C_LV + 2 * LEVELS * P
C_BGE, C_BGT, C_BLT = C_BLE + P, C_BLE + 2 * P, C_BLE + 3 * P
C_EPS = C_BLE + 4 * P
C_IOTA = C_EPS + 4
C_TOK = C_IOTA + 32
C_LT = C_TOK + NT
C_N = C_LT + P
V_PRE, V_DN, V_N1, V_N2, V_GLA, V_PS, V_BADA, V_C, V_CC = 0, 8, 9, 17, 25, 26, 30, 78, 86
V_N = 94


def shape_constants():
    i = np.arange(P)
    p, f = i[:, None], i[None, :]
    c = np.zeros((P, C_N), np.float32)
    c[:, C_ID:C_ID + P] = p == f
    c[:, C_ONE:C_ONE + P] = 1.0
    c[:, C_LE:C_LE + P] = p <= f
    c[:, C_GE:C_GE + P] = p >= f
    for k in range(LEVELS):
        b = 1 << k
        off = (p // (2 * b) == f // (2 * b)) & (p // b != f // b)
        c[:, C_LV + k * P:C_LV + (k + 1) * P] = off & (p > f)
        c[:, C_LV + (LEVELS + k) * P:C_LV + (LEVELS + k + 1) * P] = off & (p < f)
    same = p // CH2 == f // CH2
    c[:, C_BLE:C_BLE + P] = same & (p <= f)
    c[:, C_BGE:C_BGE + P] = same & (p >= f)
    c[:, C_BGT:C_BGT + P] = same & (p > f)
    c[:, C_BLT:C_BLT + P] = same & (p < f)
    c[:, C_EPS] = EPS
    c[:, C_EPS + 1] = HD * EPS
    c[:, C_EPS + 2] = 1.0
    c[:, C_IOTA:C_IOTA + 32] = np.arange(32)
    c[:, C_TOK:C_TOK + NT] = p + P * np.arange(NT)
    c[:, C_LT:C_LT + P] = p < f
    nf = HD // 4
    inv = (np.float32(ROPE_THETA) ** (-np.arange(nf, dtype=np.float32) / np.float32(nf))).astype(np.float32)
    t = np.arange(SEQ)
    ang = np.concatenate([(t // GRID_W).astype(np.float32)[:, None] * inv,
                          (t % GRID_W).astype(np.float32)[:, None] * inv], axis=1)
    rope = np.stack([np.cos(ang), np.sin(ang)], axis=1).astype(np.float32)
    rope = np.ascontiguousarray(rope.reshape(NT, P, 2, HD // 2).transpose(1, 0, 2, 3))

    def mean(n, w):
        m = np.zeros((n, n))
        lo = w // 2
        hi = w - 1 - lo
        for a in range(n):
            s, e = max(0, a - lo), min(n, a + hi + 1)
            m[a, s:e] = 1.0 / (e - s)
        return m

    pool = np.zeros((len(WINDOWS), SEQ, SEQ))
    for g, w in enumerate(WINDOWS):
        pool[g] = (np.kron(mean(SEQ // GRID_W, w), mean(GRID_W, w)) - np.eye(SEQ)).T
    pool = pool.astype(np.float32).reshape(len(WINDOWS), NT, P, SEQ).transpose(2, 0, 1, 3)
    return c, rope, np.ascontiguousarray(pool)


class Lane:

    def __init__(self, eng, chain):
        self.eng, self.chain = eng, chain
        self.raised, self.followed = {}, {}
        self.i, self.per, self.at = None, {}, None

    def value(self, table, sem):
        n = table[sem]
        if self.i is None or not self.per.get((id(table), sem), 0):
            return n
        return self.i * self.per[(id(table), sem)] + n

    def did(self, ins, sem=None, also=()):
        sem = self.chain if sem is None else sem
        ins.then_inc(sem, 1)
        self.raised[sem] = self.raised.get(sem, 0) + 1
        self.eng.wait_ge(sem, self.value(self.raised, sem))
        for s in also:
            self.raise_(s)

    def raise_(self, sem, n=1):
        self.raised[sem] = self.raised.get(sem, 0) + n
        self.eng.sem_inc(sem, n)

    def need(self, sem, n=1):
        self.followed[sem] = self.followed.get(sem, 0) + n
        self.eng.wait_ge(sem, self.value(self.followed, sem))

    def enter(self, i, raised, followed):
        self.i = i
        self.per = {}
        for s, n in raised.items():
            self.raised.setdefault(s, 0)
            self.per[(id(self.raised), s)] = n
        for s, n in followed.items():
            self.followed.setdefault(s, 0)
            self.per[(id(self.followed), s)] = n
        self.at = (dict(self.raised), dict(self.followed))

    def leave(self, turns):
        for table, before in ((self.raised, self.at[0]), (self.followed, self.at[1])):
            for s in table:
                per = self.per.get((id(table), s), 0)
                assert table[s] - before.get(s, 0) == per, (s, table[s] - before.get(s, 0), per)
                table[s] = before.get(s, 0) + turns * per
        self.i, self.per = None, {}


def build(nc, a, out, dumps):
    ctx = ExitStack()
    with ctx:
        def sb(name, *shape):
            return ctx.enter_context(nc.sbuf_tensor(name, [P, *shape], F32))

        def sem(name):
            return ctx.enter_context(nc.semaphore(name))

        const = sb("const", C_N)
        ident = const[:, C_ID:C_ID + P]
        ones = const[:, C_ONE:C_ONE + P]
        tri = [const[:, C_LE:C_LE + P], const[:, C_GE:C_GE + P]]
        blk = [const[:, C_BLE:C_BLE + P], const[:, C_BGE:C_BGE + P]]
        blk_rest = [const[:, C_BGT:C_BGT + P], const[:, C_BLT:C_BLT + P]]
        eps = const[:, C_EPS:C_EPS + 1]
        eps128 = const[:, C_EPS + 1:C_EPS + 2]
        one = const[:, C_EPS + 2:C_EPS + 3]
        wslot = sb("wslot", NW, KC * WC)
        cols = sb("cols", V_N)
        ccols = sb("ccols", CONV_K * 24)
        csilu = sb("csilu", KC, 2)
        mod = sb("mod", 48, 2)
        small = sb("small", 3 * 64)
        ss = small[:, 0:64]
        gb = sb("gb", NT, 32)
        gain = sb("gain", 3 * KC)
        gpar = sb("gpar", 3, 16)
        kcol = sb("kcol", 2, 4)

        ARENA = 44100
        arena = sb("arena", ARENA)
        top = [0]

        def at(off, *shape):
            n = int(np.prod(shape))
            assert off + n <= ARENA, (off, n)
            top[0] = off + n
            v = arena[:, off:off + n]
            if len(shape) == 1:
                return v
            names = "abcde"[:len(shape)]
            return v.rearrange(f"p ({' '.join(names)}) -> p {' '.join(names)}",
                               **{k: s for k, s in zip(names[1:], shape[1:])})

        K = 256
        hT = at(0, KC, SEQ)
        mixT = at(16 * K, KC, SEQ)
        B = 32 * K
        xt = at(B, NT, DM)
        oT = at(B, KC, SEQ)
        atok = at(B + 16 * K, NT, 1536)
        qkT = at(B + 40 * K, 10, SEQ)
        rt = at(B + 60 * K, 2, 10, HD // 2)
        rope = at(top[0], NT, 2, HD // 2)
        qkn = at(top[0], 2, HD)
        pb = at(top[0], 2, SEQ)
        pT = at(top[0], 2, NT, SEQ)
        tmpA = at(top[0], 2, SEQ)
        vecs = at(top[0], P)
        cvecs = at(top[0], P)
        sqA = at(top[0], 10, HD)
        jA = at(top[0], DM)
        qT = at(B, NH, SEQ)
        kT = at(B + 16 * K, NH, SEQ)
        ktok = at(B + 32 * K, NT, NH, HD)
        vtok = at(B + 48 * K, NT, NH, HD)
        oacc = at(B + 64 * K, NT, NH, HD)
        state = at(B + 80 * K, 2, NH, HD)
        gbuf = at(top[0], 8, NT, 16)
        D = top[0]
        conv = at(D, 2, SEQ)
        cst = at(top[0], 2, SEQ)
        crt = at(top[0], 2, SEQ)
        NB = 12
        grp = [[at(D + (d * NB + n) * 512, 4, P) for n in range(NB)] for d in range(2)]
        glast = at(D + 2 * NB * 512, 2, 4)
        onT = at(B, KC, SEQ)
        mo = at(B + 16 * K, NT, DM)
        x1 = at(B + 32 * K, NT, DM)
        x1T = at(0, KC, SEQ)
        pin = at(B + 48 * K, NT, PLE)
        pinT = at(top[0], 2, SEQ)
        sg = at(B + 64 * K, NT, DM)
        rowv = at(B + 80 * K, DM)
        rowv2 = at(top[0], DM)
        tmpB = at(top[0], 2, SEQ)
        junk = at(top[0], DM)
        xn = at(B + 16 * K, NT, DM)
        h2T = at(0, KC, SEQ)
        hcT = at(16 * K, KC, CTX)
        ctxt = at(24 * K, NTC, DM)
        q2T = at(B, 2, SEQ)
        k2T = at(B + 4 * K, 2, SEQ)
        g2T = at(B + 8 * K, H2, SEQ)
        catT = at(B + 16 * K, KC, SEQ)
        k2 = at(B + 48 * K, NT + NTC, 256)
        v2 = at(top[0], NT + NTC, 512)
        p2 = at(top[0], NT, 512)
        a2T = at(top[0], 2, SEQ + CTX)
        wdec = at(top[0], 2, 256)
        bdec = at(top[0], 512)
        wpool = at(top[0], len(WINDOWS), P)
        gtrow = at(top[0], DM)
        la = at(top[0], NT + NTC, 512)
        G = top[0]
        pm = at(G, 2, NT, SEQ)
        pmT = at(top[0], 2, SEQ)
        jc = at(top[0], DM)
        z2 = at(G, 2, 512)
        z3 = at(top[0], 2, 512)
        kst = at(top[0], NT + NTC, 512)
        eb = at(top[0], 2, SEQ)
        enb = at(top[0], 2, SEQ)
        dec2 = at(top[0], 2, 2, 12)
        swork = at(top[0], 2, 2, 2, P)
        qb = at(0, 2, 2, SEQ)
        kb = at(8 * K, 2, 2, SEQ)
        sprev = at(16 * K, 2, 2, 8, P)
        scm = at(G, 4, SEQ)
        x3 = x1
        yacc = xn
        h3T = h2T
        rowf = at(B, DM)
        rowg = at(B + 4 * K, DM)
        wrt = at(B + 8 * K, KC, 36)
        xg = at(16 * K, 2, DM)
        xe = at(24 * K, 2, KC, CAP)
        sil = at(28 * K, 2, 2 * CAP)
        hid = at(29 * K, 2, 2 * CAP)
        yb = at(0, 2, DM)
        win = at(B + 48 * K, 2, KC, 2 * DE)
        wout = at(top[0], 2, 2, DM)
        rtr = at(top[0], 10, NE)
        lg = at(top[0], 36)
        jr = at(top[0], DM)
        pick = at(top[0], NT, 2, NE)
        picked = at(top[0], NT, NE)
        place = at(top[0], NT, NE)
        ewt = at(top[0], NT, 2)
        eid = at(top[0], NT, 2)
        slot_f = at(top[0], NT, 2)
        slot_u = at(top[0], 2 * NT).bitcast(U32)
        tmax = at(top[0], 16)
        turns_u = at(top[0], 2).bitcast(U32)
        table = at(top[0], 2, CAP)
        index = at(top[0], ROUNDS * NE + 4).bitcast(U32)
        icol = at(top[0], 2).bitcast(U32)
        zero = at(top[0], P)
        ygat = at(top[0], 2, NT, DM)
        back_f = at(top[0], ROUNDS, 2 * NT)
        back_u = at(top[0], ROUNDS, 2 * NT).bitcast(U32)
        bcol = at(top[0], 2 * NT).bitcast(U32)
        tround = at(top[0], NT, 2)

        def scratch(name, *shape):
            return nc.dram_tensor(name, list(shape), F32, kind="Internal").ap()

        xn_dram = scratch("xn_dram", SEQ, DM)
        table_dram = scratch("table_dram", SLOTS, 1)
        y_dram = scratch("y_dram", NE * CAP + 1, DM)
        y_store = y_dram[0:NE * CAP, :].rearrange("(i q c) n -> i q c n", q=XPT, c=CAP)

        psv = ctx.enter_context(nc.psum_tensor("psv", [P, 4, 512], F32))
        pss = ctx.enter_context(nc.psum_tensor("pss", [P, 4, 512], F32))

        names = """chain_v chain_s chain_p phase full_v free_v full_s free_s w_used ld_const ld_vecs ld_x ld_rope
            ld_qkn ld_gpar ld_res ld_p ld_rows ld_ctx ld_small ld_rowf ld_wrt cols_ready xn_ready hT_ready
            rs_in rs_out atok_ready rope_ready qkT_ready negmax_ready probs_ready probsn_ready pT_ready
            oT_ready tmp_ready tmp_used oz_ready ga_ready ga_step gg_ready gG_ready conv_ready silu_ready
            vtok_ready sq_ready rt_ready norm_ready ktok_ready on_ready dz_ready mixT_ready mo_ready
            x1_ready x1T_ready pinT_ready sg_ready x2_ready mod_ready h2_ready hc_ready p2_ready mT_ready
            k2_ready a2_ready z_ready absz_ready lz_ready la_ready bexp_ready qb_ready kexp_ready kst_ready
            sprev_ready sc_ready o2_ready sq2_ready rt2_ready cat_ready x3_ready h3_ready lg_ready
            lexp_ready ld_out moe_used sil_ready hid_ready out_ready picked_ready icol_ready bcol_ready combined yacc_ready xn_saved table_zeroed
            slots_ready scattered table_loaded index_ready xg_k0 xg_k1 xe_ready y1_ready st_y0 st_y1
            ygat_ready turns_ready sil_used pool_used""".split()
        s = {n: sem(n) for n in names}
        for n in ("e_ready glast_ready x_ready d1_ready d2_ready l_ready at_pre at_ready "
                  "c_ready t_ready tt_ready zz_ready kbe_ready kdec_ready qg_ready nwt_ready vn_ready "
                  "group_done").split():
            for d in range(2):
                s[n, d] = sem(f"{n}{d}")
        for k in range(NW):
            s["ld_w", k] = sem(f"ld_w{k}")
        for k in range(2):
            s["ld_win", k] = sem(f"ld_win{k}")
            s["ld_wout", k] = sem(f"ld_wout{k}")
            s["ld_pm", k] = sem(f"ld_pm{k}")

        w1, w2 = a["w_in"][0], a["w_in_2"][0]
        weights = []

        def stream(key, src, col, n):
            weights.append((key, src[:, col:col + n].rearrange("(c p) n -> p c n", p=P), src.shape[0] // P, n))

        for b in range(6):
            stream(("qkv", b), w1, O_AQ + b * WC, WC)
        stream("dbda", w1, O_DB, 32)
        for b in range(4):
            stream(("az", b), w1, O_AZ + b * WC, WC)
        for b in range(4):
            stream(("bra", b), a["w_br_att"][0], b * WC, WC)
            stream(("ga", b), w1, O_GA + b * WC, WC)
        for b in range(12):
            stream(("dqkv", b), w1, O_DQ + b * WC, WC)
        for b in range(24):
            stream(("ada", b), a["w_ada_2"][0], b * WC, WC)
        for b in range(4):
            stream(("dz", b), w1, O_DZ + b * WC, WC)
        for b in range(4):
            stream(("brd", b), a["w_br_dn"][0], b * WC, WC)
            stream(("gd", b), w1, O_GD + b * WC, WC)
        for b in range(4):
            stream(("wo", b), a["w_out"][0], b * WC, WC)
        for b in range(4):
            stream(("pleg", b), a["w_ple_gate"][0], b * WC, WC)
        stream("plep", a["w_ple_proj"][0], 0, DM)
        for key, col, n in (("q2", O2_Q, 256), ("k2", O2_K, 256), (("v2", 0), O2_V, 256), (("v2", 1), O2_V + 256, 256),
                            (("g2", 0), O2_G, 256), (("g2", 1), O2_G + 256, 256), ("a2", O2_A, 32),
                            (("p2", 0), O2_P, 256), (("p2", 1), O2_P + 256, 256)):
            stream(key, w2, col, n)
        for b in range(4):
            stream(("wo2", b), a["w_out_2"][0], b * WC, WC)

        def slot_view(n):
            _, _, kc, m = weights[n]
            return wslot[:, n % NW, 0:kc * m].rearrange("p (c n) -> p c n", c=kc)

        win_src = a["w_expert_in_2"][0].rearrange("(i k) (c p) n -> i k p c n", k=2, p=P)
        wout_src = a["w_expert_out_2"][0].rearrange("(i k) (c p) n -> i k p c n", k=2, p=P)

        win_next, wout_next = win_src[1:NE // 2], wout_src[1:NE // 2]

        def rounds_of(eng):
            eng.wait_ge(s["turns_ready"], 1)
            return eng.value_load(turns_u[0:1, 0:1], min_val=1, max_val=ROUNDS)
        S_ATT = 2 + 24 + 12
        PAIRS = [(st, hg) for st in range(NT) for hg in range(2)]
        C_X, C_D1, C_E, C_C0, C_C1, C_T, C_TT, C_Z, C_VB, C_KBE, C_KDEC, C_VN = range(12)

        def tile_of(d, st):
            return st if d == 0 else NT - 1 - st

        def hcols(d, hg):
            return slice(d * 8 + hg * 4, d * 8 + hg * 4 + 4)

        def spread(v, n=P):
            return v.unsqueeze(2).broadcast_to([P, v.shape[1], n])

        def over(v, m):
            return v.unsqueeze(1).broadcast_to([P, m, v.shape[1]])

        def by4(v):
            return v.rearrange("p (h n) -> p h n", h=4)


        def chunk_at(d, n):
            c = n if n < 4 else n - 4
            if d:
                c = (3 if n < 4 else 7) - c
            return (NT if n < 4 else 0) + c // 2, c % 2

        def chunk_col(d, n):
            t, u = chunk_at(d, n)
            return 2 * t + u

        def state_at(d, m2, n):
            if n < 4:
                return swork[:, n % 2, d, m2, :]
            if n == 12:
                return None
            t, u = chunk_at(d, n)
            return sprev[:, d, m2, 2 * t + u, :]

        block = ctx.enter_context(nc.Block())

        @block.sync
        def _(sp):
            issued = [0]

            def load(dst, src, name):
                sp.dma_start(dst, src).then_inc(s[name], 16)

            def stream_to(key):
                while True:
                    n = issued[0]
                    k, src, _, _ = weights[n]
                    if n >= NW:
                        sp.wait_ge(s["w_used"], n - NW + 1)
                    sp.dma_start(slot_view(n), src).then_inc(s["ld_w", n % NW], 16)
                    issued[0] += 1
                    if k == key:
                        return

            def rows(dst, row, src, n):
                sp.dma_start(dst[row:row + n, :], src.rearrange("(r n) -> r n", n=P)).then_inc(s["ld_vecs"], 16)

            for t in range(NT):
                load(xt[:, t, :], a["x"][0, t * P:(t + 1) * P, :], "ld_x")
            load(const[:, :], a["c_masks"], "ld_const")
            rows(vecs, V_PRE, a["norm_pre"][0], 8)
            rows(vecs, V_DN, a["dn_norm"][0], 1)
            rows(vecs, V_N1, a["norm1_g_2"][0], 8)
            rows(vecs, V_N2, a["norm2_g_2"][0], 8)
            rows(vecs, V_GLA, a["gla_norm_g_2"][0], 1)
            rows(vecs, V_PS, a["pool_scale_2"][0], 4)
            rows(vecs, V_BADA, a["b_ada_2"][0], 48)
            rows(vecs, V_C, a["c_2"][0], 8)
            rows(vecs, V_CC, a["c_ctx_2"], 8)
            rows(cvecs, 0, a["conv_w"][0].rearrange("k c -> (k c)"), CONV_K * 24)
            stream_to(("qkv", 0))
            load(rope, a["c_rope"], "ld_rope")
            load(qkn[:, 0, :], a["q_norm"].partition_broadcast(P), "ld_qkn")
            load(qkn[:, 1, :], a["k_norm"].partition_broadcast(P), "ld_qkn")
            load(gpar[:, 0, :], a["a_log"].rearrange("a d h -> a (d h)").partition_broadcast(P), "ld_gpar")
            load(gpar[:, 1, :], a["dt_bias"].rearrange("a d h -> a (d h)").partition_broadcast(P), "ld_gpar")
            stream_to(("gd", 3))
            sp.wait_ge(s["phase"], 4 * 3)
            load(rowv, a["norm_post"].partition_broadcast(P), "ld_rows")
            load(rowv2, a["ple_norm"].partition_broadcast(P), "ld_rows")
            for t in range(NT):
                load(x1[:, t, :], a["x"][0, t * P:(t + 1) * P, :], "ld_res")
            load(pin, a["p"][0, 0].rearrange("(t p) n -> p t n", p=P), "ld_p")
            stream_to("plep")
            sp.wait_ge(s["phase"], 4 * 4)
            for t in range(NTC):
                load(ctxt[:, t, :], a["ctx_2"][0, t * P:(t + 1) * P, :], "ld_ctx")
            load(wdec[0:RANK, :, :], a["w_decay_2"][0].rearrange("d r k -> r d k"), "ld_small")
            load(bdec[0:1, :], a["b_decay_2"].rearrange("a d k -> a (d k)"), "ld_small")
            load(wpool, a["w_pool_2"][0].rearrange("g c d -> c g d"), "ld_small")
            for g in range(2):
                sp.dma_start(pm[:, g, :, :], a["c_pool"][:, g, :, :]).then_inc(s["ld_pm", g], 16)
            stream_to(("p2", 1))
            for g in range(2, 4):
                sp.wait_ge(s["pool_used"], g - 1)
                sp.dma_start(pm[:, g % 2, :, :], a["c_pool"][:, g, :, :]).then_inc(s["ld_pm", g % 2], 16)
            stream_to(("wo2", 3))
            sp.wait_ge(s["phase"], 4 * 6)
            load(wrt[:, :, 0:4], a["w_router_group_2"][0].rearrange("(c p) n -> p c n", p=P), "ld_wrt")
            load(wrt[:, :, 4:36], a["w_router_expert_2"][0].rearrange("(c p) n -> p c n", p=P), "ld_wrt")
            load(rowf, a["final_norm_g_2"].rearrange("(a n) -> a n", a=1).partition_broadcast(P), "ld_rowf")
            for t in range(NT):
                sp.wait_ge(s["x3_ready"], t + 1)
                load(xn_dram[t * P:(t + 1) * P, :], xn[:, t, :], "xn_saved")
            sp.wait_ge(s["slots_ready"], 1)
            load(table_dram.rearrange("(p n) o -> p (n o)", p=P), zero, "table_zeroed")
            load(y_dram[NE * CAP:, :].rearrange("o (p n) -> (o p) n", p=KC), zero[0:KC, :], "table_zeroed")
            for k in range(2):
                sp.dma_start(win[:, k, :, :], win_src[0, k]).then_inc(s["ld_win", k], 16)
                sp.dma_start(wout[:, k, :, :], wout_src[0, k]).then_inc(s["ld_wout", k], 16)
            sp.wait_ge(s["scattered"], 16 * 2 * NT)
            load(table, table_dram.rearrange("(b p n) o -> p b (n o)", b=2, p=P), "table_loaded")
            rounds = rounds_of(sp)
            with sp.Fori(0, rounds) as r:
                with sp.Fori(0, NE // 2 - 1) as i:
                    for k in range(2):
                        sp.wait_ge(s["moe_used"], r * NE + i * 2 + (k + 1))
                        sp.dma_start(win[:, k, :, :], win_next[i, k]).then_inc(s["ld_win", k], 16)
                        sp.dma_start(wout[:, k, :, :], wout_next[i, k]).then_inc(s["ld_wout", k], 16)
                with sp.If(r + 1 < rounds):
                    for k in range(2):
                        sp.wait_ge(s["moe_used"], r * NE + (NE - 1 + k))
                        sp.dma_start(win[:, k, :, :], win_src[0, k]).then_inc(s["ld_win", k], 16)
                        sp.dma_start(wout[:, k, :, :], wout_src[0, k]).then_inc(s["ld_wout", k], 16)
            for t in range(NT):
                sp.wait_ge(s["out_ready"], t + 1)
                sp.dma_start(out[0, t * P:(t + 1) * P, :], x3[:, t, :]).then_inc(s["ld_out"], 16)
            for name, ap in dumps:
                sp.dma_start(name, ap).then_inc(s["ld_out"], 16)
            sp.wait_ge(s["ld_out"], 16 * (NT + len(dumps)))

        @block.tensor
        def _(pe):
            L = Lane(pe, None)
            jobs = {"v": 0, "s": 0}
            banks = {"v": psv, "s": pss}
            at_slot = [0]
            mm, tr = nc.tensor.matmul, nc.tensor.transpose

            def bank(r):
                n = jobs[r]
                if n >= 4:
                    pe.wait_ge(s["free_" + r], n - 3)
                jobs[r] += 1
                return banks[r][:, n % 4, :]

            def slot(key):
                n = at_slot[0]
                assert weights[n][0] == key, (weights[n][0], key)
                at_slot[0] += 1
                pe.wait_ge(s["ld_w", n % NW], 16 * (n // NW + 1))
                return slot_view(n)

            def used(n=1):
                for _ in range(n):
                    pe.drain().then_inc(s["w_used"], 1)

            def phase(n):
                pe.drain().then_inc(s["phase"], 1)
                pe.wait_ge(s["phase"], 4 * n)

            def product(o, pairs):
                for n, (l, r) in enumerate(pairs):
                    m = mm(o, l, r, start=(n == 0), stop=(n == len(pairs) - 1))
                return m

            def feature_tile(r, w, j, src, kc=KC, n=SEQ):
                o = bank(r)
                product(o[:, 0:n], [(w[:, c, j * P:(j + 1) * P], src[:, c, :]) for c in range(kc)])\
                    .then_inc(s["full_" + r], 1)

            def token_tile(r, w, t, src, c0=0, n=WC, kc=KC):
                o = bank(r)
                product(o[:, 0:n], [(src[:, c, t * P:(t + 1) * P], w[:, c, c0:c0 + n]) for c in range(kc)])\
                    .then_inc(s["full_" + r], 1)

            def turn(r, parts):
                o = bank(r)
                for n, v in enumerate(parts):
                    m = tr(o[:, n * P:n * P + v.shape[0]], v, ident[0:v.shape[0], 0:v.shape[0]])
                m.then_inc(s["full_" + r], 1)

            pe.wait_ge(s["ld_const"], 16)
            pe.wait_ge(s["ld_vecs"], 160)
            turn("s", [vecs[0:V_N, :]])
            turn("s", [cvecs[0:CONV_K * 24, :]])
            for t in range(NT):
                L.need(s["xn_ready"])
                for c0 in (0, 4):
                    turn("v", [xt[:, t, c * P:(c + 1) * P] for c in range(c0, c0 + 4)])
            L.need(s["hT_ready"], 8)
            for b in range(6):
                w = slot(("qkv", b))
                for t in range(NT):
                    token_tile("s", w, t, hT)
                used()
            w = slot("dbda")
            for t in range(NT):
                token_tile("v", w, t, hT, 0, 32)
            used()
            for t in range(NT):
                L.need(s["rope_ready"])
                for h0, n in ((0, 4), (4, 4), (8, 2)):
                    turn("s", [atok[:, t, h * HD:(h + 1) * HD] for h in range(h0, h0 + n)])
            L.need(s["qkT_ready"], 12)
            L.need(s["atok_ready"], 24)
            assert jobs["s"] == S_ATT
            for i in range(NH * NT + 1):
                h, t = divmod(i, NT)
                if i < NH * NT:
                    o = bank("s")
                    mm(o, qkT[:, h, t * P:(t + 1) * P], qkT[:, NH + h // (NH // NKV), :], start=True,
                       stop=True).then_inc(s["full_s"], 1)
                if i >= 1:
                    j = i - 1
                    h, t = divmod(j, NT)
                    L.need(s["probsn_ready"])
                    turn("v", [pb[:, j % 2, k * P:(k + 1) * P] for k in range(NT)])
                    if t == NT - 1:
                        L.need(s["pT_ready"], NT)
                        kv = 1280 + (h // (NH // NKV)) * HD
                        o = bank("v")
                        product(o, [(atok[:, k, kv:kv + HD], pT[:, h % 2, k, :]) for k in range(NT)])\
                            .then_inc(s["full_v"], 1)
            for b in range(4):
                w = slot(("az", b))
                for j in range(2):
                    feature_tile("s", w, j, hT)
                used()
            L.need(s["oz_ready"], KC)
            for b in range(4):
                w, g = slot(("bra", b)), slot(("ga", b))
                for j in range(2):
                    feature_tile("v", w, j, oT)
                    feature_tile("s", g, j, hT)
                used(2)
            phase(1)

            L.need(s["gg_ready"])
            o = bank("v")
            for t in range(NT):
                for d in range(2):
                    m = mm(o[:, t * 16 + d * 8:t * 16 + d * 8 + 8], tri[d], gbuf[:, 0, t, d * 8:d * 8 + 8],
                           start=True, stop=True)
            m.then_inc(s["full_v"], 1)
            for j in range(24 + 1):
                if j < 24:
                    if j % 2 == 0:
                        w = slot(("dqkv", j // 2))
                    feature_tile("v", w, j % 2, hT)
                    if j % 2:
                        used()
                if j > 16:
                    pe.wait_ge(s["silu_ready"], j)
                    turn("s", [cst[:, (j - 1) % 2, t * P:(t + 1) * P] for t in range(NT)])
            for j in range(16 + 2):
                if j < 16:
                    L.need(s["sq_ready"])
                    o = bank("s")
                    mm(o, ones, cst[:, j % 2, :], start=True, stop=True).then_inc(s["full_s"], 1)
                if j >= 2 + 8:
                    pe.wait_ge(s["norm_ready"], j - 1)
                    turn("s", [kT[:, j - 2 - 8, t * P:(t + 1) * P] for t in range(NT)])
            phase(2)

            ada = [0]

            def ada_slot():
                if ada[0] == 24:
                    return
                w = slot(("ada", ada[0]))
                o = bank("s")
                for j in range(2):
                    m = product(o[:, 2 * j:2 * j + 2], [(w[:, c, j * P:(j + 1) * P], csilu[:, c, :])
                                                        for c in range(KC)])
                m.then_inc(s["full_s"], 1)
                used()
                ada[0] += 1

            for n, (st, hg) in enumerate(PAIRS):
                def four(r, make):
                    o = bank(r)
                    for h in range(4):
                        ps = make(h)
                        for q, (l, x) in enumerate(ps):
                            m = mm(o[:, h * P:(h + 1) * P], l, x, start=(q == 0), stop=(q == len(ps) - 1))
                    m.then_inc(s["full_" + r], 1)

                for d in range(2):
                    t = tile_of(d, st)
                    dh = d * 8 + hg * 4
                    four("s", lambda h: [(gbuf[:, 0, t, dh + h:dh + h + 1].broadcast_to([P, P]), tri[d])])
                for d in range(2):
                    tk = slice(tile_of(d, st) * P, (tile_of(d, st) + 1) * P)
                    four("v", lambda h: [(kT[:, hg * 4 + h, tk], kT[:, hg * 4 + h, tk])])
                    four("v", lambda h: [(kT[:, hg * 4 + h, tk], qT[:, hg * 4 + h, tk])])
                for d in range(2):
                    L.need(s["c_ready", d])
                    turn("v", [grp[d][C_C0][:, h, :] for h in range(4)])
                for k in range(1, LEVELS):
                    for d in range(2):
                        g = grp[d]
                        L.need(s["c_ready", d])
                        L.need(s["tt_ready", d])
                        four("s", lambda h: [(g[C_C0 + k % 2][:, h, :], g[C_TT][:, h, :])])
                    if k in (1, 3, 5):
                        ada_slot()
                    for d in range(2):
                        g = grp[d]
                        L.need(s["zz_ready", d])
                        four("v", lambda h: [(g[C_T][:, h, :], g[C_Z][:, h, :])])
                        if k < LEVELS - 1:
                            four("v", lambda h: [(g[C_Z][:, h, :], g[C_T][:, h, :])])
                for d in range(2):
                    L.need(s["kbe_ready", d])
                    L.need(s["tt_ready", d])
                    four("s", lambda h: [(grp[d][C_KBE][:, h, :], grp[d][C_TT][:, h, :])])
                for d in range(2):
                    g = grp[d]
                    L.need(s["nwt_ready", d])
                    if st:
                        pe.wait_ge(s["group_done", d], n - 1)
                    four("v", lambda h: [(g[C_TT][:, h, :], g[C_VB][:, h, :])] +
                         ([(g[C_Z][:, h, :], state[:, d, hg * 4 + h, :])] if st else []))
                for d in range(2):
                    g = grp[d]
                    L.need(s["vn_ready", d])
                    L.need(s["at_ready", d])
                    L.need(s["qg_ready", d])
                    four("v", lambda h: ([(g[C_E][:, h, :], state[:, d, hg * 4 + h, :])] if st else []) +
                         [(g[C_X][:, h, :], g[C_VN][:, h, :])])
                for d in range(2):
                    g = grp[d]
                    L.need(s["kdec_ready", d])
                    four("v", lambda h: [(g[C_KDEC][:, h, :], g[C_VN][:, h, :])])

            phase(3)
            for t in range(NT):
                L.need(s["on_ready"])
                for h0 in (0, 4):
                    turn("v", [oacc[:, t, h, :] for h in range(h0, h0 + 4)])
            for b in range(4):
                w = slot(("dz", b))
                for j in range(2):
                    feature_tile("s", w, j, hT)
                used()
            L.need(s["dz_ready"], KC)
            for b in range(4):
                w, g = slot(("brd", b)), slot(("gd", b))
                for j in range(2):
                    feature_tile("v", w, j, onT)
                    feature_tile("s", g, j, hT)
                used(2)
            L.need(s["mixT_ready"], KC)
            for b in range(4):
                w = slot(("wo", b))
                for t in range(NT):
                    token_tile("s", w, t, mixT)
                used()
            pe.wait_ge(s["ld_p"], 16)
            for t in range(NT):
                turn("v", [pin[:, t, c * P:(c + 1) * P] for c in range(2)])
            for t in range(NT):
                L.need(s["x1_ready"])
                for c0 in (0, 4):
                    turn("v", [x1[:, t, c * P:(c + 1) * P] for c in range(c0, c0 + 4)])
            L.need(s["x1T_ready"], 8)
            for b in range(4):
                w = slot(("pleg", b))
                for t in range(NT):
                    token_tile("s", w, t, x1T)
                used()
            L.need(s["pinT_ready"], NT)
            w = slot("plep")
            for t in range(NT):
                for c0 in (0, 512):
                    token_tile("v", w, t, pinT, c0, 512, 2)
            used()
            phase(4)

            for t in range(NT):
                L.need(s["x2_ready"])
                for c0 in (0, 4):
                    turn("v", [xn[:, t, c * P:(c + 1) * P] for c in range(c0, c0 + 4)])
            for t in range(NTC):
                L.need(s["x2_ready"])
                for c0 in (0, 4):
                    turn("v", [ctxt[:, t, c * P:(c + 1) * P] for c in range(c0, c0 + 4)])
            L.need(s["h2_ready"], 8)
            L.need(s["hc_ready"], 4)
            w = slot("q2")
            for j in range(2):
                feature_tile("s", w, j, h2T)
            used()
            w = slot("k2")
            for j in range(2):
                feature_tile("s", w, j, h2T)
            for t in range(NT):
                token_tile("s", w, t, h2T)
            for t in range(NTC):
                token_tile("s", w, t, hcT)
            used()
            for b in range(2):
                w = slot(("v2", b))
                for t in range(NT):
                    token_tile("v", w, t, h2T)
                for t in range(NTC):
                    token_tile("v", w, t, hcT)
                used()
            for b in range(2):
                w = slot(("g2", b))
                for j in range(2):
                    feature_tile("s", w, j, h2T)
                used()
            w = slot("a2")
            for d in range(2):
                for src, n in ((h2T, SEQ), (hcT, CTX)):
                    o = bank("v")
                    product(o[0:RANK, 0:n], [(w[:, c, d * RANK:(d + 1) * RANK], src[:, c, :]) for c in range(KC)])\
                        .then_inc(s["full_v"], 1)
            used()
            for b in range(2):
                w = slot(("p2", b))
                for t in range(NT):
                    token_tile("v", w, t, h2T)
                used()
            L.need(s["p2_ready"], 2 * NT)
            pe.wait_ge(s["ld_small"], 48)
            for g in range(4 + 1):
                if g < 4:
                    pe.wait_ge(s["ld_pm", g % 2], 16 * (g // 2 + 1))
                    o = bank("v")
                    product(o, [(p2[:, k, g * P:(g + 1) * P], pm[:, g % 2, k, :]) for k in range(NT)])\
                        .then_inc(s["full_v"], 1)
                    pe.drain().then_inc(s["pool_used"], 1)
                if g >= 1:
                    L.need(s["mT_ready"])
                    o = bank("s")
                    mm(o, wpool[:, g - 1, :], pmT[:, (g - 1) % 2, :], start=True, stop=True)\
                        .then_inc(s["full_s"], 1)
            phase(5)

            L.need(s["a2_ready"], 4)
            for t in range(NT + NTC):
                o = bank("s")
                for d in range(2):
                    mm(o[:, d * 256:(d + 1) * 256], a2T[0:RANK, d, t * P:(t + 1) * P], wdec[0:RANK, d, :],
                       start=True, stop=False)
                    m = mm(o[:, d * 256:(d + 1) * 256], ones[0:1, :], bdec[0:1, d * 256:(d + 1) * 256],
                           start=False, stop=True)
                m.then_inc(s["full_s"], 1)
            L.need(s["la_ready"], NT + NTC)
            for d in range(2):
                for m2 in range(2):
                    col = d * 256 + m2 * P
                    o = bank("s")
                    for t in range(NT):
                        m = mm(o[:, t * P:(t + 1) * P], la[:, t, col:col + P], blk[d], start=True, stop=True)
                    m.then_inc(s["full_s"], 1)
                    o = bank("s")
                    for t in range(NTC):
                        m = mm(o[:, t * P:(t + 1) * P], la[:, NT + t, col:col + P], blk[d], start=True, stop=True)
                    m.then_inc(s["full_s"], 1)
            for t in range(NT + NTC):
                o = bank("s")
                for d in range(2):
                    m = mm(o[:, d * 256:(d + 1) * 256], blk_rest[d], la[:, t, d * 256:(d + 1) * 256],
                           start=True, stop=True)
                m.then_inc(s["full_s"], 1)
            L.need(s["kst_ready"], NT + NTC)
            L.need(s["k2_ready"])
            for n in range(12):
                for d in range(2):
                    t, u = chunk_at(d, n)
                    o = bank("v")
                    for m2 in range(2):
                        m = mm(o[:, m2 * 256:(m2 + 1) * 256],
                               kst[u * CH2:(u + 1) * CH2, t, d * 256 + m2 * P:d * 256 + (m2 + 1) * P],
                               v2[u * CH2:(u + 1) * CH2, t, m2 * 256:(m2 + 1) * 256], start=True, stop=True)
                    m.then_inc(s["full_v"], 1)
            L.need(s["qb_ready"], 4)
            L.need(s["sprev_ready"])
            for h in range(H2):
                m2, hp = h // 2, slice((h % 2) * 64, (h % 2) * 64 + 64)
                for d in range(2):
                    o = bank("v")
                    for t in range(NT):
                        tk = slice(t * P, (t + 1) * P)
                        m = mm(o[:, tk], kb[hp, d, m2, tk], qb[hp, d, m2, tk], start=True, stop=True)
                    m.then_inc(s["full_v"], 1)
                L.need(s["sc_ready"], 2)
                o = bank("s")
                for d in range(2):
                    for t in range(NT):
                        tk = slice(t * P, (t + 1) * P)
                        mm(o[:, tk], v2[:, t, h * P:(h + 1) * P], scm[:, (h % 2) * 2 + d, tk],
                           start=(d == 0 and t == 0), stop=False, skip_group_check=True)
                    for c in range(8):
                        ck = slice(c * CH2, (c + 1) * CH2)
                        m = mm(o[:, ck], sprev[hp, d, m2, c, :], qb[hp, d, m2, ck], start=False,
                               stop=(d == 1 and c == 7), skip_group_check=True)
                m.then_inc(s["full_s"], 1)
                L.need(s["sq2_ready"])
                o = bank("s")
                mm(o, ones, eb[:, h % 2, :], start=True, stop=True).then_inc(s["full_s"], 1)
            L.need(s["cat_ready"], 8)
            for c0 in (0, 4):
                o = bank("v")
                for c in range(4):
                    m = mm(o[:, c * P:(c + 1) * P], mod[:, 16 + c0 + c, 0:1].broadcast_to([P, P]), ident,
                           start=True, stop=True)
                m.then_inc(s["full_v"], 1)
            for b in range(4):
                w = slot(("wo2", b))
                for t in range(NT):
                    token_tile("v", w, t, catT)
                used()
            phase(6)

            for t in range(NT):
                L.need(s["x3_ready"])
                for c0 in (0, 4):
                    turn("v", [xn[:, t, c * P:(c + 1) * P] for c in range(c0, c0 + 4)])
            L.need(s["h3_ready"], 8)
            pe.wait_ge(s["ld_wrt"], 32)
            for t in range(NT):
                token_tile("v", wrt, t, h3T, 0, 36)
            for c0 in (0, 4):
                o = bank("v")
                for c in range(4):
                    m = mm(o[:, c * P:(c + 1) * P], mod[:, 40 + c0 + c, 0:1].broadcast_to([P, P]), ident,
                           start=True, stop=True)
                m.then_inc(s["full_v"], 1)
            L.need(s["picked_ready"], NT)
            for t in range(NT):
                o = bank("v")
                product(o[:, 0:NE], [(ones, picked[:, q, :]) for q in range(t)] +
                        [(const[:, C_LT:C_LT + P], picked[:, t, :])]).then_inc(s["full_v"], 1)
            o = bank("v")
            product(o[:, 0:NE], [(ones, picked[:, q, :]) for q in range(NT)]).then_inc(s["full_v"], 1)
            pe.wait_ge(s["table_loaded"], 16)
            turn_slots = bank("v")
            for k in range(2):
                m = tr(turn_slots[0:CAP, k * P:(k + 1) * P], table[:, k, :], ident)
            m.then_inc(s["full_v"], 1)
            pe.wait_ge(s["xg_k0"], 16)
            o = bank("v")
            for c in range(KC):
                m = tr(o[:, c * CAP:(c + 1) * CAP], xg[0:CAP, 0, c * P:(c + 1) * P], ident[0:CAP, 0:CAP])
            m.then_inc(s["full_v"], 1)
            v0, s0 = jobs["v"], jobs["s"]
            VJ, SJ = 3 * XPT, 2 * XPT
            rounds = rounds_of(pe)
            with pe.Fori(0, rounds * (NE // XPT)) as i:
                nv, ns = [0], [0]

                def vbank():
                    k = nv[0]
                    nv[0] += 1
                    pe.wait_ge(s["free_v"], i * VJ + (v0 + k - 3))
                    return psv[:, (v0 + k) % 4, :]

                def sbank():
                    k = ns[0]
                    ns[0] += 1
                    pe.wait_ge(s["free_s"], i * SJ + (s0 + k - 3))
                    return pss[:, (s0 + k) % 4, :]

                for q in range(XPT):
                    k = q % 2
                    nth = i * (XPT // 2) + (q // 2 + 1)
                    pe.wait_ge(s["ld_win", k], nth * 16)
                    pe.wait_ge(s["xe_ready"], i * XPT + (q + 1))
                    pe.wait_ge(s[f"xg_k{1 - k}"], nth * 16 if k == 0 else nth * 16 + 16)
                    a_bank, u_bank, turn_bank = sbank(), vbank(), vbank()
                    for o, full, c0 in ((a_bank, "full_s", 0), (u_bank, "full_v", DE)):
                        for j in range(2):
                            m = product(o[:, j * CAP:(j + 1) * CAP],
                                        [(win[:, k, c, c0 + j * P:c0 + (j + 1) * P], xe[:, k, c, :])
                                         for c in range(KC)])
                        m.then_inc(s[full], 1)
                    for c in range(KC):
                        m = tr(turn_bank[:, c * CAP:(c + 1) * CAP], xg[0:CAP, 1 - k, c * P:(c + 1) * P],
                               ident[0:CAP, 0:CAP])
                    m.then_inc(s["full_v"], 1)
                    pe.wait_ge(s["hid_ready"], i * XPT + (q + 1))
                    pe.wait_ge(s["ld_wout", k], nth * 16)
                    for get, full, c0 in ((sbank, "full_s", 0), (vbank, "full_v", 512)):
                        product(get()[0:CAP, :], [(hid[:, k, c * CAP:(c + 1) * CAP], wout[:, k, c, c0:c0 + 512])
                                                  for c in range(2)]).then_inc(s[full], 1)
                    pe.drain().then_inc(s["moe_used"], 1)

        @block.scalar
        def _(act):
            L = Lane(act, s["chain_s"])
            seen = [0]
            A = nc.scalar.activation

            def full():
                L.need(s["full_s"])
                seen[0] += 1
                return pss[:, (seen[0] - 1) % 4, :]

            def evict(dst, n, sig, func=ACT.Copy, **kw):
                b = full()
                src = b[:, 0:n]
                if len(dst.shape) == 3:
                    src = src.rearrange("p (a b) -> p a b", b=dst.shape[2])
                L.did(A(dst, src, func, **kw), s[sig], [s["free_s"]])

            def root(v):
                L.need(s["rs_in"])
                L.did(A(v, v, ACT.Sqrt), s["rs_out"])

            def phase(n):
                act.sem_inc(s["phase"])
                act.wait_ge(s["phase"], 4 * n)

            evict(cols[:, 0:V_N], V_N, "cols_ready")
            evict(ccols[:, :], CONV_K * 24, "cols_ready")
            L.did(A(csilu[:, :, :].rearrange("p c k -> p k c"),
                    cols[:, V_C:V_C + 16].rearrange("p (k c) -> p k c", k=2), ACT.Silu))
            root(ss[:, 0:NT])
            for b in range(6):
                for t in range(NT):
                    evict(atok[:, t, b * WC:(b + 1) * WC], WC, "atok_ready")
            for t in range(NT):
                root(ss[:, 16:26])
                if t >= 1:
                    for h0, n in ((0, 4), (4, 4), (8, 2)):
                        evict(qkT[:, h0:h0 + n, (t - 1) * P:t * P], n * P, "qkT_ready")
            for h0, n in ((0, 4), (4, 4), (8, 2)):
                evict(qkT[:, h0:h0 + n, (NT - 1) * P:NT * P], n * P, "qkT_ready")
            for i in range(NH * NT):
                L.need(s["negmax_ready"])
                b = full()
                if i >= 2:
                    act.wait_ge(s["pT_ready"], i - 1)
                L.did(A(pb[:, i % 2, :], b, ACT.Exp, bias=small[:, 64 + i:65 + i], scale=HD ** -0.5,
                        accum_out=small[:, 96 + i:97 + i]), s["probs_ready"], [s["free_s"]])
            ntmp = [0]

            def gate(tmp, func):
                n = ntmp[0]
                ntmp[0] += 1
                if n >= 2:
                    act.wait_ge(s["tmp_used"], n - 1)
                evict(tmp[:, n % 2, :], SEQ, "tmp_ready", func)

            for j in range(KC):
                gate(tmpA, ACT.Silu)
            for j in range(KC):
                gate(tmpA, ACT.Sigmoid)
            phase(1)

            act.wait_ge(s["ld_gpar"], 32)
            L.did(A(gpar[:, 2, :], gpar[:, 0, :], ACT.Exp), s["ga_ready"])
            L.need(s["ga_step"])
            L.did(A(gbuf[:, 6, :, :], gbuf[:, 6, :, :], ACT.Exp))
            L.did(A(gbuf[:, 6, :, :], gbuf[:, 6, :, :], ACT.Ln, bias=one), s["ga_ready"])
            L.did(A(gbuf[:, 3, :, :], gb[:, :, 0:16], ACT.Sigmoid), s["ga_ready"])
            L.need(s["gG_ready"])
            L.did(A(gbuf[:, 2, :, :], gbuf[:, 1, :, :], ACT.Exp), s["ga_ready"])
            for j in range(24 + 1):
                if j < 24:
                    L.need(s["conv_ready"])
                    dst = qT[:, j, :] if j < 8 else kT[:, j - 8, :] if j < 16 else cst[:, j % 2, :]
                    L.did(A(dst, conv[:, j % 2, :], ACT.Silu), s["silu_ready"])
                if j > 16:
                    evict(vtok[:, :, j - 17, :], SEQ, "vtok_ready")
            for j in range(16 + 3):
                if j < 16:
                    src = qT[:, j, :] if j < 8 else kT[:, j - 8, :]
                    L.did(A(cst[:, j % 2, :], src, ACT.Square), s["sq_ready"])
                if 1 <= j <= 16:
                    n = j - 1
                    if n >= 2:
                        act.wait_ge(s["norm_ready"], n - 1)
                    if n < 8:
                        evict(crt[:, n % 2, :], SEQ, "rt_ready", ACT.Sqrt, bias=eps128, scale=float(HD))
                    else:
                        evict(crt[:, n % 2, :], SEQ, "rt_ready", ACT.Sqrt, bias=eps)
                if j >= 3 + 8:
                    evict(ktok[:, :, j - 3 - 8, :], SEQ, "ktok_ready")
            phase(2)

            ada = [0]

            def ada_slot():
                if ada[0] < 24:
                    evict(mod[:, 2 * ada[0]:2 * ada[0] + 2, :], 4, "mod_ready")
                    ada[0] += 1

            for n, (st, hg) in enumerate(PAIRS):
                for d in range(2):
                    g = grp[d]
                    if n:
                        L.need(s["group_done", d])
                    b = full()
                    L.did(A(g[C_X], by4(b), ACT.Copy))
                    L.did(A(g[C_E], by4(b), ACT.Exp), s["e_ready", d], [s["free_s"]])
                    last = P - 1 if d == 0 else 0
                    L.did(A(glast[:, d, :], g[C_E][:, :, last], ACT.Copy), s["glast_ready", d])
                for d in range(2):
                    g = grp[d]
                    L.need(s["x_ready", d])
                    L.did(A(g[C_D1], g[C_D1], ACT.Exp, scale=-1.0), s["d1_ready", d])
                    L.did(A(g[C_X], g[C_X], ACT.Exp), s["d2_ready", d])
                for k in range(1, LEVELS):
                    for d in range(2):
                        b = full()
                        L.did(A(grp[d][C_Z], by4(b), ACT.Copy), s["zz_ready", d], [s["free_s"]])
                    if k in (1, 3, 5):
                        ada_slot()
                for d in range(2):
                    b = full()
                    L.did(A(grp[d][C_Z], by4(b), ACT.Copy, scale=-1.0), s["nwt_ready", d], [s["free_s"]])
            for d in range(2):
                L.need(s["group_done", d])
            phase(3)

            root(ss[:, 0:32])
            for j in range(KC):
                gate(tmpB, ACT.Silu)
            for j in range(KC):
                gate(tmpB, ACT.Sigmoid)
            for b in range(4):
                for t in range(NT):
                    evict(mo[:, t, b * WC:(b + 1) * WC], WC, "mo_ready")
            root(ss[:, 0:NT])
            for b in range(4):
                for t in range(NT):
                    evict(sg[:, t, b * WC:(b + 1) * WC], WC, "sg_ready", ACT.Sigmoid)
            root(ss[:, 0:NT])
            phase(4)

            root(ss[:, 0:NT])
            root(ss[:, 0:NTC])
            for j in range(2):
                evict(q2T[:, j, :], SEQ, "k2_ready", ACT.Copy, scale=DK2 ** -0.5)
            for j in range(2):
                evict(k2T[:, j, :], SEQ, "k2_ready")
            for t in range(NT + NTC):
                evict(k2[:, t, :], 256, "k2_ready")
            for j in range(4):
                evict(g2T[:, j, :], SEQ, "k2_ready", ACT.Silu)
            for g in range(4):
                b = full()
                L.did(A(catT[:, 4 + g, :], b, ACT.Copy, scale=cols[:, V_PS + g:V_PS + g + 1]), s["cat_ready"], [s["free_s"]])
            phase(5)

            for t in range(NT + NTC):
                b = full()
                if t >= 2:
                    act.wait_ge(s["la_ready"], t - 1)
                L.did(A(z2[:, t % 2, :], b, ACT.Copy), s["z_ready"], [s["free_s"]])
                L.need(s["absz_ready"])
                L.did(A(z3[:, t % 2, :], z3[:, t % 2, :], ACT.Exp, scale=-1.0))
                L.did(A(z3[:, t % 2, :], z3[:, t % 2, :], ACT.Ln, bias=one), s["lz_ready"])
            for n in range(4):
                d, m2 = divmod(n, 2)
                b = full()
                if n >= 2:
                    act.wait_ge(s["qb_ready"], n - 1)
                L.did(A(eb[:, n % 2, :], b, ACT.Exp))
                L.did(A(enb[:, n % 2, :], b, ACT.Exp, scale=-1.0))
                ends = b.rearrange("p (c i) -> p c i", i=CH2)[:, :, CH2 - 1 if d == 0 else 0]
                L.did(A(dec2[:, d, m2, 0:8], ends, ACT.Exp), s["bexp_ready"], [s["free_s"]])
                b = full()
                ends = b[:, 0:CTX].rearrange("p (c i) -> p c i", i=CH2)[:, :, CH2 - 1 if d == 0 else 0]
                L.did(A(dec2[:, d, m2, 8:12], ends, ACT.Exp), s["bexp_ready"], [s["free_s"]])
            for t in range(NT + NTC):
                evict(kst[:, t, :], 512, "kexp_ready", ACT.Exp)
            L.need(s["qb_ready"], 4)
            for h in range(H2):
                b = full()
                if h >= 2:
                    act.wait_ge(s["o2_ready"], h - 1)
                L.did(A(eb[:, h % 2, :], b, ACT.Square), s["sq2_ready"])
                L.did(A(catT[:, h, :], b, ACT.Copy), s["rt2_ready"], [s["free_s"]])
                b = full()
                L.did(A(enb[:, h % 2, :], b, ACT.Sqrt, bias=eps, scale=1.0 / DV2), s["rt2_ready"], [s["free_s"]])
            phase(6)

            root(ss[:, 0:NT])
            for t in range(NT):
                L.need(s["lg_ready"])
                L.did(A(rtr[:, 7, 0:4], lg[:, 0:4], ACT.Exp, bias=rtr[:, 8, 0:1], accum_out=rtr[:, 8, 1:2]),
                      s["lexp_ready"])
                L.need(s["lg_ready"])
                L.did(A(rtr[:, 8, 2:3], rtr[:, 8, 2:3], ACT.Exp), s["lexp_ready"])
            q0 = seen[0]
            act.sem_inc(s["st_y0"], 16)
            act.sem_inc(s["st_y1"], 16)
            rounds = rounds_of(act)
            with act.Fori(0, rounds) as r:
                act.wait_ge(s["combined"], r + 1)
                with act.Fori(0, NE // XPT) as ir:
                    i = r * (NE // XPT) + ir
                    L.enter(i, {s["sil_ready"]: XPT, s["free_s"]: 2 * XPT, s["chain_s"]: XPT},
                            {s["full_s"]: 2 * XPT, s["sil_used"]: XPT, s["y1_ready"]: XPT})
                    for q in range(XPT):
                        k = q % 2
                        L.need(s["full_s"])
                        L.need(s["sil_used"])
                        L.did(A(sil[:, k, :], pss[:, (q0 + 2 * q) % 4, 0:2 * CAP], ACT.Silu), s["sil_ready"],
                              [s["free_s"]])
                        L.need(s["full_s"])
                        act.wait_ge(s[f"st_y{k}"], (i * (XPT // 2) + (q // 2 + 1)) * 16)
                        L.did(A(yb[0:CAP, k, 0:512], pss[0:CAP, (q0 + 2 * q + 1) % 4, :], ACT.Copy), None,
                              [s["free_s"]])
                        L.need(s["y1_ready"])
                        act.dma_start(y_store[ir, q], yb[0:CAP, k, :]).then_inc(s[f"st_y{k}"], 16)
                    L.leave(0)
            root(ss[:, 0:NT])

        @block.gpsimd
        def _(pool):
            L = Lane(pool, s["chain_p"])
            TT = nc.gpsimd.tensor_tensor

            def phase(n):
                pool.sem_inc(s["phase"])
                pool.wait_ge(s["phase"], 4 * n)

            phase(1)
            pool.wait_ge(s["phase"], 4)
            phase(2)
            for n, (st, hg) in enumerate(PAIRS):
                H4 = slice(hg * 4, hg * 4 + 4)
                for d in range(2):
                    g, t = grp[d], tile_of(d, st)
                    if n:
                        L.need(s["group_done", d])
                    L.did(TT(g[C_VB], vtok[:, t, H4, :], spread(gbuf[:, 3, t, hcols(d, hg)]), ALU.mult))
                    L.did(TT(g[C_KBE], ktok[:, t, H4, :], spread(gbuf[:, 4, t, hcols(d, hg)]), ALU.mult),
                          s["kbe_ready", d])
                for d in range(2):
                    g = grp[d]
                    L.need(s["l_ready", d])
                    for k in range(2):
                        lv = const[:, C_LV + (d * LEVELS + k) * P:C_LV + (d * LEVELS + k + 1) * P]
                        L.did(TT(g[C_C0 + k], g[C_D1], over(lv, 4), ALU.mult), s["c_ready", d])
                for k in range(2, LEVELS):
                    for d in range(2):
                        g, t = grp[d], tile_of(d, st)
                        if k == 2:
                            L.need(s["t_ready", d])
                        else:
                            L.need(s["zz_ready", d])
                        lv = const[:, C_LV + (d * LEVELS + k) * P:C_LV + (d * LEVELS + k + 1) * P]
                        L.did(TT(g[C_C0 + k % 2], g[C_D1], over(lv, 4), ALU.mult), s["c_ready", d])
                        if k == 2:
                            L.need(s["at_pre", d])
                            L.did(TT(g[C_X], g[C_X], over(tri[d], 4), ALU.mult), s["at_ready", d])
                        if k == 3:
                            L.did(TT(g[C_KDEC], ktok[:, t, H4, :], spread(kcol[:, d, :]), ALU.mult),
                                  s["kdec_ready", d])
                        if k == 4:
                            L.need(s["e_ready", d])
                            L.need(s["glast_ready", d])
                            L.did(TT(g[C_E], g[C_E], qT[:, H4, t * P:(t + 1) * P], ALU.mult), s["qg_ready", d])
                for d in range(2):
                    L.need(s["zz_ready", d], 2)
            phase(3)
            phase(4)
            phase(5)
            phase(6)

            pool.wait_ge(s["xn_saved"], 16 * NT)
            pool.wait_ge(s["table_zeroed"], 32)
            for t in range(NT):
                for k in range(2):
                    nc.gpsimd.indirect_dma_start(
                        table_dram, bass.IndirectOffsetOnAxis(slot_u[:, 2 * t + k:2 * t + k + 1], 0),
                        const[:, C_TOK + t:C_TOK + t + 1], None).then_inc(s["scattered"], 16)

            def gather(k):
                nc.gpsimd.indirect_dma_start(
                    xg[0:CAP, k, :], None, xn_dram, bass.IndirectOffsetOnAxis(icol[0:CAP, k:k + 1], 0))\
                    .then_inc(s[f"xg_k{k}"], 16)

            L.need(s["index_ready"])
            for k in range(2):
                L.did(nc.gpsimd.tensor_copy(icol[0:CAP, k:k + 1], index[0:CAP, k:k + 1]))
                gather(k)
            rounds = rounds_of(pool)
            with pool.Fori(0, rounds) as r:
                with pool.Fori(0, NE // XPT) as ir:
                    i = r * (NE // XPT) + ir
                    for q in range(XPT):
                        k = q % 2
                        pool.wait_ge(s["xe_ready"], i * XPT + (q + 1))
                        nc.gpsimd.tensor_copy(icol[0:CAP, k:k + 1], index[0:CAP, bass.ds(i * XPT + (q + 2), 1)])\
                            .then_inc(s["icol_ready"], 1)
                        pool.wait_ge(s["icol_ready"], 1)
                        gather(k)
                        pool.sem_inc(s["icol_ready"], -1)
                for k in range(2):
                    pool.wait_ge(s[f"st_y{k}"], r * (NE // 2 * 16) + (NE // 2 * 16 + 16))
                pool.wait_ge(s["combined"], r + 1)
                nc.gpsimd.tensor_copy(bcol, back_u[:, bass.ds(r, 1), :].rearrange("p o n -> p (o n)"))\
                    .then_inc(s["bcol_ready"], 1)
                pool.wait_ge(s["bcol_ready"], 1)
                for t in range(NT):
                    for k in range(2):
                        nc.gpsimd.indirect_dma_start(
                            ygat[:, k, t, :], None, y_dram,
                            bass.IndirectOffsetOnAxis(bcol[:, 2 * t + k:2 * t + k + 1], 0))\
                            .then_inc(s["ygat_ready"], 16)
                pool.sem_inc(s["bcol_ready"], -1)
            for k in range(2):
                pool.wait_ge(s[f"xg_k{k}"], rounds * (NE // 2 * 16) + 16)

        @block.vector
        def _(dve):
            L = Lane(dve, s["chain_v"])
            seen = [0]
            V = nc.vector

            def full():
                L.need(s["full_v"])
                seen[0] += 1
                return psv[:, (seen[0] - 1) % 4, :]

            def phase(n):
                dve.sem_inc(s["phase"])
                dve.wait_ge(s["phase"], 4 * n)

            def squares(v, dst, j):
                L.did(V.tensor_tensor_reduce(j, v, v, 1.0, 0.0, ALU.mult, ALU.add, dst))

            def inv_root(v, n):
                L.did(V.tensor_scalar(v, v, 1.0 / n, EPS, ALU.mult, ALU.add), s["rs_in"])
                L.need(s["rs_out"])
                L.did(V.reciprocal(v, v))

            def mul(o, x, y, *sig):
                L.did(V.tensor_tensor(o, x, y, ALU.mult), *sig)

            def add(o, x, y, *sig):
                L.did(V.tensor_tensor(o, x, y, ALU.add), *sig)

            def scale(o, x, c, *sig):
                L.did(V.tensor_scalar(o, x, c, None, ALU.mult), *sig)

            def turned(dst, t, gains, shifts, sig, tiles=2):
                for c0 in (0, 4):
                    b = full()
                    o = dst[:, c0:c0 + 4, t * P:(t + 1) * P]
                    if shifts is None:
                        mul(o, by4(b), spread(gains[:, c0:c0 + 4]), s[sig], [s["free_v"]])
                    else:
                        mul(o, by4(b), spread(gains[:, c0:c0 + 4]), None, [s["free_v"]])
                        add(o, o, spread(shifts[:, c0:c0 + 4]), s[sig])

            for t in range(NT):
                if t == 0:
                    dve.wait_ge(s["ld_x"], 64)
                squares(xt[:, t, :], ss[:, t:t + 1], jA)
            inv_root(ss[:, 0:NT], DM)
            for t in range(NT):
                scale(xt[:, t, :], xt[:, t, :], ss[:, t:t + 1], s["xn_ready"])
            L.need(s["cols_ready"], 2)
            for t in range(NT):
                turned(hT, t, cols[:, V_PRE:V_PRE + 8], None, "hT_ready")
            for t in range(NT):
                b = full()
                L.did(V.tensor_copy(gb[:, t, :], b[:, 0:32]), s["free_v"])
            dve.wait_ge(s["ld_rope"], 16)
            dve.wait_ge(s["ld_qkn"], 32)
            for t in range(NT):
                dve.wait_ge(s["atok_ready"], 17 + t)
                v = atok[:, t, 0:1280].rearrange("p (h n) -> p h n", h=10)
                mul(sqA, v, v)
                L.did(V.tensor_reduce(ss[:, 16:26], sqA, AXX, ALU.add))
                inv_root(ss[:, 16:26], HD)
                mul(v, v, spread(ss[:, 16:26]))
                mul(v[:, 0:8, :], v[:, 0:8, :], over(qkn[:, 0, :], 8))
                mul(v[:, 8:10, :], v[:, 8:10, :], over(qkn[:, 1, :], 2))
                pr = atok[:, t, 0:1280].rearrange("p (h n two) -> p h n two", h=10, two=2)
                x0, x1_ = pr[:, :, :, 0], pr[:, :, :, 1]
                cos, sin = over(rope[:, t, 0, :], 10), over(rope[:, t, 1, :], 10)
                sq4 = sqA.rearrange("p h (u n) -> p u h n", u=2)
                mul(rt[:, 0], x0, cos)
                mul(rt[:, 1], x1_, sin)
                mul(sq4[:, 0], x0, sin)
                mul(sq4[:, 1], x1_, cos)
                L.did(V.tensor_tensor(x0, rt[:, 0], rt[:, 1], ALU.subtract))
                add(x1_, sq4[:, 0], sq4[:, 1], s["rope_ready"])
            for i in range(NH * NT + 1):
                if i < NH * NT:
                    dve.wait_ge(s["full_s"], S_ATT + i + 1)
                    c = small[:, 64 + i:65 + i]
                    L.did(V.tensor_reduce(c, pss[:, (S_ATT + i) % 4, :], AXX, ALU.max))
                    scale(c, c, -HD ** -0.5, s["negmax_ready"])
                if i >= 1:
                    j = i - 1
                    h, t = divmod(j, NT)
                    L.need(s["probs_ready"])
                    r = small[:, 96 + j:97 + j]
                    L.did(V.reciprocal(r, r))
                    scale(pb[:, j % 2, :], pb[:, j % 2, :], r, s["probsn_ready"])
                    b = full()
                    if h >= 2 and t == 0:
                        dve.wait_ge(s["oT_ready"], h - 1)
                    L.did(V.tensor_copy(pT[:, h % 2, :, t * P:(t + 1) * P], by4(b)), s["pT_ready"], [s["free_v"]])
                    if t == NT - 1:
                        b = full()
                        L.did(V.tensor_copy(oT[:, h, :], b), s["oT_ready"], [s["free_v"]])
            ntmp = [0]

            def tmp_of(tmp):
                L.need(s["tmp_ready"])
                ntmp[0] += 1
                return tmp[:, (ntmp[0] - 1) % 2, :]

            for j in range(KC):
                mul(oT[:, j, :], oT[:, j, :], tmp_of(tmpA), s["oz_ready"], [s["tmp_used"]])
            for j in range(KC):
                b = full()
                mul(mixT[:, j, :], b, tmp_of(tmpA), s["tmp_used"], [s["free_v"]])
            phase(1)

            gz = [gbuf[:, k, :, :] for k in range(8)]
            dve.wait_ge(s["ld_gpar"], 32)
            add(gz[5], gb[:, :, 16:32], over(gpar[:, 1, :], NT))
            L.did(V.scalar_tensor_tensor(gz[6], gz[5], -1.0, gz[5], ALU.mult, ALU.max))
            scale(gz[6], gz[6], -1.0, s["ga_step"])
            L.need(s["ga_ready"], 3)
            L.did(V.scalar_tensor_tensor(gz[5], gz[5], 0.0, gz[6], ALU.max, ALU.add))
            L.did(V.scalar_tensor_tensor(gz[0], gz[5], -1.0, over(gpar[:, 2, :], NT), ALU.mult, ALU.mult),
                  s["gg_ready"])
            b = full()
            L.did(V.tensor_copy(gz[1], b[:, 0:64].rearrange("p (t n) -> p t n", t=NT)), s["gG_ready"],
                  [s["free_v"]])
            L.need(s["ga_ready"])
            mul(gz[4], gz[3], gz[2])
            for j in range(24):
                b = full()
                if j >= 2:
                    dve.wait_ge(s["silu_ready"], j - 1)
                o = conv[:, j % 2, :]
                taps = [ccols[:, k * 24 + j:k * 24 + j + 1] for k in range(CONV_K)]
                scale(o, b, taps[2])
                for k in (0, 1, 3, 4):
                    m = k - 2
                    lo, hi = max(0, -m), SEQ - max(0, m)
                    L.did(V.scalar_tensor_tensor(o[:, lo:hi], b[:, lo + m:hi + m], taps[k], o[:, lo:hi],
                                                 ALU.mult, ALU.add),
                          s["conv_ready"] if k == 4 else None, [s["free_v"]] if k == 4 else [])
            for j in range(16):
                L.need(s["rt_ready"])
                r = crt[:, j % 2, :]
                L.did(V.reciprocal(r, r))
                v = qT[:, j, :] if j < 8 else kT[:, j - 8, :]
                mul(v, v, r, s["norm_ready"])
            phase(2)

            for n, (st, hg) in enumerate(PAIRS):
                for d in range(2):
                    g, t = grp[d], tile_of(d, st)
                    L.need(s["e_ready", d])
                    x = g[C_X]
                    L.did(V.tensor_tensor(x, x, spread(gbuf[:, 1, t, hcols(d, hg)]), ALU.subtract))
                    L.did(V.tensor_scalar(g[C_D1], x, 0.0, None, ALU.max))
                    L.did(V.tensor_scalar(x, x, 0.0, None, ALU.min), s["x_ready", d])
                for d in range(2):
                    g, t = grp[d], tile_of(d, st)
                    L.need(s["d1_ready", d])
                    b = full()
                    mul(g[C_D1], by4(b), g[C_D1], s["free_v"])
                    mul(g[C_D1], g[C_D1], spread(gbuf[:, 3, t, hcols(d, hg)]), s["l_ready", d])
                    L.need(s["d2_ready", d])
                    last = P - 1 if d == 0 else 0
                    L.did(V.tensor_copy(kcol[:, d, :], g[C_X][:, :, last]))
                    b = full()
                    mul(g[C_X], by4(b), g[C_X], s["at_pre", d], [s["free_v"]])
                for d in range(2):
                    g = grp[d]
                    L.need(s["c_ready", d])
                    b = full()
                    L.did(V.tensor_tensor(g[C_T], over(ident, 4), g[C_C0], ALU.subtract))
                    L.did(V.tensor_tensor(g[C_TT], over(ident, 4), by4(b), ALU.subtract), s["tt_ready", d],
                          [s["free_v"], s["t_ready", d]])
                for k in range(1, LEVELS):
                    for d in range(2):
                        g = grp[d]
                        b = full()
                        if k < LEVELS - 1:
                            b2 = full()
                            L.did(V.tensor_tensor(g[C_T], g[C_T], by4(b2), ALU.subtract))
                        L.did(V.tensor_tensor(g[C_TT], g[C_TT], by4(b), ALU.subtract), s["tt_ready", d],
                              [s["free_v"]] * (2 if k < LEVELS - 1 else 1))
                for d in range(2):
                    b = full()
                    L.did(V.tensor_copy(grp[d][C_VN], by4(b)), s["vn_ready", d], [s["free_v"]])
                for d in range(2):
                    t = tile_of(d, st)
                    o = oacc[:, t, hg * 4:hg * 4 + 4, :]
                    b = full()
                    if st < NT // 2:
                        L.did(V.tensor_copy(o, by4(b)), s["free_v"])
                    else:
                        add(o, o, by4(b), s["free_v"])
                for d in range(2):
                    L.need(s["glast_ready", d])
                    b = full()
                    if st == 0:
                        L.did(V.tensor_copy(state[:, d, hg * 4:hg * 4 + 4, :], by4(b)), s["group_done", d],
                              [s["free_v"]])
                    else:
                        for h in range(4):
                            v = state[:, d, hg * 4 + h, :]
                            L.did(V.scalar_tensor_tensor(v, v, glast[:, d, h:h + 1], b[:, h * P:(h + 1) * P],
                                                         ALU.mult, ALU.add),
                                  s["group_done", d] if h == 3 else None, [s["free_v"]] if h == 3 else [])
            phase(3)

            for t in range(NT):
                j8 = junk.rearrange("p (h n) -> p h n", h=8)
                mul(j8, oacc[:, t], oacc[:, t])
                L.did(V.tensor_reduce(ss[:, t * 8:t * 8 + 8], j8, AXX, ALU.add))
            inv_root(ss[:, 0:32], HD)
            for t in range(NT):
                mul(oacc[:, t], oacc[:, t], spread(ss[:, t * 8:t * 8 + 8]), s["on_ready"])
            for t in range(NT):
                for h0 in (0, 4):
                    b = full()
                    scale(onT[:, h0:h0 + 4, t * P:(t + 1) * P], by4(b), cols[:, V_DN:V_DN + 1], s["free_v"])
            for j in range(KC):
                mul(onT[:, j, :], onT[:, j, :], tmp_of(tmpB), s["dz_ready"], [s["tmp_used"]])
            for j in range(KC):
                tmp = tmp_of(tmpB)
                b = full()
                mul(tmp, b, tmp, s["free_v"])
                add(mixT[:, j, :], mixT[:, j, :], tmp, s["mixT_ready"], [s["tmp_used"]])

            def normed(v, row, x, sig, also=()):
                for t in range(NT):
                    squares(v[:, t, :], ss[:, t:t + 1], junk)
                inv_root(ss[:, 0:NT], DM)
                for t in range(NT):
                    L.did(V.scalar_tensor_tensor(v[:, t, :], v[:, t, :], ss[:, t:t + 1], row, ALU.mult, ALU.mult))
                    add(x[:, t, :], x[:, t, :], v[:, t, :], *sig)

            for t in range(NT):
                b = full()
                L.did(V.tensor_copy(pinT[:, :, t * P:(t + 1) * P], b[:, 0:256].rearrange("p (c n) -> p c n", c=2)),
                      s["pinT_ready"], [s["free_v"]])
            L.need(s["mo_ready"], 16)
            dve.wait_ge(s["ld_rows"], 32)
            dve.wait_ge(s["ld_res"], 64)
            normed(mo, rowv, x1, [s["x1_ready"]])
            for t in range(NT):
                for c0 in (0, 4):
                    b = full()
                    L.did(V.tensor_copy(x1T[:, c0:c0 + 4, t * P:(t + 1) * P], by4(b)), s["x1T_ready"],
                          [s["free_v"]])
            L.need(s["sg_ready"], 16)
            for t in range(NT):
                for c0 in (0, 512):
                    b = full()
                    mul(mo[:, t, c0:c0 + 512], b, sg[:, t, c0:c0 + 512], s["free_v"])
            normed(mo, rowv2, x1, [])
            L.need(s["mod_ready"], 24)
            add(mod[:, :, :], mod[:, :, :], cols[:, V_BADA:V_BADA + 48].unsqueeze(2).broadcast_to([P, 48, 2]))
            for n, (c0, k, vn) in enumerate(((8, 0, V_N1), (8, 1, V_N1), (32, 0, V_N2))):
                L.did(V.scalar_tensor_tensor(gain[:, n * 8:n * 8 + 8], mod[:, c0:c0 + 8, k], 1.0,
                                             cols[:, vn:vn + 8], ALU.add, ALU.mult))
            phase(4)

            for t in range(NT):
                squares(x1[:, t, :], ss[:, t:t + 1], jc)
            inv_root(ss[:, 0:NT], DM)
            for t in range(NT):
                scale(xn[:, t, :], x1[:, t, :], ss[:, t:t + 1], s["x2_ready"])
            for t in range(NT):
                turned(h2T, t, gain[:, 0:8], mod[:, 0:8, 0], "h2_ready")
            dve.wait_ge(s["ld_ctx"], 32)
            for t in range(NTC):
                squares(ctxt[:, t, :], ss[:, t:t + 1], jc)
            inv_root(ss[:, 0:NTC], DM)
            for t in range(NTC):
                scale(ctxt[:, t, :], ctxt[:, t, :], ss[:, t:t + 1], s["x2_ready"])
            for t in range(NTC):
                turned(hcT, t, gain[:, 8:16], mod[:, 0:8, 1], "hc_ready")
            for b2 in range(2):
                for t in range(NT + NTC):
                    b = full()
                    L.did(V.tensor_copy(v2[:, t, b2 * 256:(b2 + 1) * 256], b[:, 0:256]), s["free_v"])
            for d in range(2):
                for c0, n in ((0, SEQ), (SEQ, CTX)):
                    b = full()
                    L.did(V.tensor_copy(a2T[0:RANK, d, c0:c0 + n], b[0:RANK, 0:n]), s["a2_ready"], [s["free_v"]])
            for b2 in range(2):
                for t in range(NT):
                    b = full()
                    L.did(V.tensor_copy(p2[:, t, b2 * 256:(b2 + 1) * 256], b[:, 0:256]), s["p2_ready"],
                          [s["free_v"]])
            for g in range(4):
                b = full()
                if g >= 2:
                    dve.wait_ge(s["cat_ready"], g - 1)
                L.did(V.tensor_copy(pmT[:, g % 2, :], b), s["mT_ready"], [s["free_v"]])
            phase(5)

            for t in range(NT + NTC):
                L.need(s["z_ready"])
                z, y = z2[:, t % 2, :], z3[:, t % 2, :]
                L.did(V.scalar_tensor_tensor(y, z, -1.0, z, ALU.mult, ALU.max), s["absz_ready"])
                L.need(s["lz_ready"])
                L.did(V.scalar_tensor_tensor(z, z, 0.0, y, ALU.min, ALU.subtract))
                scale(la[:, t, :], z, 1.0 / 16.0, s["la_ready"])
            for n in range(4):
                d, m2 = divmod(n, 2)
                L.need(s["bexp_ready"], 2)
                mul(qb[:, d, m2, :], q2T[:, m2, :], eb[:, n % 2, :])
                mul(kb[:, d, m2, :], k2T[:, m2, :], enb[:, n % 2, :], s["qb_ready"])
            for t in range(NT + NTC):
                L.need(s["kexp_ready"])
                kv = kst[:, t, :].rearrange("p (d n) -> p d n", d=2)
                mul(kv, kv, k2[:, t, :].unsqueeze(1).broadcast_to([P, 2, 256]), s["kst_ready"])
            L.did(V.memset(swork[:, 0, :, :, :], 0.0))
            for n in range(12):
                for d in range(2):
                    b = full()
                    c = chunk_col(d, n)
                    for m2 in range(2):
                        src = state_at(d, m2, n)
                        dst = state_at(d, m2, n + 1)
                        if dst is None:
                            continue
                        for hh in range(2):
                            hp = slice(hh * 64, hh * 64 + 64)
                            L.did(V.scalar_tensor_tensor(dst[hp, :], src[hp, :], dec2[hp, d, m2, c:c + 1],
                                                         b[hp, m2 * 256 + hh * P:m2 * 256 + (hh + 1) * P],
                                                         ALU.mult, ALU.add))
                    L.raise_(s["free_v"])
            L.raise_(s["sprev_ready"])
            for h in range(H2):
                for d in range(2):
                    b = full()
                    mul(by4(scm[:, (h % 2) * 2 + d, :]), by4(b), over(blk[d], 4), s["sc_ready"], [s["free_v"]])
                L.need(s["rt2_ready"], 2)
                r = enb[:, h % 2, :]
                L.did(V.reciprocal(r, r))
                mul(r, r, catT[:, h, :])
                L.did(V.scalar_tensor_tensor(catT[:, h, :], r, cols[:, V_GLA:V_GLA + 1], g2T[:, h, :],
                                             ALU.mult, ALU.mult), s["o2_ready"], [s["cat_ready"]])
            for c0 in (0, 512):
                b = full()
                L.did(V.tensor_copy(gtrow[:, c0:c0 + 512], b), s["free_v"])
            tmp = scm[:, 0, 0:WC]
            for b2 in range(4):
                cs = slice(b2 * WC, (b2 + 1) * WC)
                for t in range(NT):
                    b = full()
                    mul(tmp, b[:, 0:WC], gtrow[:, cs], s["free_v"])
                    add(x1[:, t, cs], x1[:, t, cs], tmp)
            phase(6)

            for t in range(NT):
                squares(x3[:, t, :], ss[:, t:t + 1], jr)
            inv_root(ss[:, 0:NT], DM)
            for t in range(NT):
                scale(xn[:, t, :], x3[:, t, :], ss[:, t:t + 1], s["x3_ready"])
            for t in range(NT):
                turned(h3T, t, gain[:, 16:24], mod[:, 24:32, 0], "h3_ready")
            iota = const[:, C_IOTA:C_IOTA + NE]
            R = [rtr[:, k, :] for k in range(10)]
            L.did(V.memset(R[0][:, 0:8], -1e30))
            for t in range(NT):
                b = full()
                L.did(V.tensor_copy(lg, b[:, 0:36]), s["free_v"])
                L.did(V.tensor_copy(R[0][:, 0:4], lg[:, 0:4]))
                L.did(V.max(R[1][:, 0:8], R[0][:, 0:8]))
                scale(R[8][:, 0:1], R[1][:, 0:1], -1.0, s["lg_ready"])
                L.did(V.max_index(R[2][:, 0:8].bitcast(U32), R[1][:, 0:8], R[0][:, 0:8]))
                L.did(V.tensor_copy(R[3][:, 0:1], R[2][:, 0:1].bitcast(U32)))
                scale(R[3][:, 0:1], R[3][:, 0:1], float(EPG))
                L.did(V.tensor_scalar(R[4], iota, R[3][:, 0:1], 0.0, ALU.subtract, ALU.is_ge))
                L.did(V.tensor_scalar(R[5], iota, R[3][:, 0:1], float(EPG), ALU.subtract, ALU.is_lt))
                mul(R[4], R[4], R[5])
                L.did(V.tensor_scalar(R[4], R[4], 1.0, 1e30, ALU.subtract, ALU.mult))
                add(R[4], R[4], lg[:, 4:36])
                L.did(V.max(R[1][:, 8:16], R[4]))
                L.did(V.max_index(R[2][:, 8:16].bitcast(U32), R[1][:, 8:16], R[4]))
                L.did(V.tensor_copy(R[3][:, 8:16], R[2][:, 8:16].bitcast(U32)))
                L.need(s["lexp_ready"])
                L.did(V.tensor_tensor(R[8][:, 2:3], R[1][:, 9:10], R[1][:, 8:9], ALU.subtract), s["lg_ready"])
                L.need(s["lexp_ready"])
                L.did(V.tensor_scalar(R[8][:, 3:4], R[8][:, 2:3], 1.0, None, ALU.add))
                mul(R[8][:, 3:4], R[8][:, 3:4], R[8][:, 1:2])
                L.did(V.reciprocal(R[8][:, 4:5], R[8][:, 3:4]))
                mul(R[8][:, 5:6], R[8][:, 4:5], R[8][:, 2:3])
                for k in range(2):
                    L.did(V.tensor_copy(ewt[:, t, k:k + 1], R[8][:, 4 + k:5 + k]))
                    L.did(V.tensor_copy(eid[:, t, k:k + 1], R[3][:, 8 + k:9 + k]))
                    L.did(V.tensor_scalar(pick[:, t, k, :], iota, R[3][:, 8 + k:9 + k], None, ALU.is_equal))
                add(picked[:, t, :], pick[:, t, 0, :], pick[:, t, 1, :])
                L.raise_(s["picked_ready"])
            for c0 in (0, 512):
                b = full()
                L.did(V.tensor_copy(rowg[:, c0:c0 + 512], b), s["free_v"])
            for t in range(NT):
                b = full()
                L.did(V.tensor_copy(place[:, t, :], b[:, 0:NE]), s["free_v"])
                for k in range(2):
                    u = tmax[:, 0:1]
                    mul(R[5], pick[:, t, k, :], place[:, t, :])
                    L.did(V.tensor_reduce(u, R[5], AXX, ALU.add))
                    L.did(V.tensor_scalar(R[6][:, 0:ROUNDS - 1], iota[:, 1:ROUNDS], float(CAP), u, ALU.mult, ALU.is_le))
                    L.did(V.tensor_reduce(tmax[:, 1:2], R[6][:, 0:ROUNDS - 1], AXX, ALU.add))
                    L.did(V.tensor_copy(tround[:, t, k:k + 1], tmax[:, 1:2]))
                    L.did(V.scalar_tensor_tensor(u, tmax[:, 1:2], float((NE - 1) * CAP), u, ALU.mult, ALU.add))
                    L.did(V.scalar_tensor_tensor(slot_f[:, t, k:k + 1], eid[:, t, k:k + 1], float(CAP), u,
                                                 ALU.mult, ALU.add))
            b = full()
            L.did(V.tensor_reduce(tmax[:, 2:3], b[:, 0:NE], AXX, ALU.max), s["free_v"])
            L.did(V.tensor_scalar(tmax[:, 8:8 + ROUNDS], iota[:, 0:ROUNDS], float(CAP), tmax[:, 2:3], ALU.mult, ALU.is_lt))
            L.did(V.tensor_reduce(tmax[:, 3:4], tmax[:, 8:8 + ROUNDS], AXX, ALU.add))
            L.did(V.tensor_copy(turns_u[:, 0:1], tmax[:, 3:4]), s["turns_ready"])
            L.did(V.memset(zero, 0.0))
            rnd, slf = tround.rearrange("p t k -> p (t k)"), slot_f.rearrange("p t k -> p (t k)")
            for r in range(ROUNDS):
                o = back_f[:, r, :]
                L.did(V.tensor_scalar(o, slf, float(-NE * CAP * (r + 1)), None, ALU.add))
                L.did(V.scalar_tensor_tensor(o, rnd, float(r), o, ALU.is_equal, ALU.mult))
                L.did(V.tensor_scalar(o, o, float(NE * CAP), None, ALU.add))
            L.did(V.tensor_copy(back_u, back_f))
            dve.wait_ge(s["xn_saved"], 16 * NT)
            L.did(V.memset(yacc, 0.0))
            L.did(V.memset(index[:, ROUNDS * NE:], 0))
            L.did(V.tensor_copy(slot_u, slot_f.rearrange("p t k -> p (t k)")), s["slots_ready"])
            b = full()
            L.did(V.tensor_copy(index[0:CAP, 0:ROUNDS * NE], b[0:CAP, 0:ROUNDS * NE]), s["index_ready"],
                  [s["free_v"]])

            def to_xe(b, k):
                o = xe[:, k, :, :]
                L.did(V.tensor_tensor(o, b.rearrange("p (c n) -> p c n", c=KC), spread(gain[:, 16:24], CAP),
                                      ALU.mult), s["free_v"])
                add(o, o, spread(mod[:, 24:32, 0], CAP), s["xe_ready"])

            to_xe(full(), 0)
            L.raise_(s["sil_used"], 2)
            q0 = seen[0]
            rounds = rounds_of(dve)
            dve.sem_inc(s["combined"])
            with dve.Fori(0, rounds) as r:
                with dve.Fori(0, NE // XPT) as ir:
                    i = r * (NE // XPT) + ir
                    L.enter(i, {s["hid_ready"]: XPT, s["free_v"]: 3 * XPT, s["sil_used"]: XPT, s["xe_ready"]: XPT,
                                s["y1_ready"]: XPT},
                            {s["full_v"]: 3 * XPT, s["sil_ready"]: XPT})
                    for q in range(XPT):
                        k = q % 2
                        L.need(s["sil_ready"])
                        L.need(s["full_v"])
                        L.did(V.tensor_tensor(hid[:, k, :], psv[:, (q0 + 3 * q) % 4, 0:2 * CAP], sil[:, k, :], ALU.mult),
                              s["hid_ready"], [s["free_v"], s["sil_used"]])
                        L.need(s["full_v"])
                        to_xe(psv[:, (q0 + 3 * q + 1) % 4, :], 1 - k)
                        L.need(s["full_v"])
                        dve.wait_ge(s[f"st_y{k}"], (i * (XPT // 2) + (q // 2 + 1)) * 16)
                        L.did(V.tensor_copy(yb[0:CAP, k, 512:DM], psv[0:CAP, (q0 + 3 * q + 2) % 4, :]), s["y1_ready"],
                              [s["free_v"]])
                    L.leave(0)
                dve.wait_ge(s["ygat_ready"], r * (32 * NT) + 32 * NT)
                for t in range(NT):
                    for k in range(2):
                        ins = V.scalar_tensor_tensor(yacc[:, t, :], ygat[:, k, t, :], ewt[:, t, k:k + 1],
                                                     yacc[:, t, :], ALU.mult, ALU.add)
                        ins.then_inc(s["yacc_ready"], 1)
                        dve.wait_ge(s["yacc_ready"], r * (2 * NT) + (2 * t + k + 1))
                dve.sem_inc(s["combined"])
            for t in range(NT):
                mul(yacc[:, t, :], yacc[:, t, :], rowg)
                add(x3[:, t, :], x3[:, t, :], yacc[:, t, :])
                squares(x3[:, t, :], ss[:, t:t + 1], jr)
            inv_root(ss[:, 0:NT], DM)
            dve.wait_ge(s["ld_rowf"], 16)
            for t in range(NT):
                L.did(V.scalar_tensor_tensor(x3[:, t, :], x3[:, t, :], ss[:, t:t + 1], rowf, ALU.mult, ALU.mult),
                      s["out_ready"])


_OUT = (1, SEQ, DM)
DUMP = []


def kernel(**inputs):
    import concourse.bacc as bacc
    from concourse.bass_utils import run_bass_kernel_spmd

    nc = bacc.Bacc("TRN2", target_bir_lowering=False, num_devices=1)
    masks, rope, pool = shape_constants()
    arrays = {n: np.ascontiguousarray(v) for n, v in inputs.items()}
    arrays |= {"c_masks": masks, "c_rope": rope, "c_pool": pool}
    a = {n: nc.dram_tensor(n, v.shape, F32, kind="ExternalInput").ap() for n, v in arrays.items()}
    out = nc.dram_tensor("out", _OUT, F32, kind="ExternalOutput").ap()
    build(nc, a, out, [])
    r = run_bass_kernel_spmd(nc, [arrays], core_ids=[0])
    return r.results[0]["out"]
```

```python
from contextlib import ExitStack

import numpy as np

import concourse.bass as bass
from concourse import mybir

F32 = mybir.dt.float32
U32 = mybir.dt.uint32
ALU = mybir.AluOpType
ACT = mybir.ActivationFunctionType
AXX = mybir.AxisListType.X

P = 128
SEQ, DM = 512, 1024
NT = SEQ // P
KC = DM // P
EPS = 1e-6
HD = 128
NH, NKV = 8, 2
GRID_W = 64
ROPE_THETA = 10000.0
CONV_K = 5
PLE = 256
CTX = 256
NTC = CTX // P
CH2 = 64
H2, DK2, DV2 = 4, 64, 128
RANK = 16
WINDOWS = (2, 4, 8, 16)
NE, NG, EPG, DE = 32, 4, 8, 256
CAP = 64
ROUNDS = SEQ // CAP
SLOTS = ROUNDS * NE * CAP
XPT = 4
O_AQ, O_AK, O_AV, O_AZ = 0, 1024, 1280, 1536
O_DQ, O_DB, O_DZ, O_GA, O_GD = 2560, 5632, 5664, 6688, 7712
O2_Q, O2_K, O2_V, O2_G, O2_A, O2_P = 0, 256, 512, 1024, 1536, 1568
WC = 256
LEVELS = 7

C_ID, C_ONE, C_LE, C_GE = 0, 128, 256, 384
C_LV = 512
C_BLE = C_LV + 2 * LEVELS * P
C_BGE, C_BGT, C_BLT = C_BLE + P, C_BLE + 2 * P, C_BLE + 3 * P
C_EPS = C_BLE + 4 * P
C_IOTA = C_EPS + 4
C_TOK = C_IOTA + 32
C_LT = C_TOK + NT
C_REV = C_LT + P
C_N = C_REV + EPG
V_PRE, V_DN, V_N1, V_N2, V_GLA, V_PS, V_BADA, V_C, V_CC = 0, 8, 9, 17, 25, 26, 30, 78, 86
V_N = 94


def shape_constants():
    i = np.arange(P)
    p, f = i[:, None], i[None, :]
    c = np.zeros((P, C_N), np.float32)
    c[:, C_ID:C_ID + P] = p == f
    c[:, C_ONE:C_ONE + P] = 1.0
    c[:, C_LE:C_LE + P] = p <= f
    c[:, C_GE:C_GE + P] = p >= f
    for k in range(LEVELS):
        b = 1 << k
        off = (p // (2 * b) == f // (2 * b)) & (p // b != f // b)
        c[:, C_LV + k * P:C_LV + (k + 1) * P] = off & (p > f)
        c[:, C_LV + (LEVELS + k) * P:C_LV + (LEVELS + k + 1) * P] = off & (p < f)
    same = p // CH2 == f // CH2
    c[:, C_BLE:C_BLE + P] = same & (p <= f)
    c[:, C_BGE:C_BGE + P] = same & (p >= f)
    c[:, C_BGT:C_BGT + P] = same & (p > f)
    c[:, C_BLT:C_BLT + P] = same & (p < f)
    c[:, C_EPS] = EPS
    c[:, C_EPS + 1] = HD * EPS
    c[:, C_EPS + 2] = 1.0
    c[:, C_IOTA:C_IOTA + 32] = np.arange(32)
    c[:, C_TOK:C_TOK + NT] = p + P * np.arange(NT)
    c[:, C_LT:C_LT + P] = p < f
    c[:, C_REV:C_REV + EPG] = EPG - np.arange(EPG)
    nf = HD // 4
    inv = (np.float32(ROPE_THETA) ** (-np.arange(nf, dtype=np.float32) / np.float32(nf))).astype(np.float32)
    t = np.arange(SEQ)
    ang = np.concatenate([(t // GRID_W).astype(np.float32)[:, None] * inv,
                          (t % GRID_W).astype(np.float32)[:, None] * inv], axis=1)
    rope = np.stack([np.cos(ang), np.sin(ang)], axis=1).astype(np.float32)
    rope = np.ascontiguousarray(rope.reshape(NT, P, 2, HD // 2).transpose(1, 0, 2, 3))

    def mean(n, w):
        m = np.zeros((n, n))
        lo = w // 2
        hi = w - 1 - lo
        for a in range(n):
            s, e = max(0, a - lo), min(n, a + hi + 1)
            m[a, s:e] = 1.0 / (e - s)
        return m

    pool = np.zeros((len(WINDOWS), SEQ, SEQ))
    for g, w in enumerate(WINDOWS):
        pool[g] = (np.kron(mean(SEQ // GRID_W, w), mean(GRID_W, w)) - np.eye(SEQ)).T
    pool = pool.astype(np.float32).reshape(len(WINDOWS), NT, P, SEQ).transpose(2, 0, 1, 3)
    return c, rope, np.ascontiguousarray(pool)


class Lane:

    def __init__(self, eng, chain):
        self.eng, self.chain = eng, chain
        self.raised, self.followed = {}, {}
        self.i, self.per, self.at = None, {}, None

    def value(self, table, sem):
        n = table[sem]
        if self.i is None or not self.per.get((id(table), sem), 0):
            return n
        return self.i * self.per[(id(table), sem)] + n

    def did(self, ins, sem=None, also=()):
        sem = self.chain if sem is None else sem
        ins.then_inc(sem, 1)
        self.raised[sem] = self.raised.get(sem, 0) + 1
        self.eng.wait_ge(sem, self.value(self.raised, sem))
        for s in also:
            self.raise_(s)

    def raise_(self, sem, n=1):
        self.raised[sem] = self.raised.get(sem, 0) + n
        self.eng.sem_inc(sem, n)

    def need(self, sem, n=1):
        self.followed[sem] = self.followed.get(sem, 0) + n
        self.eng.wait_ge(sem, self.value(self.followed, sem))

    def enter(self, i, raised, followed):
        self.i = i
        self.per = {}
        for s, n in raised.items():
            self.raised.setdefault(s, 0)
            self.per[(id(self.raised), s)] = n
        for s, n in followed.items():
            self.followed.setdefault(s, 0)
            self.per[(id(self.followed), s)] = n
        self.at = (dict(self.raised), dict(self.followed))

    def leave(self, turns):
        for table, before in ((self.raised, self.at[0]), (self.followed, self.at[1])):
            for s in table:
                per = self.per.get((id(table), s), 0)
                assert table[s] - before.get(s, 0) == per, (s, table[s] - before.get(s, 0), per)
                table[s] = before.get(s, 0) + turns * per
        self.i, self.per = None, {}


def build(nc, a, out, dumps):
    ctx = ExitStack()
    with ctx:
        def sb(name, *shape):
            return ctx.enter_context(nc.sbuf_tensor(name, [P, *shape], F32))

        def sem(name):
            return ctx.enter_context(nc.semaphore(name))

        const = sb("const", C_N)
        ident = const[:, C_ID:C_ID + P]
        ones = const[:, C_ONE:C_ONE + P]
        tri = [const[:, C_LE:C_LE + P], const[:, C_GE:C_GE + P]]
        blk = [const[:, C_BLE:C_BLE + P], const[:, C_BGE:C_BGE + P]]
        blk_rest = [const[:, C_BGT:C_BGT + P], const[:, C_BLT:C_BLT + P]]
        eps = const[:, C_EPS:C_EPS + 1]
        eps128 = const[:, C_EPS + 1:C_EPS + 2]
        one = const[:, C_EPS + 2:C_EPS + 3]
        wslot01 = sb("wslot01", 2, KC * WC)
        cols = sb("cols", V_N)
        ccols = sb("ccols", CONV_K * 24)
        csilu = sb("csilu", KC, 2)
        mod = sb("mod", 48, 2)
        small = sb("small", 3 * 64)
        ss = small[:, 0:64]
        gb = sb("gb", NT, 32)
        gain = sb("gain", 3 * KC)
        gpar = sb("gpar", 3, 16)
        kcol = sb("kcol", 2, 2, 4)

        ARENA = 44100
        arena = sb("arena", ARENA)
        top = [0]

        def at(off, *shape):
            n = int(np.prod(shape))
            assert off + n <= ARENA, (off, n)
            top[0] = off + n
            v = arena[:, off:off + n]
            if len(shape) == 1:
                return v
            names = "abcde"[:len(shape)]
            return v.rearrange(f"p ({' '.join(names)}) -> p {' '.join(names)}",
                               **{k: s for k, s in zip(names[1:], shape[1:])})

        K = 256
        hT = at(0, KC, SEQ)
        mixT = at(16 * K, KC, SEQ)
        B = 32 * K
        xt = at(B, NT, DM)
        oT = at(B, KC, SEQ)
        atok = at(B + 16 * K, NT, 1536)
        qkT = at(B + 40 * K, 10, SEQ)
        rt = at(B + 60 * K, 2, 10, HD // 2)
        rope = at(top[0], NT, 2, HD // 2)
        azs = at(B + 106 * K, KC, SEQ)
        assert top[0] <= ARENA - 2 * KC * WC
        qkn = at(B + 67 * K, 2, HD)
        pb = at(top[0], 3, SEQ)
        pT = at(top[0], 2, NT, SEQ)
        tmpA = at(top[0], 2, SEQ)
        vecs = at(top[0], P)
        cvecs = at(top[0], P)
        sqA = at(top[0], 10, HD)
        jA = at(top[0], DM)
        assert top[0] <= B + 106 * K, top[0] / K
        qT = at(B, NH, SEQ)
        kT = at(B + 16 * K, NH, SEQ)
        ktok = at(B + 32 * K, NT, NH, HD)
        vtok = at(B + 48 * K, NT, NH, HD)
        oacc = at(B + 64 * K, NT, NH, HD)
        state = at(B + 80 * K, 2, NH, HD)
        gbuf = at(top[0], 8, NT, 16)
        D = top[0]
        conv = at(D, 2, SEQ)
        cst = at(top[0], 2, SEQ)
        crt = at(top[0], 2, SEQ)
        csq = at(top[0], 2, SEQ)
        assert top[0] <= ARENA - 2 * KC * WC
        NB = 12
        grp = [[at(D + (d * NB + n) * 512, 4, P) for n in range(NB)] for d in range(2)]
        glast = at(D + 2 * NB * 512, 2, 2, 4)
        onT = at(B, KC, SEQ)
        mo = at(B + 16 * K, NT, DM)
        x1 = at(B + 32 * K, NT, DM)
        x1T = at(0, KC, SEQ)
        pin = at(B + 48 * K, NT, PLE)
        pinT = at(top[0], 2, SEQ)
        sg = at(B + 64 * K, NT, DM)
        rowv = at(B + 80 * K, DM)
        rowv2 = at(top[0], DM)
        tmpB = at(top[0], 2, SEQ)
        junk = at(top[0], DM)
        xn = at(B + 16 * K, NT, DM)
        h2T = at(0, KC, SEQ)
        hcT = at(16 * K, KC, CTX)
        ctxt = at(24 * K, NTC, DM)
        q2T = at(B, 2, SEQ)
        k2T = at(B + 4 * K, 2, SEQ)
        g2T = at(B + 8 * K, H2, SEQ)
        catT = at(B + 16 * K, KC, SEQ)
        k2 = at(B + 48 * K, NT + NTC, 256)
        v2 = at(top[0], NT + NTC, 512)
        p2 = at(top[0], NT, 512)
        a2T = at(top[0], 2, SEQ + CTX)
        wdec = at(top[0], 2, 256)
        bdec = at(top[0], 512)
        wpool = at(top[0], len(WINDOWS), P)
        gtrow = at(top[0], DM)
        la = at(top[0], NT + NTC, 512)
        G = top[0]
        pm = at(G, 2, NT, SEQ)
        pmT = at(top[0], 2, SEQ)
        jc = at(top[0], DM)
        z2 = at(G, 2, 512)
        z3 = at(top[0], 2, 512)
        kst = at(top[0], NT + NTC, 512)
        eb = at(top[0], 2, SEQ)
        enb = at(top[0], 2, SEQ)
        dec2 = at(top[0], 2, 2, 12)
        swork = at(top[0], 2, 2, 2, P)
        qb = at(0, 2, 2, SEQ)
        kb = at(8 * K, 2, 2, SEQ)
        sprev = at(16 * K, 2, 2, 8, P)
        scm = at(G, 4, SEQ)
        x3 = x1
        yacc = xn
        h3T = h2T
        rowf = at(B, DM)
        rowg = at(B + 4 * K, DM)
        wrt = at(B + 8 * K, KC, 36)
        xg = at(16 * K, 2, DM)
        lg = at(16 * K, NT, 4 + NE)
        rgrp = at(top[0], 3, NT, NG)
        rexp = at(top[0], NT, NE)
        rin = at(top[0], NT, EPG)
        rhot = at(top[0], 2, NT, EPG)
        rtmp = at(top[0], NT, EPG)
        rcol = at(top[0], 8, NT)
        rplace = at(top[0], NT, 2, NE)
        rthr = at(top[0], ROUNDS - 1)
        rpast = at(top[0], 2 * NT, ROUNDS - 1)
        assert top[0] <= 24 * K
        xe = at(24 * K, 2, KC, CAP)
        sil = at(28 * K, 2, 2 * CAP)
        hid = at(29 * K, 2, 2 * CAP)
        yb = at(0, 2, DM)
        win = at(B + 48 * K, 2, KC, 2 * DE)
        wout = at(top[0], 2, 2, DM)
        lexp = at(top[0], NT, NG + 1)
        jr = at(top[0], DM)
        pick = at(top[0], NT, 2, NE)
        picked = at(top[0], NT, NE)
        ewt = at(top[0], NT, 2)
        eid = at(top[0], NT, 2)
        slot_f = at(top[0], NT, 2)
        slot_u = at(top[0], 2 * NT).bitcast(U32)
        tmax = at(top[0], 16)
        turns_u = at(top[0], 2).bitcast(U32)
        table = at(top[0], 2, CAP)
        index = at(top[0], ROUNDS * NE + 4).bitcast(U32)
        icol = at(top[0], 2).bitcast(U32)
        zero = at(top[0], P)
        ygat = at(top[0], 2, NT, DM)
        back_f = at(top[0], ROUNDS, 2 * NT)
        back_u = at(top[0], ROUNDS, 2 * NT).bitcast(U32)
        bcol = at(top[0], 2 * NT).bitcast(U32)
        tround = at(top[0], NT, 2)

        def scratch(name, *shape):
            return nc.dram_tensor(name, list(shape), F32, kind="Internal").ap()

        xn_dram = scratch("xn_dram", SEQ, DM)
        table_dram = scratch("table_dram", SLOTS, 1)
        y_dram = scratch("y_dram", NE * CAP + 1, DM)
        y_store = y_dram[0:NE * CAP, :].rearrange("(i q c) n -> i q c n", q=XPT, c=CAP)

        psv = ctx.enter_context(nc.psum_tensor("psv", [P, 4, 512], F32))
        pss = ctx.enter_context(nc.psum_tensor("pss", [P, 4, 512], F32))

        names = """chain_v chain_s chain_p phase full_v free_v full_s free_s w_used ld_const ld_vecs ld_x ld_rope
            ld_qkn ld_gpar ld_res ld_p ld_rows ld_ctx ld_small ld_rowf ld_wrt cols_ready az_ready silu_z xn_ready hT_ready
            rs_in rs_out atok_ready rope_ready qkT_ready negmax_ready probs_ready probsn_ready pT_ready
            oT_ready tmp_ready tmp_used oz_ready ga_ready ga_step gg_ready gG_ready conv_ready silu_ready
            vtok_ready sq_ready rt_ready norm_ready ktok_ready on_ready dz_ready mixT_ready mo_ready
            x1_ready x1T_ready pinT_ready sg_ready x2_ready mod_ready h2_ready hc_ready p2_ready mT_ready
            k2_ready a2_ready z_ready absz_ready lz_ready la_ready bexp_ready qb_ready kexp_ready kst_ready
            sprev_ready sc_ready o2_ready sq2_ready rt2_ready cat_ready x3_ready h3_ready lg_ready
            lexp_ready ld_out moe_used sil_ready hid_ready out_ready picked_ready icol_ready bcol_ready combined yacc_ready xn_saved table_zeroed
            slots_ready scattered table_loaded index_ready xg_k0 xg_k1 xe_ready y1_ready st_y0 st_y1
            ygat_ready turns_ready sil_used pool_used""".split()
        s = {n: sem(n) for n in names}
        for n in ("e_ready glast_ready x_ready d1_ready d2_ready l_ready at_pre at_ready "
                  "c_ready t_ready tt_ready zz_ready kbe_ready kdec_ready qg_ready nwt_ready vn_ready "
                  "group_done").split():
            for d in range(2):
                s[n, d] = sem(f"{n}{d}")
        for k in range(4):
            s["ld_w", k] = sem(f"ld_w{k}")
        for k in range(2):
            s["ld_win", k] = sem(f"ld_win{k}")
            s["ld_wout", k] = sem(f"ld_wout{k}")
            s["ld_pm", k] = sem(f"ld_pm{k}")

        w1, w2 = a["w_in"][0], a["w_in_2"][0]
        weights, slot_group = [], []

        def stream(key, src, col, n):
            weights.append((key, src[:, col:col + n].rearrange("(c p) n -> p c n", p=P), src.shape[0] // P, n))

        for b in range(6):
            stream(("qkv", b), w1, O_AQ + b * WC, WC)
        stream("dbda", w1, O_DB, 32)
        for b in range(4):
            stream(("az", b), w1, O_AZ + b * WC, WC)
        for b in range(4):
            stream(("bra", b), a["w_br_att"][0], b * WC, WC)
            stream(("ga", b), w1, O_GA + b * WC, WC)
        slot_group.append((len(weights), 4))
        for b in range(12):
            stream(("dqkv", b), w1, O_DQ + b * WC, WC)
        for b in range(24):
            stream(("ada", b), a["w_ada_2"][0], b * WC, WC)
        slot_group.append((len(weights), 2))
        for b in range(4):
            stream(("dz", b), w1, O_DZ + b * WC, WC)
        for b in range(4):
            stream(("brd", b), a["w_br_dn"][0], b * WC, WC)
            stream(("gd", b), w1, O_GD + b * WC, WC)
        for b in range(4):
            stream(("wo", b), a["w_out"][0], b * WC, WC)
        for b in range(4):
            stream(("pleg", b), a["w_ple_gate"][0], b * WC, WC)
        stream("plep", a["w_ple_proj"][0], 0, DM)
        slot_group.append((len(weights), 4))
        for key, col, n in (("q2", O2_Q, 256), ("k2", O2_K, 256), (("v2", 0), O2_V, 256), (("v2", 1), O2_V + 256, 256),
                            (("g2", 0), O2_G, 256), (("g2", 1), O2_G + 256, 256), ("a2", O2_A, 32),
                            (("p2", 0), O2_P, 256), (("p2", 1), O2_P + 256, 256)):
            stream(key, w2, col, n)
        for b in range(4):
            stream(("wo2", b), a["w_out_2"][0], b * WC, WC)

        slot_group.append((len(weights), 2))
        slot_of, before, turn_of, last = [], [], [], {}
        for end, many in slot_group:
            start = len(slot_of)
            for n in range(start, end):
                k = (n - start) % many
                slot_of.append(k)
                before.append(last.get(k, (-1, 0))[0])
                turn_of.append(last.get(k, (-1, 0))[1] + 1)
                last[k] = (n, turn_of[-1])
        wslot = [wslot01[:, 0, :], wslot01[:, 1, :], arena[:, ARENA - 2 * KC * WC:ARENA - KC * WC],
                 arena[:, ARENA - KC * WC:ARENA]]

        def slot_view(n):
            _, _, kc, m = weights[n]
            return wslot[slot_of[n]][:, 0:kc * m].rearrange("p (c n) -> p c n", c=kc)

        win_src = a["w_expert_in_2"][0].rearrange("(i k) (c p) n -> i k p c n", k=2, p=P)
        wout_src = a["w_expert_out_2"][0].rearrange("(i k) (c p) n -> i k p c n", k=2, p=P)

        win_next, wout_next = win_src[1:NE // 2], wout_src[1:NE // 2]

        def rounds_of(eng):
            eng.wait_ge(s["turns_ready"], 1)
            return eng.value_load(turns_u[0:1, 0:1], min_val=1, max_val=ROUNDS)
        steps = []
        for i in range(NH * NT + 2):
            if i < NH * NT:
                steps.append(("scores", i))
            if i >= 2:
                steps.append(("turn", i - 2))
                if (i - 2) % NT == NT - 1:
                    steps.append(("head", (i - 2) // NT))
            if i in (5, 12, 19, 26):
                steps.append(("gate", 4 + (i - 5) // 7))
        S_ATT = 2 + 4 + 24 + 12 + 4
        score_job = {i: S_ATT + n for n, (what, i) in enumerate(steps) if what == "scores"}
        SUM_LAG, TURN_LAG = 4, 6
        PAIRS = [(st, hg) for st in range(NT) for hg in range(2)]
        C_X, C_D1, C_E, C_C0, C_C1, C_T, C_TT, C_Z, C_VB, C_KBE, C_KDEC, C_VN = range(12)

        role = [list(range(NB))]
        for n in range(1, len(PAIRS)):
            q = role[-1]
            nxt = list(q)
            nxt[C_X], nxt[C_D1], nxt[C_E] = q[C_D1], q[C_C0], q[C_C1]
            nxt[C_C0], nxt[C_C1], nxt[C_T] = q[C_T], q[C_X], q[C_E]
            role.append(nxt)

        def buffers(n, d):
            return [grp[d][m] for m in role[n]]

        def tile_of(d, st):
            return st if d == 0 else NT - 1 - st

        def hcols(d, hg):
            return slice(d * 8 + hg * 4, d * 8 + hg * 4 + 4)

        def spread(v, n=P):
            return v.unsqueeze(2).broadcast_to([P, v.shape[1], n])

        def over(v, m):
            return v.unsqueeze(1).broadcast_to([P, m, v.shape[1]])

        def by4(v):
            return v.rearrange("p (h n) -> p h n", h=4)


        def chunk_at(d, n):
            c = n if n < 4 else n - 4
            if d:
                c = (3 if n < 4 else 7) - c
            return (NT if n < 4 else 0) + c // 2, c % 2

        def chunk_col(d, n):
            t, u = chunk_at(d, n)
            return 2 * t + u

        def state_at(d, m2, n):
            if n < 4:
                return swork[:, n % 2, d, m2, :]
            if n == 12:
                return None
            t, u = chunk_at(d, n)
            return sprev[:, d, m2, 2 * t + u, :]

        block = ctx.enter_context(nc.Block())

        @block.sync
        def _(sp):
            issued = [0]

            def load(dst, src, name):
                sp.dma_start(dst, src).then_inc(s[name], 16)

            def stream_to(key):
                while True:
                    n = issued[0]
                    k, src, _, _ = weights[n]
                    if before[n] >= 0:
                        sp.wait_ge(s["w_used"], before[n] + 1)
                    sp.dma_start(slot_view(n), src).then_inc(s["ld_w", slot_of[n]], 16)
                    issued[0] += 1
                    if k == key:
                        return

            def rows(dst, row, src, n):
                sp.dma_start(dst[row:row + n, :], src.rearrange("(r n) -> r n", n=P)).then_inc(s["ld_vecs"], 16)

            for t in range(NT):
                load(xt[:, t, :], a["x"][0, t * P:(t + 1) * P, :], "ld_x")
            load(const[:, :], a["c_masks"], "ld_const")
            rows(vecs, V_PRE, a["norm_pre"][0], 8)
            rows(vecs, V_DN, a["dn_norm"][0], 1)
            rows(vecs, V_N1, a["norm1_g_2"][0], 8)
            rows(vecs, V_N2, a["norm2_g_2"][0], 8)
            rows(vecs, V_GLA, a["gla_norm_g_2"][0], 1)
            rows(vecs, V_PS, a["pool_scale_2"][0], 4)
            rows(vecs, V_BADA, a["b_ada_2"][0], 48)
            rows(vecs, V_C, a["c_2"][0], 8)
            rows(vecs, V_CC, a["c_ctx_2"], 8)
            rows(cvecs, 0, a["conv_w"][0].rearrange("k c -> (k c)"), CONV_K * 24)
            stream_to(("qkv", 0))
            load(rope, a["c_rope"], "ld_rope")
            load(qkn[:, 0, :], a["q_norm"].partition_broadcast(P), "ld_qkn")
            load(qkn[:, 1, :], a["k_norm"].partition_broadcast(P), "ld_qkn")
            load(gpar[:, 0, :], a["a_log"].rearrange("a d h -> a (d h)").partition_broadcast(P), "ld_gpar")
            load(gpar[:, 1, :], a["dt_bias"].rearrange("a d h -> a (d h)").partition_broadcast(P), "ld_gpar")
            stream_to(("dz", 1))
            sp.wait_ge(s["phase"], 4 * 3)
            load(rowv, a["norm_post"].partition_broadcast(P), "ld_rows")
            load(rowv2, a["ple_norm"].partition_broadcast(P), "ld_rows")
            for t in range(NT):
                load(x1[:, t, :], a["x"][0, t * P:(t + 1) * P, :], "ld_res")
            load(pin, a["p"][0, 0].rearrange("(t p) n -> p t n", p=P), "ld_p")
            stream_to("plep")
            sp.wait_ge(s["phase"], 4 * 4)
            for t in range(NTC):
                load(ctxt[:, t, :], a["ctx_2"][0, t * P:(t + 1) * P, :], "ld_ctx")
            load(wdec[0:RANK, :, :], a["w_decay_2"][0].rearrange("d r k -> r d k"), "ld_small")
            load(bdec[0:1, :], a["b_decay_2"].rearrange("a d k -> a (d k)"), "ld_small")
            load(wpool, a["w_pool_2"][0].rearrange("g c d -> c g d"), "ld_small")
            for g in range(2):
                sp.dma_start(pm[:, g, :, :], a["c_pool"][:, g, :, :]).then_inc(s["ld_pm", g], 16)
            stream_to(("p2", 1))
            for g in range(2, 4):
                sp.wait_ge(s["pool_used"], g - 1)
                sp.dma_start(pm[:, g % 2, :, :], a["c_pool"][:, g, :, :]).then_inc(s["ld_pm", g % 2], 16)
            stream_to(("wo2", 3))
            sp.wait_ge(s["phase"], 4 * 6)
            load(wrt[:, :, 0:4], a["w_router_group_2"][0].rearrange("(c p) n -> p c n", p=P), "ld_wrt")
            load(wrt[:, :, 4:36], a["w_router_expert_2"][0].rearrange("(c p) n -> p c n", p=P), "ld_wrt")
            load(rowf, a["final_norm_g_2"].rearrange("(a n) -> a n", a=1).partition_broadcast(P), "ld_rowf")
            for k in range(2):
                sp.dma_start(win[:, k, :, :], win_src[0, k]).then_inc(s["ld_win", k], 16)
                sp.dma_start(wout[:, k, :, :], wout_src[0, k]).then_inc(s["ld_wout", k], 16)
            for t in range(NT):
                sp.wait_ge(s["x3_ready"], t + 1)
                load(xn_dram[t * P:(t + 1) * P, :], xn[:, t, :], "xn_saved")
            load(table_dram.rearrange("(p n) o -> p (n o)", p=P), zero, "table_zeroed")
            load(y_dram[NE * CAP:, :].rearrange("o (p n) -> (o p) n", p=KC), zero[0:KC, :], "table_zeroed")
            sp.wait_ge(s["scattered"], 16 * 2 * NT)
            load(table, table_dram.rearrange("(b p n) o -> p b (n o)", b=2, p=P), "table_loaded")
            rounds = rounds_of(sp)
            with sp.Fori(0, rounds) as r:
                with sp.Fori(0, NE // 2 - 1) as i:
                    for k in range(2):
                        sp.wait_ge(s["moe_used"], r * NE + i * 2 + (k + 1))
                        sp.dma_start(win[:, k, :, :], win_next[i, k]).then_inc(s["ld_win", k], 16)
                        sp.dma_start(wout[:, k, :, :], wout_next[i, k]).then_inc(s["ld_wout", k], 16)
                with sp.If(r + 1 < rounds):
                    for k in range(2):
                        sp.wait_ge(s["moe_used"], r * NE + (NE - 1 + k))
                        sp.dma_start(win[:, k, :, :], win_src[0, k]).then_inc(s["ld_win", k], 16)
                        sp.dma_start(wout[:, k, :, :], wout_src[0, k]).then_inc(s["ld_wout", k], 16)
            for t in range(NT):
                sp.wait_ge(s["out_ready"], t + 1)
                sp.dma_start(out[0, t * P:(t + 1) * P, :], x3[:, t, :]).then_inc(s["ld_out"], 16)
            for name, ap in dumps:
                sp.dma_start(name, ap).then_inc(s["ld_out"], 16)
            sp.wait_ge(s["ld_out"], 16 * (NT + len(dumps)))

        @block.tensor
        def _(pe):
            L = Lane(pe, None)
            jobs = {"v": 0, "s": 0}
            banks = {"v": psv, "s": pss}
            at_slot = [0]
            mm, tr = nc.tensor.matmul, nc.tensor.transpose

            def bank(r):
                n = jobs[r]
                if n >= 4:
                    pe.wait_ge(s["free_" + r], n - 3)
                jobs[r] += 1
                return banks[r][:, n % 4, :]

            def slot(key):
                n = at_slot[0]
                assert weights[n][0] == key, (weights[n][0], key)
                at_slot[0] += 1
                pe.wait_ge(s["ld_w", slot_of[n]], 16 * turn_of[n])
                return slot_view(n)

            def used(n=1):
                for _ in range(n):
                    pe.drain().then_inc(s["w_used"], 1)

            def phase(n):
                pe.drain().then_inc(s["phase"], 1)
                pe.wait_ge(s["phase"], 4 * n)

            def product(o, pairs):
                for n, (l, r) in enumerate(pairs):
                    m = mm(o, l, r, start=(n == 0), stop=(n == len(pairs) - 1))
                return m

            def feature_tile(r, w, j, src, kc=KC, n=SEQ):
                o = bank(r)
                product(o[:, 0:n], [(w[:, c, j * P:(j + 1) * P], src[:, c, :]) for c in range(kc)])\
                    .then_inc(s["full_" + r], 1)

            def token_tile(r, w, t, src, c0=0, n=WC, kc=KC):
                o = bank(r)
                product(o[:, 0:n], [(src[:, c, t * P:(t + 1) * P], w[:, c, c0:c0 + n]) for c in range(kc)])\
                    .then_inc(s["full_" + r], 1)

            def turn(r, parts):
                o = bank(r)
                for n, v in enumerate(parts):
                    m = tr(o[:, n * P:n * P + v.shape[0]], v, ident[0:v.shape[0], 0:v.shape[0]])
                m.then_inc(s["full_" + r], 1)

            def turn_features(v):
                for r, c0 in (("v", 0), ("s", 4)):
                    turn(r, [v[:, c * P:(c + 1) * P] for c in range(c0, c0 + 4)])

            pe.wait_ge(s["ld_const"], 16)
            pe.wait_ge(s["ld_vecs"], 160)
            turn("s", [vecs[0:V_N, :]])
            turn("s", [cvecs[0:CONV_K * 24, :]])
            for t in range(NT):
                L.need(s["xn_ready"])
                turn_features(xt[:, t, :])
            L.need(s["hT_ready"], 8)
            for b in range(6):
                w = slot(("qkv", b))
                for t in range(NT):
                    token_tile("s", w, t, hT)
                used()
            w = slot("dbda")
            for t in range(NT):
                token_tile("v", w, t, hT, 0, 32)
            used()
            for t in range(NT):
                if t % 2 == 0:
                    w = slot(("az", t // 2))
                feature_tile("s", w, t % 2, hT)
                if t % 2:
                    used()
                L.need(s["rope_ready"])
                for h0, n in ((0, 4), (4, 4), (8, 2)):
                    turn("s", [atok[:, t, h * HD:(h + 1) * HD] for h in range(h0, h0 + n)])
            L.need(s["qkT_ready"], 12)
            L.need(s["atok_ready"], 24)
            assert jobs["s"] == S_ATT
            for what, i in steps:
                h, t = divmod(i, NT)
                if what == "scores":
                    mm(bank("s"), qkT[:, h, t * P:(t + 1) * P], qkT[:, NH + h // (NH // NKV), :], start=True,
                       stop=True).then_inc(s["full_s"], 1)
                elif what == "turn":
                    L.need(s["probsn_ready"])
                    turn("s", [pb[:, i % 3, k * P:(k + 1) * P] for k in range(NT)])
                elif what == "head":
                    L.need(s["pT_ready"], NT)
                    kv = 1280 + (i // (NH // NKV)) * HD
                    product(bank("s"), [(atok[:, k, kv:kv + HD], pT[:, i % 2, k, :]) for k in range(NT)])\
                        .then_inc(s["full_s"], 1)
                else:
                    if i % 2 == 0:
                        w = slot(("az", i // 2))
                    feature_tile("s", w, i % 2, hT)
                    if i % 2:
                        used()
            L.need(s["oz_ready"], KC)
            for b in range(4):
                w, g = slot(("bra", b)), slot(("ga", b))
                for j in range(2):
                    feature_tile("v", w, j, oT)
                    feature_tile("s", g, j, hT)
                used(2)
            phase(1)

            L.need(s["gg_ready"])
            o = bank("v")
            for t in range(NT):
                for d in range(2):
                    m = mm(o[:, t * 16 + d * 8:t * 16 + d * 8 + 8], tri[d], gbuf[:, 0, t, d * 8:d * 8 + 8],
                           start=True, stop=True)
            m.then_inc(s["full_v"], 1)
            for j in range(24 + 1):
                if j < 24:
                    if j % 2 == 0:
                        w = slot(("dqkv", j // 2))
                    feature_tile("v", w, j % 2, hT)
                    if j % 2:
                        used()
                if j > 16:
                    pe.wait_ge(s["silu_ready"], j)
                    turn("s", [cst[:, (j - 1) % 2, t * P:(t + 1) * P] for t in range(NT)])
                if SUM_LAG <= j < 16 + SUM_LAG:
                    L.need(s["sq_ready"])
                    o = bank("s")
                    mm(o, ones, csq[:, (j - SUM_LAG) % 2, :], start=True, stop=True).then_inc(s["full_s"], 1)
                if 8 + TURN_LAG <= j < 16 + TURN_LAG:
                    pe.wait_ge(s["norm_ready"], j - TURN_LAG + 1)
                    turn("s", [kT[:, j - TURN_LAG - 8, t * P:(t + 1) * P] for t in range(NT)])
            phase(2)

            ada = [0]

            def ada_slot():
                if ada[0] == 24:
                    return
                w = slot(("ada", ada[0]))
                o = bank("s")
                for j in range(2):
                    m = product(o[:, 2 * j:2 * j + 2], [(w[:, c, j * P:(j + 1) * P], csilu[:, c, :])
                                                        for c in range(KC)])
                m.then_inc(s["full_s"], 1)
                used()
                ada[0] += 1

            def four(r, make):
                o = bank(r)
                for h in range(4):
                    ps = make(h)
                    for q, (l, x) in enumerate(ps):
                        m = mm(o[:, h * P:(h + 1) * P], l, x, start=(q == 0), stop=(q == len(ps) - 1))
                m.then_inc(s["full_" + r], 1)

            def decay_rows(n):
                st, hg = PAIRS[n]
                for d in range(2):
                    t, dh = tile_of(d, st), d * 8 + hg * 4
                    four("s", lambda h: [(gbuf[:, 0, t, dh + h:dh + h + 1].broadcast_to([P, P]), tri[d])])

            def key_products(n):
                st, hg = PAIRS[n]
                for d in range(2):
                    tk = slice(tile_of(d, st) * P, (tile_of(d, st) + 1) * P)
                    four("v", lambda h: [(kT[:, hg * 4 + h, tk], kT[:, hg * 4 + h, tk])])
                    four("v", lambda h: [(kT[:, hg * 4 + h, tk], qT[:, hg * 4 + h, tk])])

            decay_rows(0)
            key_products(0)
            for n, (st, hg) in enumerate(PAIRS):
                for d in range(2):
                    g = buffers(n, d)
                    L.need(s["c_ready", d])
                    turn("v", [g[C_C0][:, h, :] for h in range(4)])
                for k in range(1, LEVELS):
                    for d in range(2):
                        g = buffers(n, d)
                        L.need(s["c_ready", d])
                        L.need(s["tt_ready", d])
                        four("s", lambda h: [(g[C_C0 + k % 2][:, h, :], g[C_TT][:, h, :])])
                    if k in (1, 3, 5):
                        ada_slot()
                    for d in range(2):
                        g = buffers(n, d)
                        L.need(s["zz_ready", d])
                        L.need(s["t_ready", d])
                        four("v", lambda h: [(g[C_T][:, h, :], g[C_Z][:, h, :])])
                        if k < LEVELS - 1:
                            four("v", lambda h: [(g[C_Z][:, h, :], g[C_T][:, h, :])])
                if n + 1 < len(PAIRS):
                    decay_rows(n + 1)
                for d in range(2):
                    g = buffers(n, d)
                    L.need(s["kbe_ready", d])
                    L.need(s["tt_ready", d])
                    four("s", lambda h: [(g[C_KBE][:, h, :], g[C_TT][:, h, :])])
                for d in range(2):
                    g = buffers(n, d)
                    L.need(s["nwt_ready", d])
                    if st:
                        pe.wait_ge(s["group_done", d], n - 1)
                    four("v", lambda h: [(g[C_TT][:, h, :], g[C_VB][:, h, :])] +
                         ([(g[C_Z][:, h, :], state[:, d, hg * 4 + h, :])] if st else []))
                if n + 1 < len(PAIRS):
                    key_products(n + 1)
                for d in range(2):
                    g = buffers(n, d)
                    L.need(s["vn_ready", d])
                    L.need(s["at_ready", d])
                    L.need(s["qg_ready", d])
                    four("v", lambda h: ([(g[C_E][:, h, :], state[:, d, hg * 4 + h, :])] if st else []) +
                         [(g[C_X][:, h, :], g[C_VN][:, h, :])])
                for d in range(2):
                    g = buffers(n, d)
                    L.need(s["kdec_ready", d])
                    four("v", lambda h: [(g[C_KDEC][:, h, :], g[C_VN][:, h, :])])

            phase(3)
            for t in range(NT):
                L.need(s["on_ready"])
                for h0 in (0, 4):
                    turn("v", [oacc[:, t, h, :] for h in range(h0, h0 + 4)])
            for b in range(4):
                w = slot(("dz", b))
                for j in range(2):
                    feature_tile("s", w, j, hT)
                used()
            L.need(s["dz_ready"], KC)
            for b in range(4):
                w, g = slot(("brd", b)), slot(("gd", b))
                for j in range(2):
                    feature_tile("v", w, j, onT)
                    feature_tile("s", g, j, hT)
                used(2)
            L.need(s["mixT_ready"], KC)
            for b in range(4):
                w = slot(("wo", b))
                for t in range(NT):
                    token_tile("s", w, t, mixT)
                used()
            pe.wait_ge(s["ld_p"], 16)
            for t in range(NT):
                turn("v", [pin[:, t, c * P:(c + 1) * P] for c in range(2)])
            for t in range(NT):
                L.need(s["x1_ready"])
                turn_features(x1[:, t, :])
            L.need(s["x1T_ready"], 8)
            for b in range(4):
                w = slot(("pleg", b))
                for t in range(NT):
                    token_tile("s", w, t, x1T)
                used()
            L.need(s["pinT_ready"], NT)
            w = slot("plep")
            for t in range(NT):
                for c0 in (0, 512):
                    token_tile("v", w, t, pinT, c0, 512, 2)
            used()
            phase(4)

            for t in range(NT):
                L.need(s["x2_ready"])
                turn_features(xn[:, t, :])
            for t in range(NTC):
                L.need(s["x2_ready"])
                turn_features(ctxt[:, t, :])
            L.need(s["h2_ready"], 8)
            L.need(s["hc_ready"], 4)
            w = slot("q2")
            for j in range(2):
                feature_tile("s", w, j, h2T)
            used()
            w = slot("k2")
            for j in range(2):
                feature_tile("s", w, j, h2T)
            for t in range(NT):
                token_tile("s", w, t, h2T)
            for t in range(NTC):
                token_tile("s", w, t, hcT)
            used()
            for b in range(2):
                w = slot(("v2", b))
                for t in range(NT):
                    token_tile("v", w, t, h2T)
                for t in range(NTC):
                    token_tile("v", w, t, hcT)
                used()
            for b in range(2):
                w = slot(("g2", b))
                for j in range(2):
                    feature_tile("s", w, j, h2T)
                used()
            w = slot("a2")
            for d in range(2):
                for src, n in ((h2T, SEQ), (hcT, CTX)):
                    o = bank("v")
                    product(o[0:RANK, 0:n], [(w[:, c, d * RANK:(d + 1) * RANK], src[:, c, :]) for c in range(KC)])\
                        .then_inc(s["full_v"], 1)
            used()
            for b in range(2):
                w = slot(("p2", b))
                for t in range(NT):
                    token_tile("v", w, t, h2T)
                used()
            L.need(s["p2_ready"], 2 * NT)
            pe.wait_ge(s["ld_small"], 48)
            for g in range(4 + 1):
                if g < 4:
                    pe.wait_ge(s["ld_pm", g % 2], 16 * (g // 2 + 1))
                    o = bank("v")
                    product(o, [(p2[:, k, g * P:(g + 1) * P], pm[:, g % 2, k, :]) for k in range(NT)])\
                        .then_inc(s["full_v"], 1)
                    pe.drain().then_inc(s["pool_used"], 1)
                if g >= 1:
                    L.need(s["mT_ready"])
                    o = bank("s")
                    mm(o, wpool[:, g - 1, :], pmT[:, (g - 1) % 2, :], start=True, stop=True)\
                        .then_inc(s["full_s"], 1)
            phase(5)

            L.need(s["a2_ready"], 4)
            for t in range(NT + NTC):
                o = bank("s")
                for d in range(2):
                    mm(o[:, d * 256:(d + 1) * 256], a2T[0:RANK, d, t * P:(t + 1) * P], wdec[0:RANK, d, :],
                       start=True, stop=False)
                    m = mm(o[:, d * 256:(d + 1) * 256], ones[0:1, :], bdec[0:1, d * 256:(d + 1) * 256],
                           start=False, stop=True)
                m.then_inc(s["full_s"], 1)
            L.need(s["la_ready"], NT + NTC)
            for d in range(2):
                for m2 in range(2):
                    col = d * 256 + m2 * P
                    o = bank("s")
                    for t in range(NT):
                        m = mm(o[:, t * P:(t + 1) * P], la[:, t, col:col + P], blk[d], start=True, stop=True)
                    m.then_inc(s["full_s"], 1)
                    o = bank("s")
                    for t in range(NTC):
                        m = mm(o[:, t * P:(t + 1) * P], la[:, NT + t, col:col + P], blk[d], start=True, stop=True)
                    m.then_inc(s["full_s"], 1)
            for t in range(NT + NTC):
                o = bank("s")
                for d in range(2):
                    m = mm(o[:, d * 256:(d + 1) * 256], blk_rest[d], la[:, t, d * 256:(d + 1) * 256],
                           start=True, stop=True)
                m.then_inc(s["full_s"], 1)
            L.need(s["kst_ready"], NT + NTC)
            L.need(s["k2_ready"])
            for n in range(12):
                for d in range(2):
                    t, u = chunk_at(d, n)
                    o = bank("v")
                    for m2 in range(2):
                        m = mm(o[:, m2 * 256:(m2 + 1) * 256],
                               kst[u * CH2:(u + 1) * CH2, t, d * 256 + m2 * P:d * 256 + (m2 + 1) * P],
                               v2[u * CH2:(u + 1) * CH2, t, m2 * 256:(m2 + 1) * 256], start=True, stop=True)
                    m.then_inc(s["full_v"], 1)
            L.need(s["qb_ready"], 4)
            L.need(s["sprev_ready"])
            for h in range(H2):
                m2, hp = h // 2, slice((h % 2) * 64, (h % 2) * 64 + 64)
                for d in range(2):
                    o = bank("v")
                    for t in range(NT):
                        tk = slice(t * P, (t + 1) * P)
                        m = mm(o[:, tk], kb[hp, d, m2, tk], qb[hp, d, m2, tk], start=True, stop=True)
                    m.then_inc(s["full_v"], 1)
                L.need(s["sc_ready"], 2)
                o = bank("s")
                for d in range(2):
                    for t in range(NT):
                        tk = slice(t * P, (t + 1) * P)
                        mm(o[:, tk], v2[:, t, h * P:(h + 1) * P], scm[:, (h % 2) * 2 + d, tk],
                           start=(d == 0 and t == 0), stop=False, skip_group_check=True)
                    for c in range(8):
                        ck = slice(c * CH2, (c + 1) * CH2)
                        m = mm(o[:, ck], sprev[hp, d, m2, c, :], qb[hp, d, m2, ck], start=False,
                               stop=(d == 1 and c == 7), skip_group_check=True)
                m.then_inc(s["full_s"], 1)
                L.need(s["sq2_ready"])
                o = bank("s")
                mm(o, ones, eb[:, h % 2, :], start=True, stop=True).then_inc(s["full_s"], 1)
            L.need(s["cat_ready"], 8)
            for c0 in (0, 4):
                o = bank("v")
                for c in range(4):
                    m = mm(o[:, c * P:(c + 1) * P], mod[:, 16 + c0 + c, 0:1].broadcast_to([P, P]), ident,
                           start=True, stop=True)
                m.then_inc(s["full_v"], 1)
            for b in range(4):
                w = slot(("wo2", b))
                for t in range(NT):
                    token_tile("v", w, t, catT)
                used()
            phase(6)

            for t in range(NT):
                L.need(s["x3_ready"])
                turn_features(xn[:, t, :])
            L.need(s["h3_ready"], 8)
            pe.wait_ge(s["ld_wrt"], 32)
            o = bank("v")
            for t in range(NT):
                m = product(o[:, t * 36:(t + 1) * 36], [(h3T[:, c, t * P:(t + 1) * P], wrt[:, c, :])
                                                        for c in range(KC)])
            m.then_inc(s["full_v"], 1)
            for c0 in (0, 4):
                o = bank("v")
                for c in range(4):
                    m = mm(o[:, c * P:(c + 1) * P], mod[:, 40 + c0 + c, 0:1].broadcast_to([P, P]), ident,
                           start=True, stop=True)
                m.then_inc(s["full_v"], 1)
            L.need(s["picked_ready"])
            o = bank("v")
            for t in range(NT):
                product(o[:, t * NE:(t + 1) * NE], [(ones, picked[:, q, :]) for q in range(t)] +
                        [(const[:, C_LT:C_LT + P], picked[:, t, :])])
            product(o[:, NT * NE:(NT + 1) * NE], [(ones, picked[:, q, :]) for q in range(NT)])\
                .then_inc(s["full_v"], 1)
            pe.wait_ge(s["table_loaded"], 16)
            turn_slots = bank("v")
            for k in range(2):
                m = tr(turn_slots[0:CAP, k * P:(k + 1) * P], table[:, k, :], ident)
            m.then_inc(s["full_v"], 1)
            pe.wait_ge(s["xg_k0"], 16)
            o = bank("v")
            for c in range(KC):
                m = tr(o[:, c * CAP:(c + 1) * CAP], xg[0:CAP, 0, c * P:(c + 1) * P], ident[0:CAP, 0:CAP])
            m.then_inc(s["full_v"], 1)
            v0, s0 = jobs["v"], jobs["s"]
            VJ, SJ = 3 * XPT, 2 * XPT
            rounds = rounds_of(pe)
            with pe.Fori(0, rounds * (NE // XPT)) as i:
                nv, ns = [0], [0]

                def vbank():
                    k = nv[0]
                    nv[0] += 1
                    pe.wait_ge(s["free_v"], i * VJ + (v0 + k - 3))
                    return psv[:, (v0 + k) % 4, :]

                def sbank():
                    k = ns[0]
                    ns[0] += 1
                    pe.wait_ge(s["free_s"], i * SJ + (s0 + k - 3))
                    return pss[:, (s0 + k) % 4, :]

                for q in range(XPT):
                    k = q % 2
                    nth = i * (XPT // 2) + (q // 2 + 1)
                    pe.wait_ge(s["ld_win", k], nth * 16)
                    pe.wait_ge(s["xe_ready"], i * XPT + (q + 1))
                    pe.wait_ge(s[f"xg_k{1 - k}"], nth * 16 if k == 0 else nth * 16 + 16)
                    a_bank, u_bank, turn_bank = sbank(), vbank(), vbank()
                    for o, full, c0 in ((a_bank, "full_s", 0), (u_bank, "full_v", DE)):
                        for j in range(2):
                            m = product(o[:, j * CAP:(j + 1) * CAP],
                                        [(win[:, k, c, c0 + j * P:c0 + (j + 1) * P], xe[:, k, c, :])
                                         for c in range(KC)])
                        m.then_inc(s[full], 1)
                    for c in range(KC):
                        m = tr(turn_bank[:, c * CAP:(c + 1) * CAP], xg[0:CAP, 1 - k, c * P:(c + 1) * P],
                               ident[0:CAP, 0:CAP])
                    m.then_inc(s["full_v"], 1)
                    pe.wait_ge(s["hid_ready"], i * XPT + (q + 1))
                    pe.wait_ge(s["ld_wout", k], nth * 16)
                    for get, full, c0 in ((sbank, "full_s", 0), (vbank, "full_v", 512)):
                        product(get()[0:CAP, :], [(hid[:, k, c * CAP:(c + 1) * CAP], wout[:, k, c, c0:c0 + 512])
                                                  for c in range(2)]).then_inc(s[full], 1)
                    pe.drain().then_inc(s["moe_used"], 1)

        @block.scalar
        def _(act):
            L = Lane(act, s["chain_s"])
            seen = [0]
            A = nc.scalar.activation

            def full():
                L.need(s["full_s"])
                seen[0] += 1
                return pss[:, (seen[0] - 1) % 4, :]

            def evict(dst, n, sig, func=ACT.Copy, **kw):
                b = full()
                src = b[:, 0:n]
                if len(dst.shape) == 3:
                    src = src.rearrange("p (a b) -> p a b", b=dst.shape[2])
                L.did(A(dst, src, func, **kw), s[sig], [s["free_s"]])

            def root(v):
                L.need(s["rs_in"])
                L.did(A(v, v, ACT.Sqrt), s["rs_out"])

            def turned(dst, t, gains, shifts, sig):
                b = full()
                for c in range(4, KC):
                    o, src = dst[:, c, t * P:(t + 1) * P], b[:, (c - 4) * P:(c - 3) * P]
                    g = gains[:, c:c + 1]
                    if shifts is None:
                        ins = A(o, src, ACT.Copy, scale=g)
                    else:
                        ins = A(o, src, ACT.Identity, scale=g, bias=shifts[:, c:c + 1])
                    L.did(ins, None, [s["free_s"], s[sig]] if c == KC - 1 else [])

            def phase(n):
                act.sem_inc(s["phase"])
                act.wait_ge(s["phase"], 4 * n)

            evict(cols[:, 0:V_N], V_N, "cols_ready")
            evict(ccols[:, :], CONV_K * 24, "cols_ready")
            L.did(A(csilu[:, :, :].rearrange("p c k -> p k c"),
                    cols[:, V_C:V_C + 16].rearrange("p (k c) -> p k c", k=2), ACT.Silu))
            root(ss[:, 0:NT])
            for t in range(NT):
                turned(hT, t, cols[:, V_PRE:V_PRE + 8], None, "hT_ready")
            for b in range(6):
                for t in range(NT):
                    evict(atok[:, t, b * WC:(b + 1) * WC], WC, "atok_ready")
            for t in range(NT):
                evict(azs[:, t, :], SEQ, "az_ready")
                root(ss[:, 16:26])
                for h0, n in ((0, 4), (4, 4), (8, 2)):
                    evict(qkT[:, h0:h0 + n, t * P:(t + 1) * P], n * P, "qkT_ready")
            for what, i in steps:
                h, t = divmod(i, NT)
                if what == "scores":
                    L.need(s["negmax_ready"])
                    b = full()
                    L.did(A(pb[:, i % 3, :], b, ACT.Exp, bias=small[:, 64 + i:65 + i], scale=HD ** -0.5,
                            accum_out=small[:, 96 + i:97 + i]), s["probs_ready"], [s["free_s"]])
                elif what == "turn":
                    evict(pT[:, h % 2, :, t * P:(t + 1) * P], SEQ, "pT_ready")
                elif what == "head":
                    evict(oT[:, i, :], SEQ, "oT_ready")
                else:
                    evict(azs[:, i, :], SEQ, "az_ready")
            for j in range(KC):
                L.did(A(azs[:, j, :], azs[:, j, :], ACT.Silu), s["silu_z"])
            ntmp = [0]

            def gate(tmp, func):
                n = ntmp[0]
                ntmp[0] += 1
                if n >= 2:
                    act.wait_ge(s["tmp_used"], n - 1)
                evict(tmp[:, n % 2, :], SEQ, "tmp_ready", func)

            for j in range(KC):
                gate(tmpA, ACT.Sigmoid)
            phase(1)

            act.wait_ge(s["ld_gpar"], 32)
            L.did(A(gpar[:, 2, :], gpar[:, 0, :], ACT.Exp), s["ga_ready"])
            L.need(s["ga_step"])
            L.did(A(gbuf[:, 6, :, :], gbuf[:, 6, :, :], ACT.Exp))
            L.did(A(gbuf[:, 6, :, :], gbuf[:, 6, :, :], ACT.Ln, bias=one), s["ga_ready"])
            L.did(A(gbuf[:, 3, :, :], gb[:, :, 0:16], ACT.Sigmoid), s["ga_ready"])
            L.need(s["gG_ready"])
            L.did(A(gbuf[:, 2, :, :], gbuf[:, 1, :, :], ACT.Exp), s["ga_ready"])
            for j in range(24 + 1):
                if j > 16:
                    evict(vtok[:, :, j - 17, :], SEQ, "vtok_ready")
                if SUM_LAG <= j < 16 + SUM_LAG:
                    n = j - SUM_LAG
                    if n >= 2:
                        act.wait_ge(s["norm_ready"], n - 1)
                    if n < 8:
                        evict(crt[:, n % 2, :], SEQ, "rt_ready", ACT.Sqrt, bias=eps128, scale=float(HD))
                    else:
                        evict(crt[:, n % 2, :], SEQ, "rt_ready", ACT.Sqrt, bias=eps)
                if 8 + TURN_LAG <= j < 16 + TURN_LAG:
                    evict(ktok[:, :, j - TURN_LAG - 8, :], SEQ, "ktok_ready")
                if j < 24:
                    L.need(s["conv_ready"])
                    dst = qT[:, j, :] if j < 8 else kT[:, j - 8, :] if j < 16 else cst[:, j % 2, :]
                    L.did(A(dst, conv[:, j % 2, :], ACT.Silu), s["silu_ready"])
                n = j - (SUM_LAG - 1)
                if 0 <= n < 16:
                    src = qT[:, n, :] if n < 8 else kT[:, n - 8, :]
                    L.did(A(csq[:, n % 2, :], src, ACT.Square), s["sq_ready"])
            phase(2)

            ada = [0]

            def ada_slot():
                if ada[0] < 24:
                    evict(mod[:, 2 * ada[0]:2 * ada[0] + 2, :], 4, "mod_ready")
                    ada[0] += 1

            def decay_rows(n):
                for d in range(2):
                    g = buffers(n, d)
                    if n:
                        act.wait_ge(s["c_ready", d], n * LEVELS)
                    b = full()
                    L.did(A(g[C_X], by4(b), ACT.Copy))
                    L.did(A(g[C_E], by4(b), ACT.Exp), s["e_ready", d], [s["free_s"]])
                    last = P - 1 if d == 0 else 0
                    L.did(A(glast[:, n % 2, d, :], g[C_E][:, :, last], ACT.Copy), s["glast_ready", d])

            def decays(n):
                for d in range(2):
                    g = buffers(n, d)
                    L.need(s["x_ready", d])
                    L.did(A(g[C_D1], g[C_D1], ACT.Exp, scale=-1.0), s["d1_ready", d])
                    L.did(A(g[C_X], g[C_X], ACT.Exp), s["d2_ready", d])

            decay_rows(0)
            decays(0)
            for n, (st, hg) in enumerate(PAIRS):
                for k in range(1, LEVELS):
                    for d in range(2):
                        b = full()
                        L.did(A(buffers(n, d)[C_Z], by4(b), ACT.Copy), s["zz_ready", d], [s["free_s"]])
                    if k in (1, 3, 5):
                        ada_slot()
                if n + 1 < len(PAIRS):
                    decay_rows(n + 1)
                for d in range(2):
                    b = full()
                    L.did(A(buffers(n, d)[C_Z], by4(b), ACT.Copy, scale=-1.0), s["nwt_ready", d], [s["free_s"]])
                if n + 1 < len(PAIRS):
                    decays(n + 1)
            phase(3)

            root(ss[:, 0:32])
            for j in range(KC):
                gate(tmpB, ACT.Silu)
            for j in range(KC):
                gate(tmpB, ACT.Sigmoid)
            for b in range(4):
                for t in range(NT):
                    evict(mo[:, t, b * WC:(b + 1) * WC], WC, "mo_ready")
            root(ss[:, 0:NT])
            for t in range(NT):
                b = full()
                L.did(A(x1T[:, 4:8, t * P:(t + 1) * P], by4(b), ACT.Copy), None, [s["x1T_ready"], s["free_s"]])
            for b in range(4):
                for t in range(NT):
                    evict(sg[:, t, b * WC:(b + 1) * WC], WC, "sg_ready", ACT.Sigmoid)
            root(ss[:, 0:NT])
            phase(4)

            root(ss[:, 0:NT])
            for t in range(NT):
                turned(h2T, t, gain[:, 0:8], mod[:, 0:8, 0], "h2_ready")
            root(ss[:, 0:NTC])
            for t in range(NTC):
                turned(hcT, t, gain[:, 8:16], mod[:, 0:8, 1], "hc_ready")
            for j in range(2):
                evict(q2T[:, j, :], SEQ, "k2_ready", ACT.Copy, scale=DK2 ** -0.5)
            for j in range(2):
                evict(k2T[:, j, :], SEQ, "k2_ready")
            for t in range(NT + NTC):
                evict(k2[:, t, :], 256, "k2_ready")
            for j in range(4):
                evict(g2T[:, j, :], SEQ, "k2_ready", ACT.Silu)
            for g in range(4):
                b = full()
                L.did(A(catT[:, 4 + g, :], b, ACT.Copy, scale=cols[:, V_PS + g:V_PS + g + 1]), s["cat_ready"], [s["free_s"]])
            phase(5)

            for t in range(NT + NTC):
                b = full()
                if t >= 2:
                    act.wait_ge(s["la_ready"], t - 1)
                L.did(A(z2[:, t % 2, :], b, ACT.Copy), s["z_ready"], [s["free_s"]])
                L.need(s["absz_ready"])
                L.did(A(z3[:, t % 2, :], z3[:, t % 2, :], ACT.Exp, scale=-1.0))
                L.did(A(z3[:, t % 2, :], z3[:, t % 2, :], ACT.Ln, bias=one), s["lz_ready"])
            for n in range(4):
                d, m2 = divmod(n, 2)
                b = full()
                if n >= 2:
                    act.wait_ge(s["qb_ready"], n - 1)
                L.did(A(eb[:, n % 2, :], b, ACT.Exp))
                L.did(A(enb[:, n % 2, :], b, ACT.Exp, scale=-1.0))
                ends = b.rearrange("p (c i) -> p c i", i=CH2)[:, :, CH2 - 1 if d == 0 else 0]
                L.did(A(dec2[:, d, m2, 0:8], ends, ACT.Exp), s["bexp_ready"], [s["free_s"]])
                b = full()
                ends = b[:, 0:CTX].rearrange("p (c i) -> p c i", i=CH2)[:, :, CH2 - 1 if d == 0 else 0]
                L.did(A(dec2[:, d, m2, 8:12], ends, ACT.Exp), s["bexp_ready"], [s["free_s"]])
            for t in range(NT + NTC):
                evict(kst[:, t, :], 512, "kexp_ready", ACT.Exp)
            L.need(s["qb_ready"], 4)
            for h in range(H2):
                b = full()
                if h >= 2:
                    act.wait_ge(s["o2_ready"], h - 1)
                L.did(A(eb[:, h % 2, :], b, ACT.Square), s["sq2_ready"])
                L.did(A(catT[:, h, :], b, ACT.Copy), s["rt2_ready"], [s["free_s"]])
                b = full()
                L.did(A(enb[:, h % 2, :], b, ACT.Sqrt, bias=eps, scale=1.0 / DV2), s["rt2_ready"], [s["free_s"]])
            phase(6)

            root(ss[:, 0:NT])
            for t in range(NT):
                turned(h3T, t, gain[:, 16:24], mod[:, 24:32, 0], "h3_ready")
            L.need(s["lg_ready"])
            L.did(A(lexp, lexp, ACT.Exp), s["lexp_ready"])
            q0 = seen[0]
            act.sem_inc(s["st_y0"], 16)
            act.sem_inc(s["st_y1"], 16)
            rounds = rounds_of(act)
            with act.Fori(0, rounds) as r:
                act.wait_ge(s["combined"], r + 1)
                with act.Fori(0, NE // XPT) as ir:
                    i = r * (NE // XPT) + ir
                    L.enter(i, {s["sil_ready"]: XPT, s["free_s"]: 2 * XPT, s["chain_s"]: XPT},
                            {s["full_s"]: 2 * XPT, s["sil_used"]: XPT, s["y1_ready"]: XPT})
                    for q in range(XPT):
                        k = q % 2
                        L.need(s["full_s"])
                        L.need(s["sil_used"])
                        L.did(A(sil[:, k, :], pss[:, (q0 + 2 * q) % 4, 0:2 * CAP], ACT.Silu), s["sil_ready"],
                              [s["free_s"]])
                        L.need(s["full_s"])
                        act.wait_ge(s[f"st_y{k}"], (i * (XPT // 2) + (q // 2 + 1)) * 16)
                        L.did(A(yb[0:CAP, k, 0:512], pss[0:CAP, (q0 + 2 * q + 1) % 4, :], ACT.Copy), None,
                              [s["free_s"]])
                        L.need(s["y1_ready"])
                        act.dma_start(y_store[ir, q], yb[0:CAP, k, :]).then_inc(s[f"st_y{k}"], 16)
                    L.leave(0)
            root(ss[:, 0:NT])

        @block.gpsimd
        def _(pool):
            L = Lane(pool, s["chain_p"])
            TT = nc.gpsimd.tensor_tensor

            def phase(n):
                pool.sem_inc(s["phase"])
                pool.wait_ge(s["phase"], 4 * n)

            phase(1)
            pool.wait_ge(s["phase"], 4)
            phase(2)
            def level(n, d, k):
                g = buffers(n, d)
                lv = const[:, C_LV + (d * LEVELS + k) * P:C_LV + (d * LEVELS + k + 1) * P]
                L.did(TT(g[C_C0 + k % 2], g[C_D1], over(lv, 4), ALU.mult), s["c_ready", d])

            for n, (st, hg) in enumerate(PAIRS):
                H4 = slice(hg * 4, hg * 4 + 4)
                for d in range(2):
                    g, t = buffers(n, d), tile_of(d, st)
                    if n:
                        L.need(s["vn_ready", d])
                    L.did(TT(g[C_VB], vtok[:, t, H4, :], spread(gbuf[:, 3, t, hcols(d, hg)]), ALU.mult))
                    L.did(TT(g[C_KBE], ktok[:, t, H4, :], spread(gbuf[:, 4, t, hcols(d, hg)]), ALU.mult),
                          s["kbe_ready", d])
                for d in range(2):
                    L.need(s["l_ready", d])
                    level(n, d, 0)
                for d in range(2):
                    if n:
                        L.need(s["group_done", d])
                    level(n, d, 1)
                for k in range(2, LEVELS):
                    for d in range(2):
                        g, t = buffers(n, d), tile_of(d, st)
                        if k == 2:
                            pool.wait_ge(s["t_ready", d], n * (LEVELS - 1) + 1)
                        else:
                            L.need(s["zz_ready", d])
                        level(n, d, k)
                        if k == 2:
                            L.need(s["at_pre", d])
                            L.did(TT(g[C_X], g[C_X], over(tri[d], 4), ALU.mult), s["at_ready", d])
                        if k == 3:
                            L.did(TT(g[C_KDEC], ktok[:, t, H4, :], spread(kcol[:, n % 2, d, :]), ALU.mult),
                                  s["kdec_ready", d])
                        if k == 4:
                            L.need(s["e_ready", d])
                            L.need(s["glast_ready", d])
                            L.did(TT(g[C_E], g[C_E], qT[:, H4, t * P:(t + 1) * P], ALU.mult), s["qg_ready", d])
                for d in range(2):
                    L.need(s["zz_ready", d], 2)
            phase(3)
            phase(4)
            phase(5)
            phase(6)

            pool.wait_ge(s["xn_saved"], 16 * NT)
            pool.wait_ge(s["table_zeroed"], 32)
            pool.wait_ge(s["slots_ready"], 1)
            for t in range(NT):
                for k in range(2):
                    nc.gpsimd.indirect_dma_start(
                        table_dram, bass.IndirectOffsetOnAxis(slot_u[:, 2 * t + k:2 * t + k + 1], 0),
                        const[:, C_TOK + t:C_TOK + t + 1], None).then_inc(s["scattered"], 16)

            def gather(k):
                nc.gpsimd.indirect_dma_start(
                    xg[0:CAP, k, :], None, xn_dram, bass.IndirectOffsetOnAxis(icol[0:CAP, k:k + 1], 0))\
                    .then_inc(s[f"xg_k{k}"], 16)

            L.need(s["index_ready"])
            for k in range(2):
                L.did(nc.gpsimd.tensor_copy(icol[0:CAP, k:k + 1], index[0:CAP, k:k + 1]))
                gather(k)
            rounds = rounds_of(pool)
            with pool.Fori(0, rounds) as r:
                with pool.Fori(0, NE // XPT) as ir:
                    i = r * (NE // XPT) + ir
                    for q in range(XPT):
                        k = q % 2
                        pool.wait_ge(s["xe_ready"], i * XPT + (q + 1))
                        nc.gpsimd.tensor_copy(icol[0:CAP, k:k + 1], index[0:CAP, bass.ds(i * XPT + (q + 2), 1)])\
                            .then_inc(s["icol_ready"], 1)
                        pool.wait_ge(s["icol_ready"], 1)
                        gather(k)
                        pool.sem_inc(s["icol_ready"], -1)
                for k in range(2):
                    pool.wait_ge(s[f"st_y{k}"], r * (NE // 2 * 16) + (NE // 2 * 16 + 16))
                pool.wait_ge(s["combined"], r + 1)
                nc.gpsimd.tensor_copy(bcol, back_u[:, bass.ds(r, 1), :].rearrange("p o n -> p (o n)"))\
                    .then_inc(s["bcol_ready"], 1)
                pool.wait_ge(s["bcol_ready"], 1)
                for t in range(NT):
                    for k in range(2):
                        nc.gpsimd.indirect_dma_start(
                            ygat[:, k, t, :], None, y_dram,
                            bass.IndirectOffsetOnAxis(bcol[:, 2 * t + k:2 * t + k + 1], 0))\
                            .then_inc(s["ygat_ready"], 16)
                pool.sem_inc(s["bcol_ready"], -1)
            for k in range(2):
                pool.wait_ge(s[f"xg_k{k}"], rounds * (NE // 2 * 16) + 16)

        @block.vector
        def _(dve):
            L = Lane(dve, s["chain_v"])
            seen = [0]
            V = nc.vector

            def full():
                L.need(s["full_v"])
                seen[0] += 1
                return psv[:, (seen[0] - 1) % 4, :]

            def phase(n):
                dve.sem_inc(s["phase"])
                dve.wait_ge(s["phase"], 4 * n)

            def squares(v, dst, j):
                L.did(V.tensor_tensor_reduce(j, v, v, 1.0, 0.0, ALU.mult, ALU.add, dst))

            def inv_root(v, n):
                L.did(V.tensor_scalar(v, v, 1.0 / n, EPS, ALU.mult, ALU.add), s["rs_in"])
                L.need(s["rs_out"])
                L.did(V.reciprocal(v, v))

            def mul(o, x, y, *sig):
                L.did(V.tensor_tensor(o, x, y, ALU.mult), *sig)

            def add(o, x, y, *sig):
                L.did(V.tensor_tensor(o, x, y, ALU.add), *sig)

            def scale(o, x, c, *sig):
                L.did(V.tensor_scalar(o, x, c, None, ALU.mult), *sig)

            def turned(dst, t, gains, shifts, sig):
                b = full()
                o = dst[:, 0:4, t * P:(t + 1) * P]
                if shifts is None:
                    mul(o, by4(b), spread(gains[:, 0:4]), None, [s[sig], s["free_v"]])
                else:
                    mul(o, by4(b), spread(gains[:, 0:4]), None, [s["free_v"]])
                    add(o, o, spread(shifts[:, 0:4]), None, [s[sig]])

            for t in range(NT):
                if t == 0:
                    dve.wait_ge(s["ld_x"], 64)
                squares(xt[:, t, :], ss[:, t:t + 1], jA)
            inv_root(ss[:, 0:NT], DM)
            for t in range(NT):
                scale(xt[:, t, :], xt[:, t, :], ss[:, t:t + 1], s["xn_ready"])
            L.need(s["cols_ready"], 2)
            for t in range(NT):
                turned(hT, t, cols[:, V_PRE:V_PRE + 8], None, "hT_ready")
            for t in range(NT):
                b = full()
                L.did(V.tensor_copy(gb[:, t, :], b[:, 0:32]), s["free_v"])
            dve.wait_ge(s["ld_rope"], 16)
            dve.wait_ge(s["ld_qkn"], 32)
            for t in range(NT):
                dve.wait_ge(s["atok_ready"], 17 + t)
                v = atok[:, t, 0:1280].rearrange("p (h n) -> p h n", h=10)
                mul(sqA, v, v)
                L.did(V.tensor_reduce(ss[:, 16:26], sqA, AXX, ALU.add))
                inv_root(ss[:, 16:26], HD)
                mul(v, v, spread(ss[:, 16:26]))
                mul(v[:, 0:8, :], v[:, 0:8, :], over(qkn[:, 0, :], 8))
                mul(v[:, 8:10, :], v[:, 8:10, :], over(qkn[:, 1, :], 2))
                pr = atok[:, t, 0:1280].rearrange("p (h n two) -> p h n two", h=10, two=2)
                x0, x1_ = pr[:, :, :, 0], pr[:, :, :, 1]
                cos, sin = over(rope[:, t, 0, :], 10), over(rope[:, t, 1, :], 10)
                sq4 = sqA.rearrange("p h (u n) -> p u h n", u=2)
                mul(rt[:, 0], x0, cos)
                mul(rt[:, 1], x1_, sin)
                mul(sq4[:, 0], x0, sin)
                mul(sq4[:, 1], x1_, cos)
                L.did(V.tensor_tensor(x0, rt[:, 0], rt[:, 1], ALU.subtract))
                add(x1_, sq4[:, 0], sq4[:, 1], s["rope_ready"])
            for i in range(NH * NT + 1):
                if i < NH * NT:
                    dve.wait_ge(s["full_s"], score_job[i] + 1)
                    c = small[:, 64 + i:65 + i]
                    L.did(V.tensor_reduce(c, pss[:, score_job[i] % 4, :], AXX, ALU.max))
                    scale(c, c, -HD ** -0.5, s["negmax_ready"])
                if i >= 1:
                    j = i - 1
                    L.need(s["probs_ready"])
                    r = small[:, 96 + j:97 + j]
                    L.did(V.reciprocal(r, r))
                    scale(pb[:, j % 3, :], pb[:, j % 3, :], r, s["probsn_ready"])
            ntmp = [0]

            def tmp_of(tmp):
                L.need(s["tmp_ready"])
                ntmp[0] += 1
                return tmp[:, (ntmp[0] - 1) % 2, :]

            for j in range(KC):
                L.need(s["oT_ready"])
                L.need(s["silu_z"])
                mul(oT[:, j, :], oT[:, j, :], azs[:, j, :], s["oz_ready"])
            for j in range(KC):
                b = full()
                mul(mixT[:, j, :], b, tmp_of(tmpA), s["tmp_used"], [s["free_v"]])
            phase(1)

            gz = [gbuf[:, k, :, :] for k in range(8)]
            dve.wait_ge(s["ld_gpar"], 32)
            add(gz[5], gb[:, :, 16:32], over(gpar[:, 1, :], NT))
            L.did(V.scalar_tensor_tensor(gz[6], gz[5], -1.0, gz[5], ALU.mult, ALU.max))
            scale(gz[6], gz[6], -1.0, s["ga_step"])
            L.need(s["ga_ready"], 3)
            L.did(V.scalar_tensor_tensor(gz[5], gz[5], 0.0, gz[6], ALU.max, ALU.add))
            L.did(V.scalar_tensor_tensor(gz[0], gz[5], -1.0, over(gpar[:, 2, :], NT), ALU.mult, ALU.mult),
                  s["gg_ready"])
            b = full()
            L.did(V.tensor_copy(gz[1], b[:, 0:64].rearrange("p (t n) -> p t n", t=NT)), s["gG_ready"],
                  [s["free_v"]])
            L.need(s["ga_ready"])
            mul(gz[4], gz[3], gz[2])
            for j in range(24):
                b = full()
                if j >= 2:
                    dve.wait_ge(s["silu_ready"], j - 1)
                o = conv[:, j % 2, :]
                taps = [ccols[:, k * 24 + j:k * 24 + j + 1] for k in range(CONV_K)]
                scale(o, b, taps[2])
                for k in (0, 1, 3, 4):
                    m = k - 2
                    lo, hi = max(0, -m), SEQ - max(0, m)
                    L.did(V.scalar_tensor_tensor(o[:, lo:hi], b[:, lo + m:hi + m], taps[k], o[:, lo:hi],
                                                 ALU.mult, ALU.add),
                          s["conv_ready"] if k == 4 else None, [s["free_v"]] if k == 4 else [])
                n = j - (SUM_LAG + 1)
                if 0 <= n < 16:
                    L.need(s["rt_ready"])
                    r = crt[:, n % 2, :]
                    L.did(V.reciprocal(r, r))
                    v = qT[:, n, :] if n < 8 else kT[:, n - 8, :]
                    mul(v, v, r, s["norm_ready"])
            phase(2)

            def decay_rows(n):
                st, hg = PAIRS[n]
                for d in range(2):
                    g, t = buffers(n, d), tile_of(d, st)
                    L.need(s["e_ready", d])
                    x = g[C_X]
                    L.did(V.tensor_tensor(x, x, spread(gbuf[:, 1, t, hcols(d, hg)]), ALU.subtract))
                    L.did(V.tensor_scalar(g[C_D1], x, 0.0, None, ALU.max))
                    L.did(V.tensor_scalar(x, x, 0.0, None, ALU.min), s["x_ready", d])

            def key_products(n):
                st, hg = PAIRS[n]
                for d in range(2):
                    g, t = buffers(n, d), tile_of(d, st)
                    L.need(s["d1_ready", d])
                    b = full()
                    mul(g[C_D1], by4(b), g[C_D1], s["free_v"])
                    mul(g[C_D1], g[C_D1], spread(gbuf[:, 3, t, hcols(d, hg)]), s["l_ready", d])
                    L.need(s["d2_ready", d])
                    last = P - 1 if d == 0 else 0
                    L.did(V.tensor_copy(kcol[:, n % 2, d, :], g[C_X][:, :, last]))
                    b = full()
                    mul(g[C_X], by4(b), g[C_X], s["at_pre", d], [s["free_v"]])

            decay_rows(0)
            key_products(0)
            for n, (st, hg) in enumerate(PAIRS):
                for d in range(2):
                    g = buffers(n, d)
                    dve.wait_ge(s["c_ready", d], n * LEVELS + 1)
                    b = full()
                    L.did(V.tensor_tensor(g[C_TT], over(ident, 4), by4(b), ALU.subtract), s["tt_ready", d],
                          [s["free_v"]])
                    L.did(V.tensor_tensor(g[C_T], over(ident, 4), g[C_C0], ALU.subtract), s["t_ready", d])
                for k in range(1, LEVELS):
                    for d in range(2):
                        g = buffers(n, d)
                        b = full()
                        L.did(V.tensor_tensor(g[C_TT], g[C_TT], by4(b), ALU.subtract), s["tt_ready", d],
                              [s["free_v"]])
                        if k < LEVELS - 1:
                            b = full()
                            L.did(V.tensor_tensor(g[C_T], g[C_T], by4(b), ALU.subtract), s["t_ready", d],
                                  [s["free_v"]])
                if n + 1 < len(PAIRS):
                    decay_rows(n + 1)
                for d in range(2):
                    b = full()
                    L.did(V.tensor_copy(buffers(n, d)[C_VN], by4(b)), s["vn_ready", d], [s["free_v"]])
                if n + 1 < len(PAIRS):
                    key_products(n + 1)
                for d in range(2):
                    t = tile_of(d, st)
                    o = oacc[:, t, hg * 4:hg * 4 + 4, :]
                    b = full()
                    if st < NT // 2:
                        L.did(V.tensor_copy(o, by4(b)), s["free_v"])
                    else:
                        add(o, o, by4(b), s["free_v"])
                for d in range(2):
                    L.need(s["glast_ready", d])
                    b = full()
                    if st == 0:
                        L.did(V.tensor_copy(state[:, d, hg * 4:hg * 4 + 4, :], by4(b)), s["group_done", d],
                              [s["free_v"]])
                    else:
                        for h in range(4):
                            v = state[:, d, hg * 4 + h, :]
                            L.did(V.scalar_tensor_tensor(v, v, glast[:, n % 2, d, h:h + 1],
                                                         b[:, h * P:(h + 1) * P], ALU.mult, ALU.add),
                                  s["group_done", d] if h == 3 else None, [s["free_v"]] if h == 3 else [])
            phase(3)

            for t in range(NT):
                j8 = junk.rearrange("p (h n) -> p h n", h=8)
                mul(j8, oacc[:, t], oacc[:, t])
                L.did(V.tensor_reduce(ss[:, t * 8:t * 8 + 8], j8, AXX, ALU.add))
            inv_root(ss[:, 0:32], HD)
            for t in range(NT):
                mul(oacc[:, t], oacc[:, t], spread(ss[:, t * 8:t * 8 + 8]), s["on_ready"])
            for t in range(NT):
                for h0 in (0, 4):
                    b = full()
                    scale(onT[:, h0:h0 + 4, t * P:(t + 1) * P], by4(b), cols[:, V_DN:V_DN + 1], s["free_v"])
            for j in range(KC):
                mul(onT[:, j, :], onT[:, j, :], tmp_of(tmpB), s["dz_ready"], [s["tmp_used"]])
            for j in range(KC):
                tmp = tmp_of(tmpB)
                b = full()
                mul(tmp, b, tmp, s["free_v"])
                add(mixT[:, j, :], mixT[:, j, :], tmp, s["mixT_ready"], [s["tmp_used"]])

            def normed(v, row, x, sig, also=()):
                for t in range(NT):
                    squares(v[:, t, :], ss[:, t:t + 1], junk)
                inv_root(ss[:, 0:NT], DM)
                for t in range(NT):
                    L.did(V.scalar_tensor_tensor(v[:, t, :], v[:, t, :], ss[:, t:t + 1], row, ALU.mult, ALU.mult))
                    add(x[:, t, :], x[:, t, :], v[:, t, :], *sig)

            for t in range(NT):
                b = full()
                L.did(V.tensor_copy(pinT[:, :, t * P:(t + 1) * P], b[:, 0:256].rearrange("p (c n) -> p c n", c=2)),
                      s["pinT_ready"], [s["free_v"]])
            L.need(s["mo_ready"], 16)
            dve.wait_ge(s["ld_rows"], 32)
            dve.wait_ge(s["ld_res"], 64)
            normed(mo, rowv, x1, [s["x1_ready"]])
            for t in range(NT):
                b = full()
                L.did(V.tensor_copy(x1T[:, 0:4, t * P:(t + 1) * P], by4(b)), None, [s["x1T_ready"], s["free_v"]])
            L.need(s["sg_ready"], 16)
            for t in range(NT):
                for c0 in (0, 512):
                    b = full()
                    mul(mo[:, t, c0:c0 + 512], b, sg[:, t, c0:c0 + 512], s["free_v"])
            normed(mo, rowv2, x1, [])
            L.need(s["mod_ready"], 24)
            add(mod[:, :, :], mod[:, :, :], cols[:, V_BADA:V_BADA + 48].unsqueeze(2).broadcast_to([P, 48, 2]))
            for n, (c0, k, vn) in enumerate(((8, 0, V_N1), (8, 1, V_N1), (32, 0, V_N2))):
                L.did(V.scalar_tensor_tensor(gain[:, n * 8:n * 8 + 8], mod[:, c0:c0 + 8, k], 1.0,
                                             cols[:, vn:vn + 8], ALU.add, ALU.mult))
            phase(4)

            for t in range(NT):
                squares(x1[:, t, :], ss[:, t:t + 1], jc)
            inv_root(ss[:, 0:NT], DM)
            for t in range(NT):
                scale(xn[:, t, :], x1[:, t, :], ss[:, t:t + 1], s["x2_ready"])
            for t in range(NT):
                turned(h2T, t, gain[:, 0:8], mod[:, 0:8, 0], "h2_ready")
            dve.wait_ge(s["ld_ctx"], 32)
            for t in range(NTC):
                squares(ctxt[:, t, :], ss[:, t:t + 1], jc)
            inv_root(ss[:, 0:NTC], DM)
            for t in range(NTC):
                scale(ctxt[:, t, :], ctxt[:, t, :], ss[:, t:t + 1], s["x2_ready"])
            for t in range(NTC):
                turned(hcT, t, gain[:, 8:16], mod[:, 0:8, 1], "hc_ready")
            for b2 in range(2):
                for t in range(NT + NTC):
                    b = full()
                    L.did(V.tensor_copy(v2[:, t, b2 * 256:(b2 + 1) * 256], b[:, 0:256]), s["free_v"])
            for d in range(2):
                for c0, n in ((0, SEQ), (SEQ, CTX)):
                    b = full()
                    L.did(V.tensor_copy(a2T[0:RANK, d, c0:c0 + n], b[0:RANK, 0:n]), s["a2_ready"], [s["free_v"]])
            for b2 in range(2):
                for t in range(NT):
                    b = full()
                    L.did(V.tensor_copy(p2[:, t, b2 * 256:(b2 + 1) * 256], b[:, 0:256]), s["p2_ready"],
                          [s["free_v"]])
            for g in range(4):
                b = full()
                if g >= 2:
                    dve.wait_ge(s["cat_ready"], g - 1)
                L.did(V.tensor_copy(pmT[:, g % 2, :], b), s["mT_ready"], [s["free_v"]])
            phase(5)

            for t in range(NT + NTC):
                L.need(s["z_ready"])
                z, y = z2[:, t % 2, :], z3[:, t % 2, :]
                L.did(V.scalar_tensor_tensor(y, z, -1.0, z, ALU.mult, ALU.max), s["absz_ready"])
                L.need(s["lz_ready"])
                L.did(V.scalar_tensor_tensor(z, z, 0.0, y, ALU.min, ALU.subtract))
                scale(la[:, t, :], z, 1.0 / 16.0, s["la_ready"])
            for n in range(4):
                d, m2 = divmod(n, 2)
                L.need(s["bexp_ready"], 2)
                mul(qb[:, d, m2, :], q2T[:, m2, :], eb[:, n % 2, :])
                mul(kb[:, d, m2, :], k2T[:, m2, :], enb[:, n % 2, :], s["qb_ready"])
            for t in range(NT + NTC):
                L.need(s["kexp_ready"])
                kv = kst[:, t, :].rearrange("p (d n) -> p d n", d=2)
                mul(kv, kv, k2[:, t, :].unsqueeze(1).broadcast_to([P, 2, 256]), s["kst_ready"])
            L.did(V.memset(swork[:, 0, :, :, :], 0.0))
            for n in range(12):
                for d in range(2):
                    b = full()
                    c = chunk_col(d, n)
                    for m2 in range(2):
                        src = state_at(d, m2, n)
                        dst = state_at(d, m2, n + 1)
                        if dst is None:
                            continue
                        for hh in range(2):
                            hp = slice(hh * 64, hh * 64 + 64)
                            L.did(V.scalar_tensor_tensor(dst[hp, :], src[hp, :], dec2[hp, d, m2, c:c + 1],
                                                         b[hp, m2 * 256 + hh * P:m2 * 256 + (hh + 1) * P],
                                                         ALU.mult, ALU.add))
                    L.raise_(s["free_v"])
            L.raise_(s["sprev_ready"])
            for h in range(H2):
                for d in range(2):
                    b = full()
                    mul(by4(scm[:, (h % 2) * 2 + d, :]), by4(b), over(blk[d], 4), s["sc_ready"], [s["free_v"]])
                L.need(s["rt2_ready"], 2)
                r = enb[:, h % 2, :]
                L.did(V.reciprocal(r, r))
                mul(r, r, catT[:, h, :])
                L.did(V.scalar_tensor_tensor(catT[:, h, :], r, cols[:, V_GLA:V_GLA + 1], g2T[:, h, :],
                                             ALU.mult, ALU.mult), s["o2_ready"], [s["cat_ready"]])
            for c0 in (0, 512):
                b = full()
                L.did(V.tensor_copy(gtrow[:, c0:c0 + 512], b), s["free_v"])
            tmp = scm[:, 0, 0:WC]
            for b2 in range(4):
                cs = slice(b2 * WC, (b2 + 1) * WC)
                for t in range(NT):
                    b = full()
                    mul(tmp, b[:, 0:WC], gtrow[:, cs], s["free_v"])
                    add(x1[:, t, cs], x1[:, t, cs], tmp)
            phase(6)

            L.did(V.memset(zero, 0.0))
            for t in range(NT):
                squares(x3[:, t, :], ss[:, t:t + 1], jr)
            inv_root(ss[:, 0:NT], DM)
            for t in range(NT):
                scale(xn[:, t, :], x3[:, t, :], ss[:, t:t + 1], s["x3_ready"])
            for t in range(NT):
                turned(h3T, t, gain[:, 16:24], mod[:, 24:32, 0], "h3_ready")
            iota = const[:, C_IOTA:C_IOTA + NE]
            rev = const[:, C_REV:C_REV + EPG]
            scale(rthr, iota[:, 1:ROUNDS], float(CAP))

            def along(v, m):
                return v.unsqueeze(2).broadcast_to([P, v.shape[1], m])

            def first_largest(hot, at_, v, most, tmp):
                n = v.shape[2]
                L.did(V.tensor_reduce(most, v, AXX, ALU.max))
                L.did(V.tensor_tensor(tmp, v, along(most, n), ALU.is_ge))
                mul(tmp, tmp, over(rev[:, 0:n], NT))
                L.did(V.tensor_reduce(at_, tmp, AXX, ALU.max))
                L.did(V.tensor_tensor(hot, tmp, along(at_, n), ALU.is_ge))

            b = full()
            L.did(V.tensor_copy(lg, b[:, 0:NT * 36].rearrange("p (t n) -> p t n", t=NT)), s["free_v"])
            gmax, gat, e1, e2, at1, at2, den, ids = [rcol[:, k, :] for k in range(8)]
            ghot = rgrp[:, 1]
            first_largest(ghot, gat, lg[:, :, 0:NG], gmax, rgrp[:, 0])
            ghot_e = ghot.unsqueeze(3).broadcast_to([P, NT, NG, EPG])
            by_group = rexp.rearrange("p t (g e) -> p t g e", g=NG)
            mul(by_group, lg[:, :, 4:36].rearrange("p t (g e) -> p t g e", g=NG), ghot_e)
            L.did(V.tensor_reduce(rin, rexp.rearrange("p t (g e) -> p t e g", g=NG), AXX, ALU.add))
            first_largest(rhot[:, 0], at1, rin, e1, rtmp)
            L.did(V.scalar_tensor_tensor(rin, rhot[:, 0], -1e30, rin, ALU.mult, ALU.add))
            first_largest(rhot[:, 1], at2, rin, e2, rtmp)
            L.did(V.tensor_tensor(lexp[:, :, 0:NG], lg[:, :, 0:NG], along(gmax, NG), ALU.subtract))
            L.did(V.tensor_tensor(lexp[:, :, NG], e2, e1, ALU.subtract), s["lg_ready"])
            for k in range(2):
                o = pick[:, :, k, :].rearrange("p t (g e) -> p t g e", g=NG)
                mul(o, ghot_e, rhot[:, k].unsqueeze(2).broadcast_to([P, NT, NG, EPG]))
            add(picked, pick[:, :, 0, :], pick[:, :, 1, :], s["picked_ready"])
            scale(ids, gat, float(-EPG))
            for k, a_ in enumerate((at1, at2)):
                L.did(V.tensor_tensor(eid[:, :, k], ids, a_, ALU.subtract))
            L.did(V.tensor_scalar(eid, eid, float(EPG * EPG + EPG), None, ALU.add))
            L.need(s["lexp_ready"])
            e = lexp[:, :, NG]
            L.did(V.tensor_reduce(den, lexp[:, :, 0:NG], AXX, ALU.add))
            L.did(V.scalar_tensor_tensor(den, e, 1.0, den, ALU.add, ALU.mult))
            L.did(V.reciprocal(ewt[:, :, 0], den))
            mul(ewt[:, :, 1], ewt[:, :, 0], e)
            for c0 in (0, 512):
                b = full()
                L.did(V.tensor_copy(rowg[:, c0:c0 + 512], b), s["free_v"])
            b = full()
            place = b[:, 0:NT * NE].rearrange("p (t n) -> p t n", t=NT).unsqueeze(2).broadcast_to([P, NT, 2, NE])
            mul(rplace, pick, place)
            rnd, slf = tround.rearrange("p t k -> p (t k)"), slot_f.rearrange("p t k -> p (t k)")
            L.did(V.tensor_reduce(slot_f, rplace, AXX, ALU.add))
            L.did(V.tensor_tensor(rpast, along(slf, ROUNDS - 1), over(rthr, 2 * NT), ALU.is_ge))
            L.did(V.tensor_reduce(rnd, rpast, AXX, ALU.add))
            L.did(V.scalar_tensor_tensor(slf, rnd, float((NE - 1) * CAP), slf, ALU.mult, ALU.add))
            L.did(V.scalar_tensor_tensor(slot_f, eid, float(CAP), slot_f, ALU.mult, ALU.add))
            L.did(V.tensor_copy(slot_u, slf), s["slots_ready"])
            L.did(V.tensor_reduce(tmax[:, 2:3], b[:, NT * NE:(NT + 1) * NE], AXX, ALU.max), s["free_v"])
            L.did(V.tensor_scalar(tmax[:, 8:8 + ROUNDS], iota[:, 0:ROUNDS], float(CAP), tmax[:, 2:3], ALU.mult, ALU.is_lt))
            L.did(V.tensor_reduce(tmax[:, 3:4], tmax[:, 8:8 + ROUNDS], AXX, ALU.add))
            L.did(V.tensor_copy(turns_u[:, 0:1], tmax[:, 3:4]), s["turns_ready"])
            L.did(V.memset(index[:, ROUNDS * NE:], 0))
            for r in range(ROUNDS):
                o = back_f[:, r, :]
                L.did(V.tensor_scalar(o, slf, float(-NE * CAP * (r + 1)), None, ALU.add))
                L.did(V.scalar_tensor_tensor(o, rnd, float(r), o, ALU.is_equal, ALU.mult))
                L.did(V.tensor_scalar(o, o, float(NE * CAP), None, ALU.add))
            L.did(V.tensor_copy(back_u, back_f))
            dve.wait_ge(s["xn_saved"], 16 * NT)
            L.did(V.memset(yacc, 0.0))
            b = full()
            L.did(V.tensor_copy(index[0:CAP, 0:ROUNDS * NE], b[0:CAP, 0:ROUNDS * NE]), s["index_ready"],
                  [s["free_v"]])

            def to_xe(b, k):
                o = xe[:, k, :, :]
                L.did(V.tensor_tensor(o, b.rearrange("p (c n) -> p c n", c=KC), spread(gain[:, 16:24], CAP),
                                      ALU.mult), s["free_v"])
                add(o, o, spread(mod[:, 24:32, 0], CAP), s["xe_ready"])

            to_xe(full(), 0)
            L.raise_(s["sil_used"], 2)
            q0 = seen[0]
            rounds = rounds_of(dve)
            dve.sem_inc(s["combined"])
            with dve.Fori(0, rounds) as r:
                with dve.Fori(0, NE // XPT) as ir:
                    i = r * (NE // XPT) + ir
                    L.enter(i, {s["hid_ready"]: XPT, s["free_v"]: 3 * XPT, s["sil_used"]: XPT, s["xe_ready"]: XPT,
                                s["y1_ready"]: XPT},
                            {s["full_v"]: 3 * XPT, s["sil_ready"]: XPT})
                    for q in range(XPT):
                        k = q % 2
                        L.need(s["sil_ready"])
                        L.need(s["full_v"])
                        L.did(V.tensor_tensor(hid[:, k, :], psv[:, (q0 + 3 * q) % 4, 0:2 * CAP], sil[:, k, :], ALU.mult),
                              s["hid_ready"], [s["free_v"], s["sil_used"]])
                        L.need(s["full_v"])
                        to_xe(psv[:, (q0 + 3 * q + 1) % 4, :], 1 - k)
                        L.need(s["full_v"])
                        dve.wait_ge(s[f"st_y{k}"], (i * (XPT // 2) + (q // 2 + 1)) * 16)
                        L.did(V.tensor_copy(yb[0:CAP, k, 512:DM], psv[0:CAP, (q0 + 3 * q + 2) % 4, :]), s["y1_ready"],
                              [s["free_v"]])
                    L.leave(0)
                dve.wait_ge(s["ygat_ready"], r * (32 * NT) + 32 * NT)
                for t in range(NT):
                    for k in range(2):
                        ins = V.scalar_tensor_tensor(yacc[:, t, :], ygat[:, k, t, :], ewt[:, t, k:k + 1],
                                                     yacc[:, t, :], ALU.mult, ALU.add)
                        ins.then_inc(s["yacc_ready"], 1)
                        dve.wait_ge(s["yacc_ready"], r * (2 * NT) + (2 * t + k + 1))
                dve.sem_inc(s["combined"])
            for t in range(NT):
                mul(yacc[:, t, :], yacc[:, t, :], rowg)
                add(x3[:, t, :], x3[:, t, :], yacc[:, t, :])
                squares(x3[:, t, :], ss[:, t:t + 1], jr)
            inv_root(ss[:, 0:NT], DM)
            dve.wait_ge(s["ld_rowf"], 16)
            for t in range(NT):
                L.did(V.scalar_tensor_tensor(x3[:, t, :], x3[:, t, :], ss[:, t:t + 1], rowf, ALU.mult, ALU.mult),
                      s["out_ready"])


_OUT = (1, SEQ, DM)
DUMP = []


def kernel(**inputs):
    import concourse.bacc as bacc
    from concourse.bass_utils import run_bass_kernel_spmd

    nc = bacc.Bacc("TRN2", target_bir_lowering=False, num_devices=1)
    masks, rope, pool = shape_constants()
    arrays = {n: np.ascontiguousarray(v) for n, v in inputs.items()}
    arrays |= {"c_masks": masks, "c_rope": rope, "c_pool": pool}
    a = {n: nc.dram_tensor(n, v.shape, F32, kind="ExternalInput").ap() for n, v in arrays.items()}
    out = nc.dram_tensor("out", _OUT, F32, kind="ExternalOutput").ap()
    build(nc, a, out, [])
    r = run_bass_kernel_spmd(nc, [arrays], core_ids=[0])
    return r.results[0]["out"]
```

```python
from contextlib import ExitStack

import numpy as np

import concourse.bass as bass
from concourse import mybir

F32 = mybir.dt.float32
U32 = mybir.dt.uint32
ALU = mybir.AluOpType
ACT = mybir.ActivationFunctionType
AXX = mybir.AxisListType.X

P = 128
SEQ, DM = 512, 1024
NT = SEQ // P
KC = DM // P
EPS = 1e-6
HD = 128
NH, NKV = 8, 2
GRID_W = 64
ROPE_THETA = 10000.0
CONV_K = 5
PLE = 256
CTX = 256
NTC = CTX // P
CH2 = 64
H2, DK2, DV2 = 4, 64, 128
RANK = 16
GATE_NORM = 16.0
WINDOWS = (2, 4, 8, 16)
NE, NG, EPG, DE = 32, 4, 8, 256
CAP = 64
ROUNDS = SEQ // CAP
XPT = 4
O_AQ, O_AK, O_AV, O_AZ = 0, 1024, 1280, 1536
O_DQ, O_DB, O_DZ, O_GA, O_GD = 2560, 5632, 5664, 6688, 7712
O2_Q, O2_K, O2_V, O2_G, O2_A, O2_P = 0, 256, 512, 1024, 1536, 1568
WC = 256
LEVELS = 7

C_ID, C_ONE, C_LE, C_GE = 0, 128, 256, 384
C_LV = 512
C_BLE = C_LV + 2 * LEVELS * P
C_BGE, C_BGT, C_BLT = C_BLE + P, C_BLE + 2 * P, C_BLE + 3 * P
C_EPS = C_BLE + 4 * P
C_IOTA = C_EPS + 4
C_TOK = C_IOTA + CAP
C_LT = C_TOK + NT
C_REV = C_LT + P
C_N = C_REV + EPG
V_PRE, V_DN, V_N1, V_N2, V_GLA, V_PS, V_BADA, V_C, V_CC = 0, 8, 9, 17, 25, 26, 30, 78, 86
V_N = 94


def shape_constants():
    i = np.arange(P)
    p, f = i[:, None], i[None, :]
    c = np.zeros((P, C_N), np.float32)
    c[:, C_ID:C_ID + P] = p == f
    c[:, C_ONE:C_ONE + P] = 1.0
    c[:, C_LE:C_LE + P] = p <= f
    c[:, C_GE:C_GE + P] = p >= f
    for k in range(LEVELS):
        b = 1 << k
        off = (p // (2 * b) == f // (2 * b)) & (p // b != f // b)
        c[:, C_LV + k * P:C_LV + (k + 1) * P] = off & (p > f)
        c[:, C_LV + (LEVELS + k) * P:C_LV + (LEVELS + k + 1) * P] = off & (p < f)
    same = p // CH2 == f // CH2
    c[:, C_BLE:C_BLE + P] = same & (p <= f)
    c[:, C_BGE:C_BGE + P] = same & (p >= f)
    c[:, C_BGT:C_BGT + P] = same & (p > f)
    c[:, C_BLT:C_BLT + P] = same & (p < f)
    c[:, C_EPS] = EPS
    c[:, C_EPS + 1] = HD * EPS
    c[:, C_EPS + 2] = 1.0
    c[:, C_IOTA:C_IOTA + CAP] = np.arange(CAP)
    c[:, C_TOK:C_TOK + NT] = p + P * np.arange(NT)
    c[:, C_LT:C_LT + P] = p < f
    c[:, C_REV:C_REV + EPG] = EPG - np.arange(EPG)
    nf = HD // 4
    inv = (np.float32(ROPE_THETA) ** (-np.arange(nf, dtype=np.float32) / np.float32(nf))).astype(np.float32)
    t = np.arange(SEQ)
    ang = np.concatenate([(t // GRID_W).astype(np.float32)[:, None] * inv,
                          (t % GRID_W).astype(np.float32)[:, None] * inv], axis=1)
    rope = np.stack([np.cos(ang), np.sin(ang)], axis=1).astype(np.float32)
    rope = np.ascontiguousarray(rope.reshape(NT, P, 2, HD // 2).transpose(1, 0, 2, 3))

    def mean(n, w):
        m = np.zeros((n, n))
        lo = w // 2
        hi = w - 1 - lo
        for a in range(n):
            s, e = max(0, a - lo), min(n, a + hi + 1)
            m[a, s:e] = 1.0 / (e - s)
        return m

    pool = np.zeros((len(WINDOWS), SEQ, SEQ))
    for g, w in enumerate(WINDOWS):
        pool[g] = (np.kron(mean(SEQ // GRID_W, w), mean(GRID_W, w)) - np.eye(SEQ)).T
    pool = pool.astype(np.float32).reshape(len(WINDOWS), NT, P, SEQ).transpose(2, 0, 1, 3)
    return c, rope, np.ascontiguousarray(pool)


class Lane:

    def __init__(self, eng, chain):
        self.eng, self.chain = eng, chain
        self.raised, self.followed = {}, {}
        self.i, self.per, self.at = None, {}, None

    def value(self, table, sem):
        n = table[sem]
        if self.i is None or not self.per.get((id(table), sem), 0):
            return n
        return self.i * self.per[(id(table), sem)] + n

    def did(self, ins, sem=None, also=()):
        sem = self.chain if sem is None else sem
        ins.then_inc(sem, 1)
        self.raised[sem] = self.raised.get(sem, 0) + 1
        self.eng.wait_ge(sem, self.value(self.raised, sem))
        for s in also:
            self.raise_(s)

    def raise_(self, sem, n=1):
        self.raised[sem] = self.raised.get(sem, 0) + n
        self.eng.sem_inc(sem, n)

    def need(self, sem, n=1):
        self.followed[sem] = self.followed.get(sem, 0) + n
        self.eng.wait_ge(sem, self.value(self.followed, sem))

    def enter(self, i, raised, followed):
        self.i = i
        self.per = {}
        for s, n in raised.items():
            self.raised.setdefault(s, 0)
            self.per[(id(self.raised), s)] = n
        for s, n in followed.items():
            self.followed.setdefault(s, 0)
            self.per[(id(self.followed), s)] = n
        self.at = (dict(self.raised), dict(self.followed))

    def leave(self, turns):
        for table, before in ((self.raised, self.at[0]), (self.followed, self.at[1])):
            for s in table:
                per = self.per.get((id(table), s), 0)
                assert table[s] - before.get(s, 0) == per, (s, table[s] - before.get(s, 0), per)
                table[s] = before.get(s, 0) + turns * per
        self.i, self.per = None, {}


def build(nc, a, out, dumps):
    ctx = ExitStack()
    with ctx:
        def sb(name, *shape):
            return ctx.enter_context(nc.sbuf_tensor(name, [P, *shape], F32))

        def sem(name):
            return ctx.enter_context(nc.semaphore(name))

        const = sb("const", C_N)
        ident = const[:, C_ID:C_ID + P]
        ones = const[:, C_ONE:C_ONE + P]
        tri = [const[:, C_LE:C_LE + P], const[:, C_GE:C_GE + P]]
        blk = [const[:, C_BLE:C_BLE + P], const[:, C_BGE:C_BGE + P]]
        blk_rest = [const[:, C_BGT:C_BGT + P], const[:, C_BLT:C_BLT + P]]
        eps = const[:, C_EPS:C_EPS + 1]
        eps128 = const[:, C_EPS + 1:C_EPS + 2]
        one = const[:, C_EPS + 2:C_EPS + 3]
        wslot01 = sb("wslot01", 2, KC * WC)
        cols = sb("cols", V_N)
        ccols = sb("ccols", CONV_K * 24)
        csilu = sb("csilu", KC, 2)
        mod = sb("mod", 48, 2)
        small = sb("small", 3 * 64)
        ss = small[:, 0:64]
        gb = sb("gb", NT, 32)
        gain = sb("gain", 3 * KC)
        gpar = sb("gpar", 3, 16)
        arow = sb("arow", 2, WC)
        wrt = sb("wrt", KC, NG + NE)
        kcol = sb("kcol", 2, 2, 4)

        ARENA = 44100
        arena = sb("arena", ARENA)
        top = [0]

        def at(off, *shape):
            n = int(np.prod(shape))
            assert off + n <= ARENA, (off, n)
            top[0] = off + n
            v = arena[:, off:off + n]
            if len(shape) == 1:
                return v
            names = "abcde"[:len(shape)]
            return v.rearrange(f"p ({' '.join(names)}) -> p {' '.join(names)}",
                               **{k: s for k, s in zip(names[1:], shape[1:])})

        K = 256
        hT = at(0, KC, SEQ)
        mixT = at(16 * K, KC, SEQ)
        B = 32 * K
        xt = at(B, NT, DM)
        oT = at(B, KC, SEQ)
        atok = at(B + 16 * K, NT, 1536)
        qkT = at(B + 40 * K, 10, SEQ)
        rt = at(B + 60 * K, 2, 10, HD // 2)
        rope = at(top[0], NT, 2, HD // 2)
        azs = at(B + 106 * K, KC, SEQ)
        assert top[0] <= ARENA - 2 * KC * WC
        qkn = at(B + 67 * K, 2, HD)
        pb = at(top[0], 3, SEQ)
        pT = at(top[0], 2, NT, SEQ)
        tmpA = at(top[0], 2, SEQ)
        vecs = at(top[0], P)
        cvecs = at(top[0], P)
        sqA = at(top[0], 10, HD)
        jA = at(top[0], DM)
        assert top[0] <= B + 106 * K, top[0] / K
        qT = at(B, NH, SEQ)
        kT = at(B + 16 * K, NH, SEQ)
        ktok = at(B + 32 * K, NT, NH, HD)
        vtok = at(B + 48 * K, NT, NH, HD)
        oacc = at(B + 64 * K, NT, NH, HD)
        state = at(B + 80 * K, 2, NH, HD)
        gbuf = at(top[0], 8, NT, 16)
        D = top[0]
        conv = at(D, 2, SEQ)
        cst = at(top[0], 2, SEQ)
        crt = at(top[0], 2, SEQ)
        csq = at(top[0], 2, SEQ)
        assert top[0] <= ARENA - 2 * KC * WC
        NB = 12
        grp = [[at(D + (d * NB + n) * 512, 4, P) for n in range(NB)] for d in range(2)]
        glast = at(D + 2 * NB * 512, 2, 2, 4)
        onT = at(B, KC, SEQ)
        mo = at(B + 16 * K, NT, DM)
        x1 = at(B + 32 * K, NT, DM)
        x1T = at(0, KC, SEQ)
        pin = at(B + 48 * K, NT, PLE)
        pinT = at(top[0], 2, SEQ)
        sg = at(B + 64 * K, NT, DM)
        et = at(B, NT, DM)
        hcT = at(16 * K, KC, CTX)
        ctxt = at(B + 56 * K, NTC, DM)
        rowv = at(B + 80 * K, DM)
        rowv2 = at(top[0], DM)
        tmpB = at(top[0], 2, SEQ)
        junk = at(top[0], DM)
        xn = at(B + 16 * K, NT, DM)
        h2T = at(0, KC, SEQ)
        q2T = at(B, 2, SEQ)
        k2T = at(B + 4 * K, 2, SEQ)
        g2T = at(B + 8 * K, H2, SEQ)
        catT = at(B + 16 * K, KC, SEQ)
        k2 = at(B + 48 * K, NT + NTC, 256)
        v2 = at(top[0], NT + NTC, 512)
        p2 = at(top[0], NT, 512)
        a2T = at(top[0], 2, SEQ + CTX)
        wdec = at(top[0], 2, 256)
        bdec = at(top[0], 512)
        wpool = at(top[0], len(WINDOWS), P)
        gtrow = at(top[0], DM)
        la_at = top[0]
        la = at(top[0], NT + NTC, 512)
        G = top[0]
        pm = at(G, 2, NT, SEQ)
        pmT = at(top[0], 2, SEQ)
        top[0] = G + 2048
        kst_at = top[0]
        kst = at(top[0], NT + NTC, 512)
        eb = at(top[0], 2, SEQ)
        enb = at(top[0], 2, SEQ)
        dec2 = at(top[0], 2, 2, 12)
        swork = at(top[0], 2, 2, 2, P)
        qb = at(0, 2, 2, SEQ)
        kb = at(8 * K, 2, 2, SEQ)
        sprev = at(16 * K, 2, 2, 8, P)
        wo23 = [at(la_at, KC, WC), at(kst_at, KC, WC)]
        scm01, scm23 = at(G, 4, SEQ), at(B + 66 * K, 4, SEQ)
        scm = [scm01[:, n] for n in range(4)] + [scm23[:, n] for n in range(4)]
        zab = at(24 * K, 4, 512)
        zabs = [zab[:, n] for n in range(4)] + [at(B + 16 * K, 2, 512)[:, n] for n in range(2)]
        x3 = x1
        x3n = at(B, NT, DM)
        yacc = x3n
        h3T = h2T
        rowf = at(B + 16 * K, DM)
        rowg = at(B + 20 * K, DM)
        xg = at(16 * K, 2, DM)
        lg = at(16 * K, NT, 4 + NE)
        rgrp = at(top[0], 3, NT, NG)
        rexp = at(top[0], NT, NE)
        rin = at(top[0], NT, EPG)
        rhot = at(top[0], 2, NT, EPG)
        rtmp = at(top[0], NT, EPG)
        rcol = at(top[0], 8, NT)
        rplace = at(top[0], NT, 2, NE)
        rthr = at(top[0], ROUNDS - 1)
        rpast = at(top[0], 2 * NT, ROUNDS - 1)
        rround = at(top[0], 2 * NT, ROUNDS)
        rfirst = at(top[0], NT, 2)
        rplaced = at(top[0], 2 * NT, CAP)
        rtok = at(top[0], NT, 2, NE)
        before_t = at(top[0], NT + 1, NE)
        assert top[0] <= 24 * K
        xe = at(24 * K, 2, KC, CAP)
        sil = at(28 * K, 2, 2 * CAP)
        hid = at(29 * K, 2, 2 * CAP)
        yb = at(0, 2, DM)
        win01 = at(B + 48 * K, 2, KC, 2 * DE)
        wout01 = at(top[0], 2, 2, DM)
        lexp = at(top[0], NT, NG + 1)
        pick = at(top[0], NT, 2, NE)
        picked = at(top[0], NT, NE)
        ewt = at(top[0], NT, 2)
        eid = at(top[0], NT, 2)
        slot_f = at(top[0], NT, 2)
        tmax = at(top[0], 16)
        turns_u = at(top[0], 2).bitcast(U32)
        index = at(top[0], ROUNDS * NE + 4).bitcast(U32)
        icol = at(top[0], 2).bitcast(U32)
        zero = arow[:, 0, 0:P]
        ygat = at(top[0], 2, NT, DM)
        Y = top[0] - 2 * NT * DM
        after_ygat = top[0]
        tok_at = at(Y, NT, 2, ROUNDS, NE)
        win = [win01[:, 0], win01[:, 1], wslot01[:, :, :].rearrange("p a (c n) -> p (a c) n", n=2 * DE),
               at(Y, KC, 2 * DE)]
        wout = [wout01[:, 0], wout01[:, 1], at(top[0], 2, DM), at(top[0], 2, DM)]
        assert top[0] <= after_ygat
        top[0] = after_ygat
        back_f = at(top[0], ROUNDS, 2 * NT)
        back_u = at(top[0], ROUNDS, 2 * NT).bitcast(U32)
        bcol = at(top[0], 2 * NT).bitcast(U32)
        tround = at(top[0], NT, 2)

        def scratch(name, *shape):
            return nc.dram_tensor(name, list(shape), F32, kind="Internal").ap()

        xn_dram = scratch("xn_dram", SEQ, DM)
        y_dram = scratch("y_dram", NE * CAP + 1, DM)
        y_store = y_dram[0:NE * CAP, :].rearrange("(i q c) n -> i q c n", q=XPT, c=CAP)

        psv = ctx.enter_context(nc.psum_tensor("psv", [P, 4, 512], F32))
        pss = ctx.enter_context(nc.psum_tensor("pss", [P, 4, 512], F32))

        names = """chain_v chain_s chain_p phase full_v free_v full_s free_s w_used ld_const ld_vecs ld_x ld_rope
            ld_gpar ld_res ld_p ld_rows ld_ctx ld_small ld_rowf ld_wrt cols_ready silu_z xn_ready hT_ready
            rs_in rs_out atok_ready rope_ready qkT_ready negmax_ready probs_ready probsn_ready pT_ready
            oT_ready tmp_ready tmp_used oz_ready ga_ready ga_step gg_ready gG_ready conv_ready silu_ready
            half_ready row_ready sq_ready rt_ready norm_ready on_ready dz_ready mixT_ready mo_ready
            x1_ready x1T_ready pinT_ready sg_ready x2_ready mod_ready h2_ready hc_ready p2_ready mT_ready
            k2_ready a2_ready z_ready absz_ready lz_ready la_ready bexp_ready qb_ready kexp_ready kst_ready
            sprev_ready sc_ready o2_ready sq2_ready rt2_ready cat_ready x3_ready h3_ready lg_ready
            lexp_ready ld_out moe_used sil_ready hid_ready out_ready picked_ready icol_ready bcol_ready combined yacc_ready xn_saved zeros_saved
            table_ready index_ready xg_k0 xg_k1 xe_ready y1_ready st_y0 st_y1
            turns_ready sil_used pool_used""".split()
        s = {n: sem(n) for n in names}
        for n in ("e_ready glast_ready x_ready d1_ready d2_ready l_ready at_pre at_ready "
                  "c_ready t_ready tt_ready zz_ready kbe_ready kdec_ready qg_ready nwt_ready vn_ready "
                  "group_done").split():
            for d in range(2):
                s[n, d] = sem(f"{n}{d}")
        for k in range(4):
            s["ld_w", k] = sem(f"ld_w{k}")
            s["ld_expert", k] = sem(f"ld_expert{k}")
        for k in range(2):
            s["ld_pm", k] = sem(f"ld_pm{k}")
            s["ygat_ready", k] = sem(f"ygat_ready{k}")

        w1, w2 = a["w_in"][0], a["w_in_2"][0]
        weights, slot_group = [], []

        def stream(key, src, col, n):
            weights.append((key, src[:, col:col + n].rearrange("(c p) n -> p c n", p=P), src.shape[0] // P, n))

        for b in range(6):
            stream(("qkv", b), w1, O_AQ + b * WC, WC)
        stream("dbda", w1, O_DB, 32)
        for b in range(2):
            stream(("az", b), w1, O_AZ + b * WC, WC)
            for k in range(4 * b, 4 * b + 4):
                stream(("ada", k), a["w_ada_2"][0], k * WC, WC)
        for what, b in (("ada", 8), ("az", 2), ("ada", 9), ("ada", 10), ("az", 3), ("ada", 11)):
            if what == "ada":
                stream(("ada", b), a["w_ada_2"][0], b * WC, WC)
            else:
                stream(("az", b), w1, O_AZ + b * WC, WC)
        for b in range(4):
            stream(("bra", b), a["w_br_att"][0], b * WC, WC)
            stream(("ga", b), w1, O_GA + b * WC, WC)
        slot_group.append((len(weights), 4))
        for b in range(12):
            stream(("dqkv", b), w1, O_DQ + b * WC, WC)
        for b in range(12, 24):
            stream(("ada", b), a["w_ada_2"][0], b * WC, WC)
        slot_group.append((len(weights), 2))
        for b in range(4):
            stream(("dz", b), w1, O_DZ + b * WC, WC)
        for b in range(4):
            stream(("brd", b), a["w_br_dn"][0], b * WC, WC)
            stream(("gd", b), w1, O_GD + b * WC, WC)
        for b in range(4):
            stream(("wo", b), a["w_out"][0], b * WC, WC)
        stream("plep", a["w_ple_proj"][0], 0, DM)
        slot_group.append((len(weights), 4))
        for b in range(4):
            stream(("pleg", b), a["w_ple_gate"][0], b * WC, WC)
        slot_group.append((len(weights), 4))
        for key, col, n in (("k2", O2_K, 256), (("v2", 0), O2_V, 256), (("v2", 1), O2_V + 256, 256), ("q2", O2_Q, 256),
                            (("g2", 0), O2_G, 256), (("g2", 1), O2_G + 256, 256), ("a2", O2_A, 32),
                            (("p2", 0), O2_P, 256), (("p2", 1), O2_P + 256, 256)):
            stream(key, w2, col, n)
        for b in range(2):
            stream(("wo2", b), a["w_out_2"][0], b * WC, WC)

        slot_group.append((len(weights), 2))
        slot_of, before, turn_of, last = [], [], [], {}
        for end, many in slot_group:
            start = len(slot_of)
            for n in range(start, end):
                k = (n - start) % many
                slot_of.append(k)
                before.append(last.get(k, (-1, 0))[0])
                turn_of.append(last.get(k, (-1, 0))[1] + 1)
                last[k] = (n, turn_of[-1])
        wslot = [wslot01[:, 0, :], wslot01[:, 1, :], arena[:, ARENA - 2 * KC * WC:ARENA - KC * WC],
                 arena[:, ARENA - KC * WC:ARENA]]

        def slot_view(n):
            _, _, kc, m = weights[n]
            return wslot[slot_of[n]][:, 0:kc * m].rearrange("p (c n) -> p c n", c=kc)

        win_src = a["w_expert_in_2"][0].rearrange("(i k) (c p) n -> i k p c n", k=XPT, p=P)
        wout_src = a["w_expert_out_2"][0].rearrange("(i k) (c p) n -> i k p c n", k=XPT, p=P)

        win_next, wout_next = win_src[1:NE // XPT], wout_src[1:NE // XPT]

        def rounds_of(eng):
            eng.wait_ge(s["turns_ready"], 1)
            return eng.value_load(turns_u[0:1, 0:1], min_val=1, max_val=ROUNDS)
        steps = []
        for i in range(NH * NT + 2):
            if i < NH * NT:
                steps.append(("scores", i))
            if i >= 2:
                steps.append(("turn", i - 2))
                if (i - 2) % NT == NT - 1:
                    steps.append(("head", (i - 2) // NT))
            if i in (2, 11, 16, 25):
                steps.append(("ada_rows", i))
            if i in (4, 13, 18, 27):
                steps.append(("ada_turn", i))
            if i in (6, 8, 20, 22):
                steps.append(("gate", 4 + (6, 8, 20, 22).index(i)))
        S_ATT = 2 + 4 + 24 + 12 + 4 + 16
        score_job = {i: S_ATT + n for n, (what, i) in enumerate(steps) if what == "scores"}
        SUM_LAG, TURN_LAG = 4, 6
        PAIRS = [(st, hg) for st in range(NT) for hg in range(2)]
        C_X, C_D1, C_E, C_C0, C_C1, C_T, C_TT, C_Z, C_VB, C_KBE, C_KDEC, C_VN = range(12)

        role = [list(range(NB))]
        for n in range(1, len(PAIRS)):
            q = role[-1]
            nxt = list(q)
            nxt[C_X], nxt[C_D1], nxt[C_E] = q[C_D1], q[C_C0], q[C_C1]
            nxt[C_C0], nxt[C_C1], nxt[C_T] = q[C_T], q[C_X], q[C_E]
            role.append(nxt)

        ADA_AT = [(1, 3) if n < 4 else (2,) for n in range(len(PAIRS))]

        def buffers(n, d):
            return [grp[d][m] for m in role[n]]

        def tile_of(d, st):
            return st if d == 0 else NT - 1 - st

        def hcols(d, hg):
            return slice(d * 8 + hg * 4, d * 8 + hg * 4 + 4)

        def spread(v, n=P):
            return v.unsqueeze(2).broadcast_to([P, v.shape[1], n])

        def over(v, m):
            return v.unsqueeze(1).broadcast_to([P, m, v.shape[1]])

        def by4(v):
            return v.rearrange("p (h n) -> p h n", h=4)


        def chunk_at(d, n):
            c = n if n < 4 else n - 4
            if d:
                c = (3 if n < 4 else 7) - c
            return (NT if n < 4 else 0) + c // 2, c % 2

        def chunk_col(d, n):
            t, u = chunk_at(d, n)
            return 2 * t + u

        def state_at(d, m2, n):
            if n < 4:
                return swork[:, n % 2, d, m2, :]
            if n == 12:
                return None
            t, u = chunk_at(d, n)
            return sprev[:, d, m2, 2 * t + u, :]

        block = ctx.enter_context(nc.Block())

        @block.sync
        def _(sp):
            issued = [0]

            def load(dst, src, name):
                sp.dma_start(dst, src).then_inc(s[name], 16)

            def stream_to(key):
                while True:
                    n = issued[0]
                    k, src, _, _ = weights[n]
                    if before[n] >= 0:
                        sp.wait_ge(s["w_used"], before[n] + 1)
                    sp.dma_start(slot_view(n), src).then_inc(s["ld_w", slot_of[n]], 16)
                    issued[0] += 1
                    if k == key:
                        return

            def load_expert(k, w_in, w_out):
                sp.dma_start(win[k], w_in).then_inc(s["ld_expert", k], 16)
                sp.dma_start(wout[k], w_out).then_inc(s["ld_expert", k], 16)

            def rows(dst, row, src, n):
                sp.dma_start(dst[row:row + n, :], src.rearrange("(r n) -> r n", n=P)).then_inc(s["ld_vecs"], 16)

            for t in range(NT):
                load(xt[:, t, :], a["x"][0, t * P:(t + 1) * P, :], "ld_x")
            load(const[:, :], a["c_masks"], "ld_const")
            rows(vecs, V_PRE, a["norm_pre"][0], 8)
            rows(vecs, V_DN, a["dn_norm"][0], 1)
            rows(vecs, V_N1, a["norm1_g_2"][0], 8)
            rows(vecs, V_N2, a["norm2_g_2"][0], 8)
            rows(vecs, V_GLA, a["gla_norm_g_2"][0], 1)
            rows(vecs, V_PS, a["pool_scale_2"][0], 4)
            rows(vecs, V_BADA, a["b_ada_2"][0], 48)
            rows(vecs, V_C, a["c_2"][0], 8)
            rows(vecs, V_CC, a["c_ctx_2"], 8)
            rows(cvecs, 0, a["conv_w"][0].rearrange("k c -> (k c)"), CONV_K * 24)
            stream_to(("qkv", 0))
            load(rope, a["c_rope"], "ld_rope")
            load(qkn[:, 0, :], a["q_norm"].partition_broadcast(P), "ld_rope")
            load(qkn[:, 1, :], a["k_norm"].partition_broadcast(P), "ld_rope")
            load(gpar[:, 0, :], a["a_log"].rearrange("a d h -> a (d h)").partition_broadcast(P), "ld_gpar")
            load(gpar[:, 1, :], a["dt_bias"].rearrange("a d h -> a (d h)").partition_broadcast(P), "ld_gpar")
            stream_to(("dz", 1))
            sp.wait_ge(s["phase"], 4 * 3)
            load(rowv, a["norm_post"].partition_broadcast(P), "ld_rows")
            load(rowv2, a["ple_norm"].partition_broadcast(P), "ld_rows")
            for t in range(NT):
                load(x1[:, t, :], a["x"][0, t * P:(t + 1) * P, :], "ld_res")
            load(pin, a["p"][0, 0].rearrange("(t p) n -> p t n", p=P), "ld_p")
            for t in range(NTC):
                load(ctxt[:, t, :], a["ctx_2"][0, t * P:(t + 1) * P, :], "ld_ctx")
            stream_to(("v2", 0))
            sp.wait_ge(s["phase"], 4 * 4)
            load(wdec[0:RANK, :, :], a["w_decay_2"][0].rearrange("d r k -> r d k"), "ld_small")
            load(bdec[0:1, :], a["b_decay_2"].rearrange("a d k -> a (d k)"), "ld_small")
            load(wpool, a["w_pool_2"][0].rearrange("g c d -> c g d"), "ld_small")
            for g in range(2):
                sp.dma_start(pm[:, g, :, :], a["c_pool"][:, g, :, :]).then_inc(s["ld_pm", g], 16)
            stream_to(("p2", 1))
            for g in range(2, 4):
                sp.wait_ge(s["pool_used"], g - 1)
                sp.dma_start(pm[:, g % 2, :, :], a["c_pool"][:, g, :, :]).then_inc(s["ld_pm", g % 2], 16)
            stream_to(("wo2", 1))
            load(wrt[:, :, 0:4], a["w_router_group_2"][0].rearrange("(c p) n -> p c n", p=P), "ld_wrt")
            load(wrt[:, :, 4:36], a["w_router_expert_2"][0].rearrange("(c p) n -> p c n", p=P), "ld_wrt")
            wo2 = a["w_out_2"][0].rearrange("(c p) n -> p c n", p=P)
            sp.wait_ge(s["kst_ready"], NT + NTC)
            load(wo23[0], wo2[:, :, 2 * WC:3 * WC], "ld_small")
            sp.wait_ge(s["sprev_ready"], 1)
            load(wo23[1], wo2[:, :, 3 * WC:4 * WC], "ld_small")
            sp.wait_ge(s["phase"], 4 * 6)
            load(rowf, a["final_norm_g_2"].rearrange("(a n) -> a n", a=1).partition_broadcast(P), "ld_rowf")
            for k in range(2):
                load_expert(k, win_src[0, k], wout_src[0, k])
            for t in range(NT):
                sp.wait_ge(s["x3_ready"], t + 1)
                load(xn_dram[t * P:(t + 1) * P, :], x3n[:, t, :], "xn_saved")
            load(y_dram[NE * CAP:, :].rearrange("o (p n) -> (o p) n", p=KC), zero[0:KC, :], "zeros_saved")
            load_expert(2, win_src[0, 2], wout_src[0, 2])
            for k in range(2):
                sp.wait_ge(s[f"xg_k{k}"], 16)
            load_expert(3, win_src[0, 3], wout_src[0, 3])
            rounds = rounds_of(sp)
            with sp.Fori(0, rounds) as r:
                with sp.Fori(0, NE // XPT - 1) as i:
                    for k in range(XPT):
                        sp.wait_ge(s["moe_used"], r * NE + i * XPT + (k + 1))
                        load_expert(k, win_next[i, k], wout_next[i, k])
                with sp.If(r + 1 < rounds):
                    for k in range(XPT):
                        if k < 2:
                            sp.wait_ge(s["moe_used"], r * NE + (NE - XPT + 1 + k))
                        elif k == 2:
                            sp.wait_ge(s["combined"], r + 2)
                        load_expert(k, win_src[0, k], wout_src[0, k])
            for t in range(NT):
                sp.wait_ge(s["out_ready"], t + 1)
                sp.dma_start(out[0, t * P:(t + 1) * P, :], x3[:, t, :]).then_inc(s["ld_out"], 16)
            for name, ap in dumps:
                sp.dma_start(name, ap).then_inc(s["ld_out"], 16)
            sp.wait_ge(s["ld_out"], 16 * (NT + len(dumps)))

        @block.tensor
        def _(pe):
            L = Lane(pe, None)
            jobs = {"v": 0, "s": 0}
            banks = {"v": psv, "s": pss}
            at_slot = [0]
            mm, tr = nc.tensor.matmul, nc.tensor.transpose

            def bank(r):
                n = jobs[r]
                if n >= 4:
                    pe.wait_ge(s["free_" + r], n - 3)
                jobs[r] += 1
                return banks[r][:, n % 4, :]

            def slot(key):
                n = at_slot[0]
                assert weights[n][0] == key, (weights[n][0], key)
                at_slot[0] += 1
                pe.wait_ge(s["ld_w", slot_of[n]], 16 * turn_of[n])
                return slot_view(n)

            def used(n=1):
                for _ in range(n):
                    pe.drain().then_inc(s["w_used"], 1)

            def phase(n):
                pe.drain().then_inc(s["phase"], 1)
                pe.wait_ge(s["phase"], 4 * n)

            def product(o, pairs):
                for n, (l, r) in enumerate(pairs):
                    m = mm(o, l, r, start=(n == 0), stop=(n == len(pairs) - 1))
                return m

            def feature_tile(r, w, j, src, kc=KC, n=SEQ):
                o = bank(r)
                product(o[:, 0:n], [(w[:, c, j * P:(j + 1) * P], src[:, c, :]) for c in range(kc)])\
                    .then_inc(s["full_" + r], 1)

            def token_tile(r, w, t, src, c0=0, n=WC, kc=KC):
                o = bank(r)
                product(o[:, 0:n], [(src[:, c, t * P:(t + 1) * P], w[:, c, c0:c0 + n]) for c in range(kc)])\
                    .then_inc(s["full_" + r], 1)

            def turn(r, parts):
                o = bank(r)
                for n, v in enumerate(parts):
                    m = tr(o[:, n * P:n * P + v.shape[0]], v, ident[0:v.shape[0], 0:v.shape[0]])
                m.then_inc(s["full_" + r], 1)

            def turn_features(v):
                for r, c0 in (("v", 0), ("s", 4)):
                    turn(r, [v[:, c * P:(c + 1) * P] for c in range(c0, c0 + 4)])

            ada = [0, 0]

            def ada_rows():
                w = slot(("ada", ada[0]))
                o = bank("s")
                product(o[0:2, 0:WC], [(csilu[:, c, :], w[:, c, :]) for c in range(KC)]).then_inc(s["full_s"], 1)
                used()
                ada[0] += 1

            def ada_turn():
                L.need(s["row_ready"])
                turn("s", [arow[0:2, ada[1] % 2, j * P:(j + 1) * P] for j in range(2)])
                ada[1] += 1

            pe.wait_ge(s["ld_const"], 16)
            pe.wait_ge(s["ld_vecs"], 160)
            turn("s", [vecs[0:V_N, :]])
            turn("s", [cvecs[0:CONV_K * 24, :]])
            for t in range(NT):
                L.need(s["xn_ready"])
                turn_features(xt[:, t, :])
            for b in range(6):
                w = slot(("qkv", b))
                for t in range(NT):
                    if b == 0:
                        L.need(s["hT_ready"])
                        L.need(s["half_ready"])
                    token_tile("s", w, t, hT)
                used()
            w = slot("dbda")
            for t in range(NT):
                token_tile("v", w, t, hT, 0, 32)
            used()
            for t in range(NT):
                if t % 2 == 0:
                    w = slot(("az", t // 2))
                    feature_tile("s", w, 0, hT)
                    feature_tile("s", w, 1, hT)
                    used()
                for _ in range(2):
                    ada_rows()
                for _ in range(2):
                    ada_turn()
                L.need(s["rope_ready"])
                for h0, n in ((0, 4), (4, 4), (8, 2)):
                    turn("s", [atok[:, t, h * HD:(h + 1) * HD] for h in range(h0, h0 + n)])
            L.need(s["qkT_ready"], 12)
            L.need(s["atok_ready"], 24)
            assert jobs["s"] == S_ATT
            for what, i in steps:
                h, t = divmod(i, NT)
                if what == "scores":
                    mm(bank("s"), qkT[:, h, t * P:(t + 1) * P], qkT[:, NH + h // (NH // NKV), :], start=True,
                       stop=True).then_inc(s["full_s"], 1)
                elif what == "turn":
                    L.need(s["probsn_ready"])
                    turn("s", [pb[:, i % 3, k * P:(k + 1) * P] for k in range(NT)])
                elif what == "ada_rows":
                    ada_rows()
                elif what == "ada_turn":
                    ada_turn()
                elif what == "head":
                    L.need(s["pT_ready"], NT)
                    kv = 1280 + (i // (NH // NKV)) * HD
                    product(bank("s"), [(atok[:, k, kv:kv + HD], pT[:, i % 2, k, :]) for k in range(NT)])\
                        .then_inc(s["full_s"], 1)
                else:
                    if i % 2 == 0:
                        w = slot(("az", i // 2))
                    feature_tile("s", w, i % 2, hT)
                    if i % 2:
                        used()
            for b in range(4):
                w, g = slot(("bra", b)), slot(("ga", b))
                for j in range(2):
                    feature_tile("s", g, j, hT)
                if b == 0:
                    L.need(s["oz_ready"], KC)
                for j in range(2):
                    feature_tile("v", w, j, oT)
                used(2)
            phase(1)

            for j in range(24 + 1):
                if j == 2:
                    L.need(s["gg_ready"])
                    o = bank("v")
                    for t in range(NT):
                        for d in range(2):
                            m = mm(o[:, t * 16 + d * 8:t * 16 + d * 8 + 8], tri[d],
                                   gbuf[:, 0, t, d * 8:d * 8 + 8], start=True, stop=True)
                    m.then_inc(s["full_v"], 1)
                if j < 24:
                    if j % 2 == 0:
                        w = slot(("dqkv", j // 2))
                    feature_tile("v", w, j % 2, hT)
                    if j % 2:
                        used()
                if j > 16:
                    pe.wait_ge(s["silu_ready"], j)
                    turn("s", [cst[:, (j - 1) % 2, t * P:(t + 1) * P] for t in range(NT)])
                if SUM_LAG <= j < 16 + SUM_LAG:
                    L.need(s["sq_ready"])
                    o = bank("s")
                    mm(o, ones, csq[:, (j - SUM_LAG) % 2, :], start=True, stop=True).then_inc(s["full_s"], 1)
                if 8 + TURN_LAG <= j < 16 + TURN_LAG:
                    pe.wait_ge(s["norm_ready"], j - TURN_LAG + 1)
                    turn("s", [kT[:, j - TURN_LAG - 8, t * P:(t + 1) * P] for t in range(NT)])
            phase(2)

            def four(r, make):
                o = bank(r)
                for h in range(4):
                    ps = make(h)
                    for q, (l, x) in enumerate(ps):
                        m = mm(o[:, h * P:(h + 1) * P], l, x, start=(q == 0), stop=(q == len(ps) - 1))
                m.then_inc(s["full_" + r], 1)

            def decay_rows(n):
                st, hg = PAIRS[n]
                for d in range(2):
                    t, dh = tile_of(d, st), d * 8 + hg * 4
                    four("s", lambda h: [(gbuf[:, 0, t, dh + h:dh + h + 1].broadcast_to([P, P]), tri[d])])

            def key_products(n):
                st, hg = PAIRS[n]
                for d in range(2):
                    tk = slice(tile_of(d, st) * P, (tile_of(d, st) + 1) * P)
                    four("v", lambda h: [(kT[:, hg * 4 + h, tk], kT[:, hg * 4 + h, tk])])
                    four("v", lambda h: [(kT[:, hg * 4 + h, tk], qT[:, hg * 4 + h, tk])])

            decay_rows(0)
            key_products(0)
            for n, (st, hg) in enumerate(PAIRS):
                for d in range(2):
                    g = buffers(n, d)
                    L.need(s["c_ready", d])
                    turn("v", [g[C_C0][:, h, :] for h in range(4)])
                for k in range(1, LEVELS):
                    for d in range(2):
                        g = buffers(n, d)
                        L.need(s["c_ready", d])
                        L.need(s["tt_ready", d])
                        four("s", lambda h: [(g[C_C0 + k % 2][:, h, :], g[C_TT][:, h, :])])
                    if k in ADA_AT[n]:
                        ada_rows()
                    if k - 1 in ADA_AT[n]:
                        ada_turn()
                    for d in range(2):
                        g = buffers(n, d)
                        L.need(s["zz_ready", d])
                        L.need(s["t_ready", d])
                        four("v", lambda h: [(g[C_T][:, h, :], g[C_Z][:, h, :])])
                        if k < LEVELS - 1:
                            four("v", lambda h: [(g[C_Z][:, h, :], g[C_T][:, h, :])])
                if n + 1 < len(PAIRS):
                    decay_rows(n + 1)
                for d in range(2):
                    g = buffers(n, d)
                    L.need(s["kbe_ready", d])
                    L.need(s["tt_ready", d])
                    four("s", lambda h: [(g[C_KBE][:, h, :], g[C_TT][:, h, :])])
                for d in range(2):
                    g = buffers(n, d)
                    L.need(s["nwt_ready", d])
                    if st:
                        pe.wait_ge(s["group_done", d], n - 1)
                    four("v", lambda h: [(g[C_TT][:, h, :], g[C_VB][:, h, :])] +
                         ([(g[C_Z][:, h, :], state[:, d, hg * 4 + h, :])] if st else []))
                if n + 1 < len(PAIRS):
                    key_products(n + 1)
                for d in range(2):
                    g = buffers(n, d)
                    L.need(s["vn_ready", d])
                    L.need(s["at_ready", d])
                    L.need(s["qg_ready", d])
                    four("v", lambda h: ([(g[C_E][:, h, :], state[:, d, hg * 4 + h, :])] if st else []) +
                         [(g[C_X][:, h, :], g[C_VN][:, h, :])])
                for d in range(2):
                    g = buffers(n, d)
                    L.need(s["kdec_ready", d])
                    four("v", lambda h: [(g[C_KDEC][:, h, :], g[C_VN][:, h, :])])

            phase(3)
            for b in range(4):
                if b == 3:
                    for t in range(NT):
                        L.need(s["on_ready"])
                        for h0 in (0, 4):
                            turn("v", [oacc[:, t, h, :] for h in range(h0, h0 + 4)])
                w = slot(("dz", b))
                for j in range(2):
                    feature_tile("s", w, j, hT)
                used()
            L.need(s["dz_ready"], KC)
            for b in range(4):
                w, g = slot(("brd", b)), slot(("gd", b))
                for j in range(2):
                    feature_tile("v", w, j, onT)
                    feature_tile("s", g, j, hT)
                used(2)
            pe.wait_ge(s["ld_p"], 16)
            for t in range(NT):
                turn("v", [pin[:, t, c * P:(c + 1) * P] for c in range(2)])
            L.need(s["mixT_ready"], KC)
            for b in range(4):
                w = slot(("wo", b))
                for t in range(NT):
                    token_tile("s", w, t, mixT)
                used()
            L.need(s["pinT_ready"], NT)
            w = slot("plep")
            for t in range(NT):
                for c0 in (0, 512):
                    token_tile("s", w, t, pinT, c0, 512, 2)
            used()
            for t in range(NT):
                L.need(s["x1_ready"])
                turn_features(x1[:, t, :])
            for b in range(4):
                w = slot(("pleg", b))
                for t in range(NT):
                    if b == 0:
                        L.need(s["x1T_ready"])
                        L.need(s["half_ready"])
                    token_tile("s", w, t, x1T)
                used()
                if b == 1:
                    for t in range(NTC):
                        L.need(s["x2_ready"])
                        turn_features(ctxt[:, t, :])
            L.need(s["hc_ready"], NTC)
            L.need(s["half_ready"], NTC)
            wk, wv = slot("k2"), slot(("v2", 0))
            for t in range(NTC):
                token_tile("s", wk, t, hcT)
            for t in range(NTC):
                token_tile("v", wv, t, hcT)
            phase(4)
            for t in range(NT):
                L.need(s["x2_ready"])
                turn_features(xn[:, t, :])
            for t in range(NT):
                L.need(s["h2_ready"])
                L.need(s["half_ready"])
                token_tile("s", wk, t, h2T)
            for j in range(2):
                feature_tile("s", wk, j, h2T)
            used()
            for t in range(NT):
                token_tile("v", wv, t, h2T)
            used()
            w = slot(("v2", 1))
            for t in range(NT):
                token_tile("v", w, t, h2T)
            for t in range(NTC):
                token_tile("v", w, t, hcT)
            used()
            w = slot("q2")
            for j in range(2):
                feature_tile("s", w, j, h2T)
            used()
            for b in range(2):
                w = slot(("g2", b))
                for j in range(2):
                    feature_tile("s", w, j, h2T)
                used()
            w = slot("a2")
            for d in range(2):
                for src, n in ((h2T, SEQ), (hcT, CTX)):
                    o = bank("v")
                    product(o[0:RANK, 0:n], [(w[:, c, d * RANK:(d + 1) * RANK], src[:, c, :]) for c in range(KC)])\
                        .then_inc(s["full_v"], 1)
            used()
            for b in range(2):
                w = slot(("p2", b))
                for t in range(NT):
                    token_tile("v", w, t, h2T)
                used()
                if b == 0:
                    pe.wait_ge(s["ld_small"], 48)
                    L.need(s["a2_ready"], 4)
                    for t in range(NT + NTC):
                        o = bank("s")
                        for d in range(2):
                            mm(o[:, d * 256:(d + 1) * 256], a2T[0:RANK, d, t * P:(t + 1) * P], wdec[0:RANK, d, :],
                               start=True, stop=False)
                            m = mm(o[:, d * 256:(d + 1) * 256], ones[0:1, :], bdec[0:1, d * 256:(d + 1) * 256],
                                   start=False, stop=True)
                        m.then_inc(s["full_s"], 1)
            L.need(s["p2_ready"], 2 * NT)
            for g in range(4 + 1):
                if g < 4:
                    pe.wait_ge(s["ld_pm", g % 2], 16 * (g // 2 + 1))
                    o = bank("v")
                    product(o, [(p2[:, k, g * P:(g + 1) * P], pm[:, g % 2, k, :]) for k in range(NT)])\
                        .then_inc(s["full_v"], 1)
                    pe.drain().then_inc(s["pool_used"], 1)
                if g >= 1:
                    L.need(s["mT_ready"])
                    o = bank("s")
                    mm(o, wpool[:, g - 1, :], pmT[:, (g - 1) % 2, :], start=True, stop=True)\
                        .then_inc(s["full_s"], 1)
            phase(5)

            L.need(s["la_ready"], NT + NTC)
            for d in range(2):
                for m2 in range(2):
                    col = d * 256 + m2 * P
                    o = bank("s")
                    for t in range(NT):
                        m = mm(o[:, t * P:(t + 1) * P], la[:, t, col:col + P], blk[d], start=True, stop=True)
                    m.then_inc(s["full_s"], 1)
                    o = bank("s")
                    for t in range(NTC):
                        m = mm(o[:, t * P:(t + 1) * P], la[:, NT + t, col:col + P], blk[d], start=True, stop=True)
                    m.then_inc(s["full_s"], 1)
            for t in range(NT + NTC):
                o = bank("s")
                for d in range(2):
                    m = mm(o[:, d * 256:(d + 1) * 256], blk_rest[d], la[:, t, d * 256:(d + 1) * 256],
                           start=True, stop=True)
                m.then_inc(s["full_s"], 1)
            L.need(s["kst_ready"], NT + NTC)
            L.need(s["k2_ready"])
            for n in range(12):
                for d in range(2):
                    t, u = chunk_at(d, n)
                    o = bank("v")
                    for m2 in range(2):
                        m = mm(o[:, m2 * 256:(m2 + 1) * 256],
                               kst[u * CH2:(u + 1) * CH2, t, d * 256 + m2 * P:d * 256 + (m2 + 1) * P],
                               v2[u * CH2:(u + 1) * CH2, t, m2 * 256:(m2 + 1) * 256], start=True, stop=True)
                    m.then_inc(s["full_v"], 1)
                if n < 2 * H2:
                    h, d = divmod(n, 2)
                    m2, hp = h // 2, slice((h % 2) * 64, (h % 2) * 64 + 64)
                    if n == 0:
                        L.need(s["qb_ready"], 4)
                    o = bank("v")
                    for t in range(NT):
                        tk = slice(t * P, (t + 1) * P)
                        m = mm(o[:, tk], kb[hp, d, m2, tk], qb[hp, d, m2, tk], start=True, stop=True)
                    m.then_inc(s["full_v"], 1)
            for c0 in (0, 4):
                o = bank("v")
                for c in range(4):
                    m = mm(o[:, c * P:(c + 1) * P], mod[:, 16 + c0 + c, 0:1].broadcast_to([P, P]), ident,
                           start=True, stop=True)
                m.then_inc(s["full_v"], 1)
            L.need(s["sc_ready"], 2 * H2)
            L.need(s["sprev_ready"])
            for h in range(H2 + 1):
                if h < H2:
                    m2, hp = h // 2, slice((h % 2) * 64, (h % 2) * 64 + 64)
                    o = bank("s")
                    for d in range(2):
                        for t in range(NT):
                            tk = slice(t * P, (t + 1) * P)
                            mm(o[:, tk], v2[:, t, h * P:(h + 1) * P], scm[2 * h + d][:, tk],
                               start=(d == 0 and t == 0), stop=False, skip_group_check=True)
                        for c in range(8):
                            ck = slice(c * CH2, (c + 1) * CH2)
                            m = mm(o[:, ck], sprev[hp, d, m2, c, :], qb[hp, d, m2, ck], start=False,
                                   stop=(d == 1 and c == 7), skip_group_check=True)
                    m.then_inc(s["full_s"], 1)
                if h >= 1:
                    L.need(s["sq2_ready"])
                    o = bank("s")
                    mm(o, ones, eb[:, (h - 1) % 2, :], start=True, stop=True).then_inc(s["full_s"], 1)
            wo2 = [slot(("wo2", 0)), slot(("wo2", 1))] + wo23
            pe.wait_ge(s["ld_small"], 80)
            pe.wait_ge(s["ld_wrt"], 32)

            def logits(t):
                L.need(s["h3_ready"])
                L.need(s["half_ready"])
                token_tile("v", wrt, t, h3T, 0, NG + NE)

            def turn_x3(t):
                L.need(s["x3_ready"])
                turn_features(x3n[:, t, :])

            first = [bank("v") for _ in range(4)]
            for b in range(4):
                for c in range(4, KC):
                    mm(first[b][:, 0:WC], catT[:, c, 0:P], wo2[b][:, c, :], start=(c == 4), stop=False)
            L.need(s["cat_ready"], 8)
            for b in range(4):
                for c in range(4):
                    m = mm(first[b][:, 0:WC], catT[:, c, 0:P], wo2[b][:, c, :], start=False, stop=(c == 3))
                m.then_inc(s["full_v"], 1)
            for t in range(1, NT):
                for b in range(4):
                    token_tile("v", wo2[b], t, catT)
                turn_x3(t - 1)
                if t >= 2:
                    logits(t - 2)
            pe.drain().then_inc(s["phase"], 1)
            turn_x3(NT - 1)
            logits(NT - 2)
            logits(NT - 1)

            for c0 in (0, 4):
                o = bank("v")
                for c in range(4):
                    m = mm(o[:, c * P:(c + 1) * P], mod[:, 40 + c0 + c, 0:1].broadcast_to([P, P]), ident,
                           start=True, stop=True)
                m.then_inc(s["full_v"], 1)
            L.need(s["picked_ready"])
            o = bank("v")
            mm(o[:, 0:NT * NE], const[:, C_LT:C_LT + P], picked.rearrange("p t n -> p (t n)"), start=True, stop=False)
            ahead = before_t.rearrange("p t n -> p (t n)")
            mm(o[:, 0:NT * NE], ones, ahead[:, 0:NT * NE], start=False, stop=True)
            mm(o[:, NT * NE:(NT + 1) * NE], ones, ahead[:, NT * NE:], start=True, stop=True)\
                .then_inc(s["full_v"], 1)
            o = bank("v")
            for t in range(NT):
                L.need(s["table_ready"])
                for k in range(2):
                    m = mm(o[0:CAP, 0:ROUNDS * NE], rplaced[:, 2 * t + k, :],
                           tok_at[:, t, k, :, :].rearrange("p r e -> p (r e)"), start=(t == 0 and k == 0),
                           stop=(t == NT - 1 and k == 1))
            m.then_inc(s["full_v"], 1)
            pe.wait_ge(s["xg_k0"], 16)
            o = bank("v")
            for c in range(KC):
                m = tr(o[:, c * CAP:(c + 1) * CAP], xg[0:CAP, 0, c * P:(c + 1) * P], ident[0:CAP, 0:CAP])
            m.then_inc(s["full_v"], 1)
            v0, s0 = jobs["v"], jobs["s"]
            VJ, SJ = 3 * XPT, 2 * XPT
            rounds = rounds_of(pe)
            with pe.Fori(0, rounds * (NE // XPT)) as i:
                nv, ns = [0], [0]

                def vbank():
                    k = nv[0]
                    nv[0] += 1
                    pe.wait_ge(s["free_v"], i * VJ + (v0 + k - 3))
                    return psv[:, (v0 + k) % 4, :]

                def sbank():
                    k = ns[0]
                    ns[0] += 1
                    pe.wait_ge(s["free_s"], i * SJ + (s0 + k - 3))
                    return pss[:, (s0 + k) % 4, :]

                for q in range(XPT):
                    k = q % 2
                    nth = i * (XPT // 2) + (q // 2 + 1)
                    pe.wait_ge(s["ld_expert", q], i * 32 + 32)
                    pe.wait_ge(s["xe_ready"], i * XPT + (q + 1))
                    pe.wait_ge(s[f"xg_k{1 - k}"], nth * 16 if k == 0 else nth * 16 + 16)
                    a_bank, u_bank, turn_bank = sbank(), vbank(), vbank()
                    for o, full, c0 in ((a_bank, "full_s", 0), (u_bank, "full_v", DE)):
                        for j in range(2):
                            m = product(o[:, j * CAP:(j + 1) * CAP],
                                        [(win[q][:, c, c0 + j * P:c0 + (j + 1) * P], xe[:, k, c, :])
                                         for c in range(KC)])
                        m.then_inc(s[full], 1)
                    for c in range(KC):
                        m = tr(turn_bank[:, c * CAP:(c + 1) * CAP], xg[0:CAP, 1 - k, c * P:(c + 1) * P],
                               ident[0:CAP, 0:CAP])
                    m.then_inc(s["full_v"], 1)
                    pe.wait_ge(s["hid_ready"], i * XPT + (q + 1))
                    for get, full, c0 in ((sbank, "full_s", 0), (vbank, "full_v", 512)):
                        product(get()[0:CAP, :], [(hid[:, k, c * CAP:(c + 1) * CAP], wout[q][:, c, c0:c0 + 512])
                                                  for c in range(2)]).then_inc(s[full], 1)
                    pe.drain().then_inc(s["moe_used"], 1)

        @block.scalar
        def _(act):
            L = Lane(act, s["chain_s"])
            seen = [0]
            A = nc.scalar.activation

            def full():
                L.need(s["full_s"])
                seen[0] += 1
                return pss[:, (seen[0] - 1) % 4, :]

            def evict(dst, n, sig, func=ACT.Copy, **kw):
                b = full()
                src = b[:, 0:n]
                if len(dst.shape) == 3:
                    src = src.rearrange("p (a b) -> p a b", b=dst.shape[2])
                L.did(A(dst, src, func, **kw), s[sig] if sig else None, [s["free_s"]])

            def root(v):
                L.need(s["rs_in"])
                L.did(A(v, v, ACT.Sqrt), s["rs_out"])

            ada = [0, 0]

            def ada_rows():
                b = full()
                L.did(A(arow[0:2, ada[0] % 2, :], b[0:2, 0:WC], ACT.Copy), s["row_ready"], [s["free_s"]])
                ada[0] += 1

            def ada_turn():
                n = 2 * ada[1]
                b = full()
                L.did(A(mod[:, n:n + 2, :], b[:, 0:2 * P].rearrange("p (j n) -> p j n", j=2)[:, :, 0:2], ACT.Copy),
                      s["mod_ready"], [s["free_s"]])
                ada[1] += 1

            def turned(dst, t, gains, shifts):
                b = full()
                for c in range(4, KC):
                    o, src = dst[:, c, t * P:(t + 1) * P], b[:, (c - 4) * P:(c - 3) * P]
                    g = gains[:, c:c + 1]
                    if shifts is None:
                        ins = A(o, src, ACT.Copy, scale=g)
                    else:
                        ins = A(o, src, ACT.Identity, scale=g, bias=shifts[:, c:c + 1])
                    L.did(ins, None, [s["free_s"], s["half_ready"]] if c == KC - 1 else [])

            def phase(n):
                act.sem_inc(s["phase"])
                act.wait_ge(s["phase"], 4 * n)

            evict(cols[:, 0:V_N], V_N, "cols_ready")
            evict(ccols[:, :], CONV_K * 24, "cols_ready")
            L.did(A(csilu[:, :, :].rearrange("p c k -> p k c"),
                    cols[:, V_C:V_C + 16].rearrange("p (k c) -> p k c", k=2), ACT.Silu))
            root(ss[:, 0:NT])
            for t in range(NT):
                turned(hT, t, cols[:, V_PRE:V_PRE + 8], None)
            for b in range(6):
                for t in range(NT):
                    evict(atok[:, t, b * WC:(b + 1) * WC], WC, "atok_ready")
            for t in range(NT):
                root(ss[:, 16:26])
                if t % 2 == 0:
                    for j in range(t, t + 2):
                        evict(azs[:, j, :], SEQ, None)
                for _ in range(2):
                    ada_rows()
                for _ in range(2):
                    ada_turn()
                for h0, n in ((0, 4), (4, 4), (8, 2)):
                    evict(qkT[:, h0:h0 + n, t * P:(t + 1) * P], n * P, "qkT_ready")
            for what, i in steps:
                h, t = divmod(i, NT)
                if what == "scores":
                    L.need(s["negmax_ready"])
                    b = full()
                    L.did(A(pb[:, i % 3, :], b, ACT.Exp, bias=small[:, 64 + i:65 + i], scale=HD ** -0.5,
                            accum_out=small[:, 96 + i:97 + i]), s["probs_ready"], [s["free_s"]])
                elif what == "turn":
                    evict(pT[:, h % 2, :, t * P:(t + 1) * P], SEQ, "pT_ready")
                elif what == "ada_rows":
                    ada_rows()
                elif what == "ada_turn":
                    ada_turn()
                elif what == "head":
                    evict(oT[:, i, :], SEQ, "oT_ready")
                else:
                    evict(azs[:, i, :], SEQ, None)
            for j in range(KC):
                L.did(A(azs[:, j, :], azs[:, j, :], ACT.Silu), s["silu_z"])
            ntmp = [0]

            def gate(tmp, func):
                n = ntmp[0]
                ntmp[0] += 1
                if n >= 2:
                    act.wait_ge(s["tmp_used"], n - 1)
                evict(tmp[:, n % 2, :], SEQ, "tmp_ready", func)

            for j in range(KC):
                gate(tmpA, ACT.Sigmoid)
            phase(1)

            act.wait_ge(s["ld_gpar"], 32)
            L.did(A(gpar[:, 2, :], gpar[:, 0, :], ACT.Exp), s["ga_ready"])
            L.need(s["ga_step"])
            L.did(A(gbuf[:, 6, :, :], gbuf[:, 6, :, :], ACT.Exp))
            L.did(A(gbuf[:, 6, :, :], gbuf[:, 6, :, :], ACT.Ln, bias=one), s["ga_ready"])
            L.did(A(gbuf[:, 3, :, :], gb[:, :, 0:16], ACT.Sigmoid), s["ga_ready"])
            for j in range(24 + 1):
                if j == 2:
                    L.need(s["gG_ready"])
                    L.did(A(gbuf[:, 2, :, :], gbuf[:, 1, :, :], ACT.Exp), s["ga_ready"])
                if j > 16:
                    evict(vtok[:, :, j - 17, :], SEQ, None)
                if SUM_LAG <= j < 16 + SUM_LAG:
                    n = j - SUM_LAG
                    if n >= 2:
                        act.wait_ge(s["norm_ready"], n - 1)
                    if n < 8:
                        evict(crt[:, n % 2, :], SEQ, "rt_ready", ACT.Sqrt, bias=eps128, scale=float(HD))
                    else:
                        evict(crt[:, n % 2, :], SEQ, "rt_ready", ACT.Sqrt, bias=eps)
                if 8 + TURN_LAG <= j < 16 + TURN_LAG:
                    evict(ktok[:, :, j - TURN_LAG - 8, :], SEQ, None)
                if j < 24:
                    L.need(s["conv_ready"])
                    dst = qT[:, j, :] if j < 8 else kT[:, j - 8, :] if j < 16 else cst[:, j % 2, :]
                    L.did(A(dst, conv[:, j % 2, :], ACT.Silu), s["silu_ready"])
                n = j - (SUM_LAG - 1)
                if 0 <= n < 16:
                    src = qT[:, n, :] if n < 8 else kT[:, n - 8, :]
                    L.did(A(csq[:, n % 2, :], src, ACT.Square), s["sq_ready"])
            phase(2)

            def decay_rows(n):
                for d in range(2):
                    g = buffers(n, d)
                    if n:
                        act.wait_ge(s["c_ready", d], n * LEVELS)
                    b = full()
                    L.did(A(g[C_X], by4(b), ACT.Copy))
                    L.did(A(g[C_E], by4(b), ACT.Exp), s["e_ready", d], [s["free_s"]])
                    last = P - 1 if d == 0 else 0
                    L.did(A(glast[:, n % 2, d, :], g[C_E][:, :, last], ACT.Copy), s["glast_ready", d])

            def decays(n):
                for d in range(2):
                    g = buffers(n, d)
                    L.need(s["x_ready", d])
                    L.did(A(g[C_D1], g[C_D1], ACT.Exp, scale=-1.0), s["d1_ready", d])
                    L.did(A(g[C_X], g[C_X], ACT.Exp), s["d2_ready", d])

            decay_rows(0)
            decays(0)
            for n, (st, hg) in enumerate(PAIRS):
                for k in range(1, LEVELS):
                    for d in range(2):
                        b = full()
                        L.did(A(buffers(n, d)[C_Z], by4(b), ACT.Copy), s["zz_ready", d], [s["free_s"]])
                    if k in ADA_AT[n]:
                        ada_rows()
                    if k - 1 in ADA_AT[n]:
                        ada_turn()
                if n + 1 < len(PAIRS):
                    decay_rows(n + 1)
                for d in range(2):
                    b = full()
                    L.did(A(buffers(n, d)[C_Z], by4(b), ACT.Copy, scale=-1.0), s["nwt_ready", d], [s["free_s"]])
                if n + 1 < len(PAIRS):
                    decays(n + 1)
            phase(3)

            for j in range(KC):
                if j == 2:
                    root(ss[:, 0:32])
                gate(tmpB, ACT.Silu)
            for j in range(KC):
                gate(tmpB, ACT.Sigmoid)
            for b in range(4):
                for t in range(NT):
                    evict(mo[:, t, b * WC:(b + 1) * WC], WC, "mo_ready")
            for t in range(NT):
                if t == 1:
                    root(ss[:, 0:NT])
                for c0 in (0, 512):
                    evict(et[:, t, c0:c0 + 512], 512, None)
            for t in range(NT):
                b = full()
                L.did(A(x1T[:, 4:8, t * P:(t + 1) * P], by4(b), ACT.Copy), None, [s["half_ready"], s["free_s"]])
            for b in range(4):
                for t in range(NT):
                    evict(sg[:, t, b * WC:(b + 1) * WC], WC, "sg_ready", ACT.Sigmoid)
                if b == 0:
                    root(ss[:, 40:40 + NTC])
                if b == 1:
                    for t in range(NTC):
                        turned(hcT, t, gain[:, 8:16], mod[:, 0:8, 1])
            root(ss[:, 0:NT])
            for t in range(NTC):
                evict(k2[:, NT + t, :], 256, None)
            for t in range(NT):
                act.wait_ge(s["x1_ready"], NT + t + 1)
                L.did(A(sg[:, NT - 1, :], x1[:, t, :], ACT.Square, accum_out=ss[:, 32 + t:33 + t]))
            L.did(A(ss[:, 32:32 + NT], ss[:, 32:32 + NT], ACT.Sqrt, bias=eps, scale=1.0 / DM), s["rs_out"])
            phase(4)

            for t in range(NT):
                turned(h2T, t, gain[:, 0:8], mod[:, 0:8, 0])
            for t in range(NT):
                evict(k2[:, t, :], 256, None)
            for j in range(2):
                evict(k2T[:, j, :], SEQ, "k2_ready")
            for j in range(2):
                evict(q2T[:, j, :], SEQ, "k2_ready", ACT.Copy, scale=DK2 ** -0.5)
            for j in range(4):
                evict(g2T[:, j, :], SEQ, "k2_ready", ACT.Silu)
            for t in range(NT + NTC):
                evict(la[:, t, :], 512, "z_ready")
            for t in range(NT + NTC):
                L.need(s["absz_ready"])
                L.did(A(zabs[t], zabs[t], ACT.Exp, scale=-1.0))
            for t in range(NT + NTC):
                L.did(A(zabs[t], zabs[t], ACT.Ln, bias=one), s["lz_ready"])
            for g in range(4):
                b = full()
                L.did(A(catT[:, 4 + g, :], b, ACT.Copy, scale=cols[:, V_PS + g:V_PS + g + 1]), s["cat_ready"], [s["free_s"]])
            phase(5)

            for n in range(4):
                d, m2 = divmod(n, 2)
                b = full()
                if n >= 2:
                    act.wait_ge(s["qb_ready"], n - 1)
                L.did(A(eb[:, n % 2, :], b, ACT.Exp, scale=1.0 / GATE_NORM))
                L.did(A(enb[:, n % 2, :], b, ACT.Exp, scale=-1.0 / GATE_NORM))
                ends = b.rearrange("p (c i) -> p c i", i=CH2)[:, :, CH2 - 1 if d == 0 else 0]
                L.did(A(dec2[:, d, m2, 0:8], ends, ACT.Exp, scale=1.0 / GATE_NORM), s["bexp_ready"], [s["free_s"]])
                b = full()
                ends = b[:, 0:CTX].rearrange("p (c i) -> p c i", i=CH2)[:, :, CH2 - 1 if d == 0 else 0]
                L.did(A(dec2[:, d, m2, 8:12], ends, ACT.Exp, scale=1.0 / GATE_NORM), s["bexp_ready"], [s["free_s"]])
            for t in range(NT + NTC):
                evict(kst[:, t, :], 512, "kexp_ready", ACT.Exp, scale=1.0 / GATE_NORM)
            L.need(s["qb_ready"], 4)
            for h in range(H2 + 1):
                if h < H2:
                    b = full()
                    L.did(A(eb[:, h % 2, :], b, ACT.Square), s["sq2_ready"])
                    L.did(A(catT[:, h, :], b, ACT.Copy), s["rt2_ready"], [s["free_s"]])
                if h >= 1:
                    b = full()
                    if h >= 3:
                        act.wait_ge(s["o2_ready"], h - 2)
                    L.did(A(enb[:, (h - 1) % 2, :], b, ACT.Sqrt, bias=eps, scale=1.0 / DV2), s["rt2_ready"],
                          [s["free_s"]])
            act.sem_inc(s["phase"])
            for t in range(NT):
                if t:
                    turned(h3T, t - 1, gain[:, 16:24], mod[:, 24:32, 0])
                root(ss[:, t:t + 1])
            turned(h3T, NT - 1, gain[:, 16:24], mod[:, 24:32, 0])
            L.need(s["lg_ready"])
            L.did(A(lexp, lexp, ACT.Exp), s["lexp_ready"])
            q0 = seen[0]
            act.sem_inc(s["st_y0"], 16)
            act.sem_inc(s["st_y1"], 16)
            rounds = rounds_of(act)
            with act.Fori(0, rounds) as r:
                act.wait_ge(s["combined"], r + 1)
                with act.Fori(0, NE // XPT) as ir:
                    i = r * (NE // XPT) + ir
                    L.enter(i, {s["sil_ready"]: XPT, s["free_s"]: 2 * XPT, s["chain_s"]: XPT},
                            {s["full_s"]: 2 * XPT, s["sil_used"]: XPT, s["y1_ready"]: XPT})
                    for q in range(XPT):
                        k = q % 2
                        L.need(s["full_s"])
                        L.need(s["sil_used"])
                        L.did(A(sil[:, k, :], pss[:, (q0 + 2 * q) % 4, 0:2 * CAP], ACT.Silu), s["sil_ready"],
                              [s["free_s"]])
                        L.need(s["full_s"])
                        act.wait_ge(s[f"st_y{k}"], (i * (XPT // 2) + (q // 2 + 1)) * 16)
                        L.did(A(yb[0:CAP, k, 0:512], pss[0:CAP, (q0 + 2 * q + 1) % 4, :], ACT.Copy), None,
                              [s["free_s"]])
                        L.need(s["y1_ready"])
                        act.dma_start(y_store[ir, q], yb[0:CAP, k, :]).then_inc(s[f"st_y{k}"], 16)
                    L.leave(0)
            for t in range(NT):
                act.wait_ge(s["x3_ready"], NT + t + 1)
                L.did(A(ygat[:, 0, t, :], x3[:, t, :], ACT.Square, accum_out=ss[:, t:t + 1]), s["sq_ready"])
                L.did(A(ss[:, t:t + 1], ss[:, t:t + 1], ACT.Sqrt, bias=eps, scale=1.0 / DM), s["rs_out"])

        @block.gpsimd
        def _(pool):
            L = Lane(pool, s["chain_p"])
            TT = nc.gpsimd.tensor_tensor

            def phase(n):
                pool.sem_inc(s["phase"])
                pool.wait_ge(s["phase"], 4 * n)

            phase(1)
            pool.wait_ge(s["phase"], 4)
            phase(2)
            def level(n, d, k):
                g = buffers(n, d)
                lv = const[:, C_LV + (d * LEVELS + k) * P:C_LV + (d * LEVELS + k + 1) * P]
                L.did(TT(g[C_C0 + k % 2], g[C_D1], over(lv, 4), ALU.mult), s["c_ready", d])

            for n, (st, hg) in enumerate(PAIRS):
                H4 = slice(hg * 4, hg * 4 + 4)
                for d in range(2):
                    g, t = buffers(n, d), tile_of(d, st)
                    if n:
                        L.need(s["vn_ready", d])
                    L.did(TT(g[C_VB], vtok[:, t, H4, :], spread(gbuf[:, 3, t, hcols(d, hg)]), ALU.mult))
                    L.did(TT(g[C_KBE], ktok[:, t, H4, :], spread(gbuf[:, 4, t, hcols(d, hg)]), ALU.mult),
                          s["kbe_ready", d])
                for d in range(2):
                    L.need(s["l_ready", d])
                    level(n, d, 0)
                for d in range(2):
                    if n:
                        L.need(s["group_done", d])
                    level(n, d, 1)
                for k in range(2, LEVELS):
                    for d in range(2):
                        g, t = buffers(n, d), tile_of(d, st)
                        if k == 2:
                            pool.wait_ge(s["t_ready", d], n * (LEVELS - 1) + 1)
                        else:
                            L.need(s["zz_ready", d])
                        level(n, d, k)
                        if k == 2:
                            L.need(s["at_pre", d])
                            L.did(TT(g[C_X], g[C_X], over(tri[d], 4), ALU.mult), s["at_ready", d])
                        if k == 3:
                            L.did(TT(g[C_KDEC], ktok[:, t, H4, :], spread(kcol[:, n % 2, d, :]), ALU.mult),
                                  s["kdec_ready", d])
                        if k == 4:
                            L.need(s["e_ready", d])
                            L.need(s["glast_ready", d])
                            L.did(TT(g[C_E], g[C_E], qT[:, H4, t * P:(t + 1) * P], ALU.mult), s["qg_ready", d])
                for d in range(2):
                    L.need(s["zz_ready", d], 2)
            phase(3)
            phase(4)
            phase(5)
            pool.sem_inc(s["phase"])

            pool.wait_ge(s["xn_saved"], 16 * NT)
            pool.wait_ge(s["zeros_saved"], 16)

            def gather(k):
                nc.gpsimd.indirect_dma_start(
                    xg[0:CAP, k, :], None, xn_dram, bass.IndirectOffsetOnAxis(icol[0:CAP, k:k + 1], 0))\
                    .then_inc(s[f"xg_k{k}"], 16)

            L.need(s["index_ready"])
            for k in range(2):
                L.did(nc.gpsimd.tensor_copy(icol[0:CAP, k:k + 1], index[0:CAP, k:k + 1]))
                gather(k)
            rounds = rounds_of(pool)
            with pool.Fori(0, rounds) as r:
                with pool.Fori(0, NE // XPT) as ir:
                    i = r * (NE // XPT) + ir
                    for q in range(XPT):
                        k = q % 2
                        pool.wait_ge(s["xe_ready"], i * XPT + (q + 1))
                        nc.gpsimd.tensor_copy(icol[0:CAP, k:k + 1], index[0:CAP, bass.ds(i * XPT + (q + 2), 1)])\
                            .then_inc(s["icol_ready"], 1)
                        pool.wait_ge(s["icol_ready"], 1)
                        gather(k)
                        pool.sem_inc(s["icol_ready"], -1)
                for k in range(2):
                    pool.wait_ge(s[f"st_y{k}"], r * (NE // 2 * 16) + (NE // 2 * 16 + 16))
                pool.wait_ge(s["combined"], r + 1)
                nc.gpsimd.tensor_copy(bcol, back_u[:, bass.ds(r, 1), :].rearrange("p o n -> p (o n)"))\
                    .then_inc(s["bcol_ready"], 1)
                pool.wait_ge(s["bcol_ready"], 1)
                for t in range(NT):
                    for k in range(2):
                        nc.gpsimd.indirect_dma_start(
                            ygat[:, k, t, :], None, y_dram,
                            bass.IndirectOffsetOnAxis(bcol[:, 2 * t + k:2 * t + k + 1], 0))\
                            .then_inc(s["ygat_ready", t // 2], 16)
                pool.sem_inc(s["bcol_ready"], -1)
            for k in range(2):
                pool.wait_ge(s[f"xg_k{k}"], rounds * (NE // 2 * 16) + 16)

        @block.vector
        def _(dve):
            L = Lane(dve, s["chain_v"])
            seen = [0]
            V = nc.vector

            def full():
                L.need(s["full_v"])
                seen[0] += 1
                return psv[:, (seen[0] - 1) % 4, :]

            def phase(n):
                dve.sem_inc(s["phase"])
                dve.wait_ge(s["phase"], 4 * n)

            def squares(v, dst, j):
                L.did(V.tensor_tensor_reduce(j, v, v, 1.0, 0.0, ALU.mult, ALU.add, dst))

            def inv_root(v, n):
                L.did(V.tensor_scalar(v, v, 1.0 / n, EPS, ALU.mult, ALU.add), s["rs_in"])
                L.need(s["rs_out"])
                L.did(V.reciprocal(v, v))

            def mul(o, x, y, *sig):
                L.did(V.tensor_tensor(o, x, y, ALU.mult), *sig)

            def add(o, x, y, *sig):
                L.did(V.tensor_tensor(o, x, y, ALU.add), *sig)

            def scale(o, x, c, *sig):
                L.did(V.tensor_scalar(o, x, c, None, ALU.mult), *sig)

            def turned(dst, t, gains, shifts, sig):
                b = full()
                o = dst[:, 0:4, t * P:(t + 1) * P]
                if shifts is None:
                    mul(o, by4(b), spread(gains[:, 0:4]), None, [s[sig], s["free_v"]])
                else:
                    mul(o, by4(b), spread(gains[:, 0:4]), None, [s["free_v"]])
                    add(o, o, spread(shifts[:, 0:4]), None, [s[sig]])

            for t in range(NT):
                if t == 0:
                    dve.wait_ge(s["ld_x"], 64)
                squares(xt[:, t, :], ss[:, t:t + 1], jA)
            inv_root(ss[:, 0:NT], DM)
            for t in range(NT):
                scale(xt[:, t, :], xt[:, t, :], ss[:, t:t + 1], s["xn_ready"])
            L.need(s["cols_ready"], 2)
            for t in range(NT):
                turned(hT, t, cols[:, V_PRE:V_PRE + 8], None, "hT_ready")
            for t in range(NT):
                b = full()
                L.did(V.tensor_copy(gb[:, t, :], b[:, 0:32]), s["free_v"])
            dve.wait_ge(s["ld_rope"], 48)
            for t in range(NT):
                dve.wait_ge(s["atok_ready"], 17 + t)
                v = atok[:, t, 0:1280].rearrange("p (h n) -> p h n", h=10)
                mul(sqA, v, v)
                L.did(V.tensor_reduce(ss[:, 16:26], sqA, AXX, ALU.add))
                inv_root(ss[:, 16:26], HD)
                mul(v, v, spread(ss[:, 16:26]))
                mul(v[:, 0:8, :], v[:, 0:8, :], over(qkn[:, 0, :], 8))
                mul(v[:, 8:10, :], v[:, 8:10, :], over(qkn[:, 1, :], 2))
                pr = atok[:, t, 0:1280].rearrange("p (h n two) -> p h n two", h=10, two=2)
                x0, x1_ = pr[:, :, :, 0], pr[:, :, :, 1]
                cos, sin = over(rope[:, t, 0, :], 10), over(rope[:, t, 1, :], 10)
                sq4 = sqA.rearrange("p h (u n) -> p u h n", u=2)
                mul(rt[:, 0], x0, cos)
                mul(rt[:, 1], x1_, sin)
                mul(sq4[:, 0], x0, sin)
                mul(sq4[:, 1], x1_, cos)
                L.did(V.tensor_tensor(x0, rt[:, 0], rt[:, 1], ALU.subtract))
                add(x1_, sq4[:, 0], sq4[:, 1], s["rope_ready"])
            for i in range(NH * NT + 1):
                if i < NH * NT:
                    dve.wait_ge(s["full_s"], score_job[i] + 1)
                    c = small[:, 64 + i:65 + i]
                    L.did(V.tensor_reduce(c, pss[:, score_job[i] % 4, :], AXX, ALU.max))
                    scale(c, c, -HD ** -0.5, s["negmax_ready"])
                if i >= 1:
                    j = i - 1
                    L.need(s["probs_ready"])
                    r = small[:, 96 + j:97 + j]
                    L.did(V.reciprocal(r, r))
                    scale(pb[:, j % 3, :], pb[:, j % 3, :], r, s["probsn_ready"])
            ntmp = [0]

            def tmp_of(tmp):
                L.need(s["tmp_ready"])
                ntmp[0] += 1
                return tmp[:, (ntmp[0] - 1) % 2, :]

            for j in range(KC):
                L.need(s["oT_ready"])
                L.need(s["silu_z"])
                mul(oT[:, j, :], oT[:, j, :], azs[:, j, :], s["oz_ready"])
            for j in range(KC):
                b = full()
                mul(mixT[:, j, :], b, tmp_of(tmpA), s["tmp_used"], [s["free_v"]])
            phase(1)

            gz = [gbuf[:, k, :, :] for k in range(8)]
            dve.wait_ge(s["ld_gpar"], 32)
            add(gz[5], gb[:, :, 16:32], over(gpar[:, 1, :], NT))
            L.did(V.scalar_tensor_tensor(gz[6], gz[5], -1.0, gz[5], ALU.mult, ALU.max))
            scale(gz[6], gz[6], -1.0, s["ga_step"])
            L.need(s["ga_ready"], 3)
            L.did(V.scalar_tensor_tensor(gz[5], gz[5], 0.0, gz[6], ALU.max, ALU.add))
            L.did(V.scalar_tensor_tensor(gz[0], gz[5], -1.0, over(gpar[:, 2, :], NT), ALU.mult, ALU.mult),
                  s["gg_ready"])
            for j in range(24):
                if j == 2:
                    b = full()
                    L.did(V.tensor_copy(gz[1], b[:, 0:64].rearrange("p (t n) -> p t n", t=NT)), s["gG_ready"],
                          [s["free_v"]])
                if j == 4:
                    L.need(s["ga_ready"])
                    mul(gz[4], gz[3], gz[2])
                b = full()
                if j >= 2:
                    dve.wait_ge(s["silu_ready"], j - 1)
                o = conv[:, j % 2, :]
                taps = [ccols[:, k * 24 + j:k * 24 + j + 1] for k in range(CONV_K)]
                scale(o, b, taps[2])
                for k in (0, 1, 3, 4):
                    m = k - 2
                    lo, hi = max(0, -m), SEQ - max(0, m)
                    L.did(V.scalar_tensor_tensor(o[:, lo:hi], b[:, lo + m:hi + m], taps[k], o[:, lo:hi],
                                                 ALU.mult, ALU.add),
                          s["conv_ready"] if k == 4 else None, [s["free_v"]] if k == 4 else [])
                n = j - (SUM_LAG + 1)
                if 0 <= n < 16:
                    L.need(s["rt_ready"])
                    r = crt[:, n % 2, :]
                    L.did(V.reciprocal(r, r))
                    v = qT[:, n, :] if n < 8 else kT[:, n - 8, :]
                    mul(v, v, r, s["norm_ready"])
            phase(2)

            def decay_rows(n):
                st, hg = PAIRS[n]
                for d in range(2):
                    g, t = buffers(n, d), tile_of(d, st)
                    L.need(s["e_ready", d])
                    x = g[C_X]
                    L.did(V.tensor_tensor(x, x, spread(gbuf[:, 1, t, hcols(d, hg)]), ALU.subtract))
                    L.did(V.tensor_scalar(g[C_D1], x, 0.0, None, ALU.max))
                    L.did(V.tensor_scalar(x, x, 0.0, None, ALU.min), s["x_ready", d])

            def key_products(n):
                st, hg = PAIRS[n]
                for d in range(2):
                    g, t = buffers(n, d), tile_of(d, st)
                    L.need(s["d1_ready", d])
                    b = full()
                    mul(g[C_D1], by4(b), g[C_D1], s["free_v"])
                    mul(g[C_D1], g[C_D1], spread(gbuf[:, 3, t, hcols(d, hg)]), s["l_ready", d])
                    L.need(s["d2_ready", d])
                    last = P - 1 if d == 0 else 0
                    L.did(V.tensor_copy(kcol[:, n % 2, d, :], g[C_X][:, :, last]))
                    b = full()
                    mul(g[C_X], by4(b), g[C_X], s["at_pre", d], [s["free_v"]])

            decay_rows(0)
            key_products(0)
            for n, (st, hg) in enumerate(PAIRS):
                for d in range(2):
                    g = buffers(n, d)
                    dve.wait_ge(s["c_ready", d], n * LEVELS + 1)
                    b = full()
                    L.did(V.tensor_tensor(g[C_TT], over(ident, 4), by4(b), ALU.subtract), s["tt_ready", d],
                          [s["free_v"]])
                    L.did(V.tensor_tensor(g[C_T], over(ident, 4), g[C_C0], ALU.subtract), s["t_ready", d])
                for k in range(1, LEVELS):
                    for d in range(2):
                        g = buffers(n, d)
                        b = full()
                        L.did(V.tensor_tensor(g[C_TT], g[C_TT], by4(b), ALU.subtract), s["tt_ready", d],
                              [s["free_v"]])
                        if k < LEVELS - 1:
                            b = full()
                            L.did(V.tensor_tensor(g[C_T], g[C_T], by4(b), ALU.subtract), s["t_ready", d],
                                  [s["free_v"]])
                if n + 1 < len(PAIRS):
                    decay_rows(n + 1)
                for d in range(2):
                    b = full()
                    L.did(V.tensor_copy(buffers(n, d)[C_VN], by4(b)), s["vn_ready", d], [s["free_v"]])
                if n + 1 < len(PAIRS):
                    key_products(n + 1)
                for d in range(2):
                    t = tile_of(d, st)
                    o = oacc[:, t, hg * 4:hg * 4 + 4, :]
                    b = full()
                    if st < NT // 2:
                        L.did(V.tensor_copy(o, by4(b)), s["free_v"])
                    else:
                        add(o, o, by4(b), s["free_v"])
                for d in range(2):
                    L.need(s["glast_ready", d])
                    b = full()
                    if st == 0:
                        L.did(V.tensor_copy(state[:, d, hg * 4:hg * 4 + 4, :], by4(b)), s["group_done", d],
                              [s["free_v"]])
                    else:
                        for h in range(4):
                            v = state[:, d, hg * 4 + h, :]
                            L.did(V.scalar_tensor_tensor(v, v, glast[:, n % 2, d, h:h + 1],
                                                         b[:, h * P:(h + 1) * P], ALU.mult, ALU.add),
                                  s["group_done", d] if h == 3 else None, [s["free_v"]] if h == 3 else [])
            phase(3)

            for t in range(NT):
                j8 = junk.rearrange("p (h n) -> p h n", h=8)
                mul(j8, oacc[:, t], oacc[:, t])
                L.did(V.tensor_reduce(ss[:, t * 8:t * 8 + 8], j8, AXX, ALU.add))
            inv_root(ss[:, 0:32], HD)
            for t in range(NT):
                mul(oacc[:, t], oacc[:, t], spread(ss[:, t * 8:t * 8 + 8]), s["on_ready"])
            for t in range(NT):
                for h0 in (0, 4):
                    b = full()
                    scale(onT[:, h0:h0 + 4, t * P:(t + 1) * P], by4(b), cols[:, V_DN:V_DN + 1], s["free_v"])
            for j in range(KC):
                mul(onT[:, j, :], onT[:, j, :], tmp_of(tmpB), s["dz_ready"], [s["tmp_used"]])
            for j in range(KC):
                tmp = tmp_of(tmpB)
                b = full()
                mul(tmp, b, tmp, s["free_v"])
                add(mixT[:, j, :], mixT[:, j, :], tmp, s["mixT_ready"], [s["tmp_used"]])

            def add_normed(x, v, row):
                inv_root(ss[:, 0:NT], DM)
                for t in range(NT):
                    L.did(V.scalar_tensor_tensor(v[:, t, :], v[:, t, :], ss[:, t:t + 1], row, ALU.mult, ALU.mult))
                    add(x[:, t, :], x[:, t, :], v[:, t, :], s["x1_ready"])

            for t in range(NT):
                b = full()
                L.did(V.tensor_copy(pinT[:, :, t * P:(t + 1) * P], b[:, 0:256].rearrange("p (c n) -> p c n", c=2)),
                      s["pinT_ready"], [s["free_v"]])
            L.need(s["mo_ready"], 12)
            for t in range(NT):
                L.need(s["mo_ready"])
                squares(mo[:, t, :], ss[:, t:t + 1], junk)
            dve.wait_ge(s["ld_rows"], 32)
            dve.wait_ge(s["ld_res"], 64)
            add_normed(x1, mo, rowv)
            for t in range(NT):
                b = full()
                L.did(V.tensor_copy(x1T[:, 0:4, t * P:(t + 1) * P], by4(b)), None, [s["x1T_ready"], s["free_v"]])
            L.need(s["mod_ready"], 24)
            add(mod[:, :, :], mod[:, :, :], cols[:, V_BADA:V_BADA + 48].unsqueeze(2).broadcast_to([P, 48, 2]))
            for n, (c0, k, vn) in enumerate(((8, 0, V_N1), (8, 1, V_N1), (32, 0, V_N2))):
                L.did(V.scalar_tensor_tensor(gain[:, n * 8:n * 8 + 8], mod[:, c0:c0 + 8, k], 1.0,
                                             cols[:, vn:vn + 8], ALU.add, ALU.mult))
            dve.wait_ge(s["ld_ctx"], 32)
            for t in range(NTC):
                squares(ctxt[:, t, :], ss[:, 40 + t:41 + t], junk)
            inv_root(ss[:, 40:40 + NTC], DM)
            for t in range(NTC):
                scale(ctxt[:, t, :], ctxt[:, t, :], ss[:, 40 + t:41 + t], s["x2_ready"])
            for b in range(4):
                cs = slice(b * WC, (b + 1) * WC)
                for t in range(NT):
                    L.need(s["sg_ready"])
                    mul(et[:, t, cs], et[:, t, cs], sg[:, t, cs])
                    if b == 3:
                        squares(et[:, t, :], ss[:, t:t + 1], junk)
                if b == 1:
                    for t in range(NTC):
                        turned(hcT, t, gain[:, 8:16], mod[:, 0:8, 1], "hc_ready")
            add_normed(x1, et, rowv2)
            for t in range(NTC):
                b = full()
                L.did(V.tensor_copy(v2[:, NT + t, 0:256], b[:, 0:256]), s["free_v"])
            L.need(s["rs_out"])
            L.did(V.reciprocal(ss[:, 32:32 + NT], ss[:, 32:32 + NT]))
            phase(4)

            for t in range(NT):
                scale(xn[:, t, :], x1[:, t, :], ss[:, 32 + t:33 + t], s["x2_ready"])
            for t in range(NT):
                turned(h2T, t, gain[:, 0:8], mod[:, 0:8, 0], "h2_ready")
            for b2 in range(2):
                for t in range(NT + (NTC if b2 else 0)):
                    b = full()
                    L.did(V.tensor_copy(v2[:, t, b2 * 256:(b2 + 1) * 256], b[:, 0:256]), s["free_v"])
            for d in range(2):
                for c0, n in ((0, SEQ), (SEQ, CTX)):
                    b = full()
                    L.did(V.tensor_copy(a2T[0:RANK, d, c0:c0 + n], b[0:RANK, 0:n]), s["a2_ready"], [s["free_v"]])
            for b2 in range(2):
                for t in range(NT):
                    b = full()
                    L.did(V.tensor_copy(p2[:, t, b2 * 256:(b2 + 1) * 256], b[:, 0:256]), s["p2_ready"],
                          [s["free_v"]])
                if b2 == 0:
                    for t in range(NT + NTC):
                        L.need(s["z_ready"])
                        z = la[:, t, :]
                        L.did(V.scalar_tensor_tensor(zabs[t], z, -1.0, z, ALU.mult, ALU.max), s["absz_ready"])
            for g in range(4):
                b = full()
                if g >= 2:
                    dve.wait_ge(s["cat_ready"], g - 1)
                L.did(V.tensor_copy(pmT[:, g % 2, :], b), s["mT_ready"], [s["free_v"]])
                if g == 1:
                    for t in range(NT + NTC):
                        L.need(s["lz_ready"])
                        z = la[:, t, :]
                        L.did(V.scalar_tensor_tensor(z, z, 0.0, zabs[t], ALU.min, ALU.subtract), s["la_ready"])
            phase(5)

            for n in range(4):
                d, m2 = divmod(n, 2)
                L.need(s["bexp_ready"], 2)
                mul(qb[:, d, m2, :], q2T[:, m2, :], eb[:, n % 2, :])
                mul(kb[:, d, m2, :], k2T[:, m2, :], enb[:, n % 2, :], s["qb_ready"])
            for t in range(NT + NTC):
                L.need(s["kexp_ready"])
                kv = kst[:, t, :].rearrange("p (d n) -> p d n", d=2)
                mul(kv, kv, k2[:, t, :].unsqueeze(1).broadcast_to([P, 2, 256]), s["kst_ready"])
            L.did(V.memset(swork[:, 0, :, :, :], 0.0))
            for n in range(12):
                for d in range(2):
                    b = full()
                    c = chunk_col(d, n)
                    for m2 in range(2):
                        src = state_at(d, m2, n)
                        dst = state_at(d, m2, n + 1)
                        if dst is None:
                            continue
                        for hh in range(2):
                            hp = slice(hh * 64, hh * 64 + 64)
                            L.did(V.scalar_tensor_tensor(dst[hp, :], src[hp, :], dec2[hp, d, m2, c:c + 1],
                                                         b[hp, m2 * 256 + hh * P:m2 * 256 + (hh + 1) * P],
                                                         ALU.mult, ALU.add))
                    L.raise_(s["free_v"])
                if n < 2 * H2:
                    b = full()
                    mul(by4(scm[n]), by4(b), over(blk[n % 2], 4), s["sc_ready"], [s["free_v"]])
            L.raise_(s["sprev_ready"])
            for c0 in (0, 512):
                b = full()
                L.did(V.tensor_copy(gtrow[:, c0:c0 + 512], b), s["free_v"])
            for h in range(H2):
                L.need(s["rt2_ready"], 3 if h == 0 else 2 if h < H2 - 1 else 1)
                r = enb[:, h % 2, :]
                L.did(V.reciprocal(r, r))
                mul(r, r, catT[:, h, :])
                L.did(V.scalar_tensor_tensor(catT[:, h, :], r, cols[:, V_GLA:V_GLA + 1], g2T[:, h, :],
                                             ALU.mult, ALU.mult), s["o2_ready"], [s["cat_ready"]])
            L.did(V.memset(zero, 0.0))
            tmp = scm01[:, 0, 0:WC]

            def turned_x3(t):
                turned(h3T, t, gain[:, 16:24], mod[:, 24:32, 0], "h3_ready")

            def logits(t):
                b = full()
                L.did(V.tensor_copy(lg[:, t, :], b[:, 0:NG + NE]), s["free_v"])

            for t in range(NT):
                for b2 in range(4):
                    cs = slice(b2 * WC, (b2 + 1) * WC)
                    b = full()
                    mul(tmp, b[:, 0:WC], gtrow[:, cs], s["free_v"])
                    add(x1[:, t, cs], x1[:, t, cs], tmp)
                if t == NT - 1:
                    dve.sem_inc(s["phase"])
                if t >= 1:
                    turned_x3(t - 1)
                if t >= 2:
                    logits(t - 2)
                squares(x3[:, t, :], ss[:, t:t + 1], scm01[:, 2:4, :].rearrange("p a n -> p (a n)"))
                inv_root(ss[:, t:t + 1], DM)
                scale(x3n[:, t, :], x3[:, t, :], ss[:, t:t + 1], s["x3_ready"])
            turned_x3(NT - 1)
            logits(NT - 2)
            logits(NT - 1)

            iota = const[:, C_IOTA:C_IOTA + NE]
            rev = const[:, C_REV:C_REV + EPG]
            scale(rthr, iota[:, 1:ROUNDS], float(CAP))

            def along(v, m):
                return v.unsqueeze(2).broadcast_to([P, v.shape[1], m])

            def first_largest(hot, at_, v, most, tmp):
                n = v.shape[2]
                L.did(V.tensor_reduce(most, v, AXX, ALU.max))
                L.did(V.tensor_tensor(tmp, v, along(most, n), ALU.is_ge))
                mul(tmp, tmp, over(rev[:, 0:n], NT))
                L.did(V.tensor_reduce(at_, tmp, AXX, ALU.max))
                L.did(V.tensor_tensor(hot, tmp, along(at_, n), ALU.is_ge))

            gmax, gat, e1, e2, at1, at2, den, ids = [rcol[:, k, :] for k in range(8)]
            ghot = rgrp[:, 1]
            first_largest(ghot, gat, lg[:, :, 0:NG], gmax, rgrp[:, 0])
            ghot_e = ghot.unsqueeze(3).broadcast_to([P, NT, NG, EPG])
            by_group = rexp.rearrange("p t (g e) -> p t g e", g=NG)
            mul(by_group, lg[:, :, 4:36].rearrange("p t (g e) -> p t g e", g=NG), ghot_e)
            L.did(V.tensor_reduce(rin, rexp.rearrange("p t (g e) -> p t e g", g=NG), AXX, ALU.add))
            first_largest(rhot[:, 0], at1, rin, e1, rtmp)
            L.did(V.scalar_tensor_tensor(rin, rhot[:, 0], -1e30, rin, ALU.mult, ALU.add))
            first_largest(rhot[:, 1], at2, rin, e2, rtmp)
            L.did(V.tensor_tensor(lexp[:, :, 0:NG], lg[:, :, 0:NG], along(gmax, NG), ALU.subtract))
            L.did(V.tensor_tensor(lexp[:, :, NG], e2, e1, ALU.subtract), s["lg_ready"])
            for k in range(2):
                o = pick[:, :, k, :].rearrange("p t (g e) -> p t g e", g=NG)
                mul(o, ghot_e, rhot[:, k].unsqueeze(2).broadcast_to([P, NT, NG, EPG]))
            add(picked, pick[:, :, 0, :], pick[:, :, 1, :])
            L.did(V.memset(before_t[:, 0, :], 0.0))
            for t in range(NT):
                add(before_t[:, t + 1, :], before_t[:, t, :], picked[:, t, :],
                    s["picked_ready"] if t == NT - 1 else None)
            mul(rtok, pick, const[:, C_TOK:C_TOK + NT].unsqueeze(2).unsqueeze(3).broadcast_to([P, NT, 2, NE]))
            scale(ids, gat, float(-EPG))
            for k, a_ in enumerate((at1, at2)):
                L.did(V.tensor_tensor(eid[:, :, k], ids, a_, ALU.subtract))
            L.did(V.tensor_scalar(eid, eid, float(EPG * EPG + EPG), None, ALU.add))
            L.need(s["lexp_ready"])
            e = lexp[:, :, NG]
            L.did(V.tensor_reduce(den, lexp[:, :, 0:NG], AXX, ALU.add))
            L.did(V.scalar_tensor_tensor(den, e, 1.0, den, ALU.add, ALU.mult))
            L.did(V.reciprocal(ewt[:, :, 0], den))
            mul(ewt[:, :, 1], ewt[:, :, 0], e)
            for c0 in (0, 512):
                b = full()
                L.did(V.tensor_copy(rowg[:, c0:c0 + 512], b), s["free_v"])
            b = full()
            place = b[:, 0:NT * NE].rearrange("p (t n) -> p t n", t=NT).unsqueeze(2).broadcast_to([P, NT, 2, NE])
            mul(rplace, pick, place)
            rnd, slf = tround.rearrange("p t k -> p (t k)"), slot_f.rearrange("p t k -> p (t k)")
            L.did(V.tensor_reduce(slot_f, rplace, AXX, ALU.add))
            L.did(V.tensor_tensor(rpast, along(slf, ROUNDS - 1), over(rthr, 2 * NT), ALU.is_ge))
            L.did(V.tensor_reduce(rnd, rpast, AXX, ALU.add))
            fst = rfirst.rearrange("p t k -> p (t k)")
            L.did(V.scalar_tensor_tensor(fst, rnd, float(-CAP), slf, ALU.mult, ALU.add))
            L.did(V.tensor_tensor(rplaced, along(fst, CAP), over(const[:, C_IOTA:C_IOTA + CAP], 2 * NT),
                                  ALU.is_equal))
            L.did(V.tensor_tensor(rround, along(rnd, ROUNDS), over(iota[:, 0:ROUNDS], 2 * NT), ALU.is_equal))
            for t in range(NT):
                mul(tok_at[:, t], rtok[:, t].unsqueeze(2).broadcast_to([P, 2, ROUNDS, NE]),
                    rround[:, 2 * t:2 * t + 2, :].unsqueeze(3).broadcast_to([P, 2, ROUNDS, NE]), s["table_ready"])
            L.did(V.tensor_reduce(tmax[:, 2:3], b[:, NT * NE:(NT + 1) * NE], AXX, ALU.max), s["free_v"])
            L.did(V.tensor_scalar(tmax[:, 8:8 + ROUNDS], iota[:, 0:ROUNDS], float(CAP), tmax[:, 2:3], ALU.mult, ALU.is_lt))
            L.did(V.tensor_reduce(tmax[:, 3:4], tmax[:, 8:8 + ROUNDS], AXX, ALU.add))
            L.did(V.tensor_copy(turns_u[:, 0:1], tmax[:, 3:4]), s["turns_ready"])
            L.did(V.memset(index[:, ROUNDS * NE:], 0))
            b = full()
            L.did(V.tensor_copy(index[0:CAP, 0:ROUNDS * NE], b[0:CAP, 0:ROUNDS * NE]), s["index_ready"],
                  [s["free_v"]])
            def to_xe(b, k):
                o = xe[:, k, :, :]
                L.did(V.tensor_tensor(o, b.rearrange("p (c n) -> p c n", c=KC), spread(gain[:, 16:24], CAP),
                                      ALU.mult), s["free_v"])
                add(o, o, spread(mod[:, 24:32, 0], CAP), s["xe_ready"])

            to_xe(full(), 0)
            L.did(V.scalar_tensor_tensor(slf, rnd, float((NE - 1) * CAP), slf, ALU.mult, ALU.add))
            L.did(V.scalar_tensor_tensor(slot_f, eid, float(CAP), slot_f, ALU.mult, ALU.add))
            for r in range(ROUNDS):
                o = back_f[:, r, :]
                L.did(V.tensor_scalar(o, slf, float(-NE * CAP * (r + 1)), None, ALU.add))
                L.did(V.scalar_tensor_tensor(o, rnd, float(r), o, ALU.is_equal, ALU.mult))
                L.did(V.tensor_scalar(o, o, float(NE * CAP), None, ALU.add))
            L.did(V.tensor_copy(back_u, back_f))
            dve.wait_ge(s["xn_saved"], 16 * NT)
            L.did(V.memset(yacc, 0.0))
            L.raise_(s["sil_used"], 2)
            q0 = seen[0]
            rounds = rounds_of(dve)
            dve.sem_inc(s["combined"])
            with dve.Fori(0, rounds) as r:
                with dve.Fori(0, NE // XPT) as ir:
                    i = r * (NE // XPT) + ir
                    L.enter(i, {s["hid_ready"]: XPT, s["free_v"]: 3 * XPT, s["sil_used"]: XPT, s["xe_ready"]: XPT,
                                s["y1_ready"]: XPT},
                            {s["full_v"]: 3 * XPT, s["sil_ready"]: XPT})
                    for q in range(XPT):
                        k = q % 2
                        L.need(s["sil_ready"])
                        L.need(s["full_v"])
                        L.did(V.tensor_tensor(hid[:, k, :], psv[:, (q0 + 3 * q) % 4, 0:2 * CAP], sil[:, k, :], ALU.mult),
                              s["hid_ready"], [s["free_v"], s["sil_used"]])
                        L.need(s["full_v"])
                        to_xe(psv[:, (q0 + 3 * q + 1) % 4, :], 1 - k)
                        L.need(s["full_v"])
                        dve.wait_ge(s[f"st_y{k}"], (i * (XPT // 2) + (q // 2 + 1)) * 16)
                        L.did(V.tensor_copy(yb[0:CAP, k, 512:DM], psv[0:CAP, (q0 + 3 * q + 2) % 4, :]), s["y1_ready"],
                              [s["free_v"]])
                    L.leave(0)
                for t in range(NT):
                    if t % 2 == 0:
                        dve.wait_ge(s["ygat_ready", t // 2], r * (32 * NT // 2) + 32 * NT // 2)
                    for k in range(2):
                        ins = V.scalar_tensor_tensor(yacc[:, t, :], ygat[:, k, t, :], ewt[:, t, k:k + 1],
                                                     yacc[:, t, :], ALU.mult, ALU.add)
                        ins.then_inc(s["yacc_ready"], 1)
                        dve.wait_ge(s["yacc_ready"], r * (2 * NT) + (2 * t + k + 1))
                dve.sem_inc(s["combined"])
            for t in range(NT):
                mul(yacc[:, t, :], yacc[:, t, :], rowg)
                add(x3[:, t, :], x3[:, t, :], yacc[:, t, :], s["x3_ready"])
            dve.wait_ge(s["ld_rowf"], 16)
            for t in range(NT):
                L.need(s["rs_out"])
                L.did(V.reciprocal(ss[:, t:t + 1], ss[:, t:t + 1]))
                L.did(V.scalar_tensor_tensor(x3[:, t, :], x3[:, t, :], ss[:, t:t + 1], rowf, ALU.mult, ALU.mult),
                      s["out_ready"])


_OUT = (1, SEQ, DM)
DUMP = []


def kernel(**inputs):
    import concourse.bacc as bacc
    from concourse.bass_utils import run_bass_kernel_spmd

    nc = bacc.Bacc("TRN2", target_bir_lowering=False, num_devices=1)
    masks, rope, pool = shape_constants()
    arrays = {n: np.ascontiguousarray(v) for n, v in inputs.items()}
    arrays |= {"c_masks": masks, "c_rope": rope, "c_pool": pool}
    a = {n: nc.dram_tensor(n, v.shape, F32, kind="ExternalInput").ap() for n, v in arrays.items()}
    out = nc.dram_tensor("out", _OUT, F32, kind="ExternalOutput").ap()
    build(nc, a, out, [])
    r = run_bass_kernel_spmd(nc, [arrays], core_ids=[0])
    return r.results[0]["out"]
```
